# Optimizing a Trainium2 kernel written in Bass

```python
import math
import jax
import jax.numpy as jnp
from jax import lax
import numpy as np
import jax, jax.numpy as jnp

D_MODEL = 1024
BATCH = 1
SEQ = 512
DEPTH = 1

N_MIXERS = 2
HEAD_DIM = 64
MIX_WIDTH = 3 * D_MODEL // 4
MEM_WIDTH = D_MODEL - MIX_WIDTH
MEM_HEADS = 4
MEM_HEAD_DIM = MEM_WIDTH // MEM_HEADS
MEM_TOKENS = 256
RWKV_HEADS = MIX_WIDTH // HEAD_DIM
DECAY_LORA = 64
ICLR_LORA = 64
GATE_LORA = 128
RWKV_COLS = 3 * MIX_WIDTH + DECAY_LORA + ICLR_LORA + GATE_LORA
RWKV_IN = RWKV_COLS + MEM_WIDTH
DIFF_HEADS = MIX_WIDTH // (2 * HEAD_DIM)
DIFF_IN = 3 * MIX_WIDTH + MEM_WIDTH
D_FF = 4 * D_MODEL
N_RWKV_LAYERS = (DEPTH + N_MIXERS - 1) // N_MIXERS
N_DIFF_LAYERS = DEPTH // N_MIXERS
Q_BLOCK = 128
RMS_EPS = 1e-6
GN_EPS = 64e-5


def rms_norm(x, g=None):
    xf = x.astype(jnp.float32)
    y = xf * lax.rsqrt(jnp.mean(jnp.square(xf), axis=-1, keepdims=True) + RMS_EPS)
    if g is not None:
        y = y * g.astype(jnp.float32)
    return y.astype(x.dtype)

def token_shift(z, mu):
    z_prev = jnp.pad(z[:, :-1], ((0, 0), (1, 0), (0, 0)))
    return z + (z_prev - z) * mu

def delta_rule_scan(r, w, k, v, a, b):
    B, T, H, N = r.shape
    xs = tuple(jnp.moveaxis(z.astype(jnp.float32), 1, 0) for z in (r, w, k, v, a, b))

    def step(S, inp):
        r_t, w_t, k_t, v_t, a_t, b_t = inp
        sa = jnp.einsum('bhvk,bhk->bhv', S, a_t)
        S = (S * w_t[:, :, None, :] + sa[..., None] * b_t[:, :, None, :]
             + v_t[..., None] * k_t[:, :, None, :])
        return S, jnp.einsum('bhvk,bhk->bhv', S, r_t)

    S0 = jnp.zeros((B, H, N, N), jnp.float32)
    _, y = lax.scan(step, S0, xs)
    return jnp.moveaxis(y, 0, 1)

def rwkv7_time_mix(h, w_in, mu, w0, w2, a0, a2, g2, k_k, k_a, r_k, lnx_g, lnx_b):
    B, T, _ = h.shape
    H, N = RWKV_HEADS, HEAD_DIM
    proj = h @ w_in
    slab = token_shift(proj[..., :RWKV_COLS], mu)
    q_mem = proj[..., RWKV_COLS:]
    c3 = 3 * MIX_WIDTH
    r, k, v, wd, ad, gd = jnp.split(
        slab, [MIX_WIDTH, 2 * MIX_WIDTH, c3, c3 + DECAY_LORA, c3 + DECAY_LORA + ICLR_LORA], axis=-1)
    log_w = -jax.nn.softplus(-(w0 + jnp.tanh(wd) @ w2)) - 0.5
    decay = jnp.exp(-jnp.exp(log_w.astype(jnp.float32)))
    a = jax.nn.sigmoid(a0 + ad @ a2)
    g = jax.nn.sigmoid(gd) @ g2

    def heads(z):
        return z.reshape(B, T, H, N)

    kk = heads(k * k_k).astype(jnp.float32)
    kk = kk / jnp.maximum(jnp.sqrt(jnp.sum(jnp.square(kk), axis=-1, keepdims=True)), 1e-12)
    k = k * (1.0 + (a - 1.0) * k_a)
    a_h = heads(a).astype(jnp.float32)
    r_h, k_h, v_h = heads(r), heads(k), heads(v)
    y = delta_rule_scan(r_h, heads(decay), k_h, v_h, -kk, kk * a_h)
    mean = jnp.mean(y, axis=-1, keepdims=True)
    var = jnp.mean(jnp.square(y - mean), axis=-1, keepdims=True)
    y = ((y - mean) * lax.rsqrt(var + GN_EPS)).reshape(B, T, MIX_WIDTH)
    y = (y * lnx_g.astype(jnp.float32) + lnx_b.astype(jnp.float32)).astype(h.dtype)
    bonus = (jnp.sum(r_h * k_h * r_k, axis=-1, keepdims=True) * v_h).reshape(B, T, MIX_WIDTH)
    return (y + bonus) * g, q_mem

def alibi_slopes(n):
    return jnp.exp2(-8.0 * jnp.arange(1, n + 1, dtype=jnp.float32) / n)

def causal_diff_attention(q, k, v, lam, slopes):
    B, T, H, _, d = q.shape
    nb = T // Q_BLOCK
    qb = jnp.moveaxis(q.reshape(B, nb, Q_BLOCK, H, 2, d), 1, 0)
    starts = jnp.arange(nb, dtype=jnp.int32) * Q_BLOCK
    k_pos = jnp.arange(T, dtype=jnp.int32)
    scale = d ** -0.5

    def block(args):
        q_blk, start = args
        q_pos = start + jnp.arange(Q_BLOCK, dtype=jnp.int32)
        dist = q_pos[:, None] - k_pos[None, :]
        bias = -slopes[:, None, None] * dist.astype(jnp.float32)[None]
        s = jnp.einsum('bqhcd,bkhcd->bhcqk', q_blk, k).astype(jnp.float32) * scale
        s = jnp.where(dist >= 0, s + bias[None, :, None], -jnp.inf)
        p = jax.nn.softmax(s, axis=-1)
        p = p[:, :, 0] - lam * p[:, :, 1]
        return jnp.einsum('bhqk,bkhe->bqhe', p.astype(v.dtype), v)

    out = lax.map(block, (qb, starts))
    return jnp.moveaxis(out, 0, 1).reshape(B, T, H, 2 * d)

def diff_lambda_init(layer):
    return 0.8 - 0.6 * math.exp(-0.3 * layer)

def diff_attention_mixer(h, w_in, q_g, k_g, lq1, lk1, lq2, lk2, subln_g, lambda_init):
    B, T, _ = h.shape
    H, d = DIFF_HEADS, HEAD_DIM
    proj = h @ w_in
    q = rms_norm(proj[..., :MIX_WIDTH].reshape(B, T, H, 2, d), q_g)
    k = rms_norm(proj[..., MIX_WIDTH:2 * MIX_WIDTH].reshape(B, T, H, 2, d), k_g)
    v = proj[..., 2 * MIX_WIDTH:3 * MIX_WIDTH].reshape(B, T, H, 2 * d)
    q_mem = proj[..., 3 * MIX_WIDTH:]
    lam = (jnp.exp(jnp.sum(lq1 * lk1).astype(jnp.float32))
           - jnp.exp(jnp.sum(lq2 * lk2).astype(jnp.float32)) + lambda_init)
    o = causal_diff_attention(q, k, v, lam, alibi_slopes(H))
    o = rms_norm(o, subln_g) * (1.0 - lambda_init)
    return o.reshape(B, T, MIX_WIDTH), q_mem

def memory_cross_attention(q_mem, k_mem, v_mem, q_g, k_g):
    B, T, _ = q_mem.shape
    q = rms_norm(q_mem.reshape(B, T, MEM_HEADS, MEM_HEAD_DIM), q_g)
    k = k_mem * k_g
    s = jnp.einsum('bthd,bmhd->bhtm', q, k).astype(jnp.float32) * MEM_HEAD_DIM ** -0.5
    p = jax.nn.softmax(s, axis=-1).astype(v_mem.dtype)
    return jnp.einsum('bhtm,bmhd->bthd', p, v_mem).reshape(B, T, MEM_WIDTH)

def first_inputs(seed: int = 0) -> dict:
    key = jax.random.key(seed)
    keys = jax.random.split(key, 40)
    counter = [0]

    def next_key():
        counter[0] += 1
        return keys[counter[0] - 1]

    def nrm(shape, scale):
        return jax.random.normal(next_key(), shape, jnp.float32) * scale

    def gain(shape):
        return 1.0 + nrm(shape, 0.05)

    def unif(shape, lo, hi):
        return jax.random.uniform(next_key(), shape, jnp.float32, lo, hi)

    NR, ND = N_RWKV_LAYERS, N_DIFF_LAYERS
    return {
        "x": nrm((BATCH, SEQ, D_MODEL), 1.0),
        "mem": nrm((BATCH, MEM_TOKENS, D_MODEL), 1.0),
        "norm_mix_g": gain((DEPTH, D_MODEL)),
        "norm_ffn_g": gain((DEPTH, D_MODEL)),
        "w_out": nrm((DEPTH, D_MODEL, D_MODEL), D_MODEL ** -0.5),
        "w_ff1": nrm((DEPTH, D_MODEL, D_FF), D_MODEL ** -0.5),
        "w_ff2": nrm((DEPTH, D_FF, D_MODEL), D_FF ** -0.5),
        "mem_norm_g": gain((D_MODEL,)),
        "w_mem_kv": nrm((D_MODEL, 2 * MEM_WIDTH), D_MODEL ** -0.5),
        "mem_q_norm_g": gain((DEPTH, MEM_HEAD_DIM)),
        "mem_k_norm_g": gain((DEPTH, MEM_HEAD_DIM)),
        "rw_in": nrm((NR, D_MODEL, RWKV_IN), D_MODEL ** -0.5),
        "rw_mu": unif((NR, RWKV_COLS), 0.0, 1.0),
        "rw_w0": unif((NR, MIX_WIDTH), -6.0, -1.0),
        "rw_w2": nrm((NR, DECAY_LORA, MIX_WIDTH), 0.5 * DECAY_LORA ** -0.5),
        "rw_a0": nrm((NR, MIX_WIDTH), 0.1),
        "rw_a2": nrm((NR, ICLR_LORA, MIX_WIDTH), ICLR_LORA ** -0.5),
        "rw_g2": nrm((NR, GATE_LORA, MIX_WIDTH), GATE_LORA ** -0.5),
        "rw_k_k": 0.85 + nrm((NR, MIX_WIDTH), 0.05),
        "rw_k_a": gain((NR, MIX_WIDTH)),
        "rw_r_k": nrm((NR, RWKV_HEADS, HEAD_DIM), 0.1),
        "rw_lnx_g": gain((NR, MIX_WIDTH)),
        "rw_lnx_b": nrm((NR, MIX_WIDTH), 0.01),
        "df_in": nrm((ND, D_MODEL, DIFF_IN), D_MODEL ** -0.5),
        "df_q_norm_g": gain((ND, 2, HEAD_DIM)),
        "df_k_norm_g": gain((ND, 2, HEAD_DIM)),
        "df_lq1": nrm((ND, HEAD_DIM), 0.1),
        "df_lk1": nrm((ND, HEAD_DIM), 0.1),
        "df_lq2": nrm((ND, HEAD_DIM), 0.1),
        "df_lk2": nrm((ND, HEAD_DIM), 0.1),
        "df_subln_g": gain((ND, 2 * HEAD_DIM)),
    }

def first_block(x, mem, norm_mix_g, norm_ffn_g, w_out, w_ff1, w_ff2, mem_norm_g, w_mem_kv,
              mem_q_norm_g, mem_k_norm_g, rw_in, rw_mu, rw_w0, rw_w2, rw_a0, rw_a2, rw_g2,
              rw_k_k, rw_k_a, rw_r_k, rw_lnx_g, rw_lnx_b, df_in, df_q_norm_g, df_k_norm_g,
              df_lq1, df_lk1, df_lq2, df_lk2, df_subln_g):
    B, M, _ = mem.shape
    kv = rms_norm(mem, mem_norm_g) @ w_mem_kv
    k_mem = rms_norm(kv[..., :MEM_WIDTH].reshape(B, M, MEM_HEADS, MEM_HEAD_DIM))
    v_mem = kv[..., MEM_WIDTH:].reshape(B, M, MEM_HEADS, MEM_HEAD_DIM)

    for layer in range(DEPTH):
        j = layer // N_MIXERS
        h = rms_norm(x, norm_mix_g[layer])
        if layer % N_MIXERS == 0:
            mix, q_mem = rwkv7_time_mix(h, rw_in[j], rw_mu[j], rw_w0[j], rw_w2[j], rw_a0[j],
                                        rw_a2[j], rw_g2[j], rw_k_k[j], rw_k_a[j], rw_r_k[j],
                                        rw_lnx_g[j], rw_lnx_b[j])
        else:
            mix, q_mem = diff_attention_mixer(h, df_in[j], df_q_norm_g[j], df_k_norm_g[j],
                                              df_lq1[j], df_lk1[j], df_lq2[j], df_lk2[j],
                                              df_subln_g[j], diff_lambda_init(layer))
        mem_out = memory_cross_attention(q_mem, k_mem, v_mem, mem_q_norm_g[layer],
                                         mem_k_norm_g[layer])
        x = x + jnp.concatenate([mix, mem_out], axis=-1) @ w_out[layer]
        u = rms_norm(x, norm_ffn_g[layer]) @ w_ff1[layer]
        x = x + jnp.square(jax.nn.relu(u)) @ w_ff2[layer]
    return x


GRID_W = 64
NA_HEADS = 8
NA_KH_MAX = 8
NA_KW = 16
NA_QCB = NA_KW
NA_SPAN = 2 * NA_KW
SW_HEADS = 8
SW_KV_HEADS = 2
SW_WINDOW = 128
SW_BLOCK = 128
T5_BUCKETS = 32
T5_MAX_DIST = 128
FFN_HIDDEN = -(-8 * D_MODEL // (3 * 256)) * 256

A_W = NA_HEADS * HEAD_DIM
B_QW = SW_HEADS * HEAD_DIM
B_KVW = SW_KV_HEADS * HEAD_DIM
IN_WIDTHS = [A_W, A_W, A_W, B_QW, B_KVW, B_KVW, D_MODEL, D_MODEL]
IN_WIDTH = sum(IN_WIDTHS)
IN_SPLITS = list(np.cumsum(IN_WIDTHS)[:-1])
NEG_INF = -1e30


def rms_norm_2(x, g):
    xf = x.astype(jnp.float32)
    y = xf * lax.rsqrt(jnp.mean(xf * xf, axis=-1, keepdims=True) + RMS_EPS)
    return y.astype(x.dtype) * g

def t5_bucket(rel):
    half = T5_BUCKETS // 2
    max_exact = half // 2
    ret = (rel > 0).astype(np.int32) * half
    n = np.abs(rel)
    large = max_exact + (np.log(np.maximum(n, 1) / max_exact)
                         / np.log(T5_MAX_DIST / max_exact) * (half - max_exact)).astype(np.int32)
    large = np.minimum(large, half - 1)
    return ret + np.where(n < max_exact, n, large)

def neighbourhood_attention(q, k, v, rpb):
    B, T, H, D = q.shape
    rows = T // GRID_W
    kh = min(NA_KH_MAX, rows)
    ncb = GRID_W // NA_QCB
    r = np.arange(rows)
    row_start = np.clip(r - kh // 2, 0, rows - kh)
    key_rows = row_start[:, None] + np.arange(kh)[None, :]
    j = np.arange(ncb)
    span_start = np.clip(j * NA_QCB - NA_KW // 2, 0, GRID_W - NA_SPAN)
    key_cols = span_start[:, None] + np.arange(NA_SPAN)[None, :]
    q_cols = j[:, None] * NA_QCB + np.arange(NA_QCB)[None, :]
    win_start = np.clip(q_cols - NA_KW // 2, 0, GRID_W - NA_KW)
    kc = key_cols[:, None, :]
    in_win = (kc >= win_start[..., None]) & (kc < win_start[..., None] + NA_KW)

    idx = (key_rows[:, None, :, None] * GRID_W + key_cols[None, :, None, :]).reshape(rows, ncb, kh * NA_SPAN)
    kg = jnp.take(k, idx, axis=1)
    vg = jnp.take(v, idx, axis=1)
    qb = q.reshape(B, rows, ncb, NA_QCB, H, D)
    s = jnp.einsum('brjqhd,brjkhd->brjhqk', qb, kg,
                   preferred_element_type=jnp.float32) * (HEAD_DIM ** -0.5)

    dr = key_rows - r[:, None] + (NA_KH_MAX - 1)
    dc = np.clip(kc - q_cols[..., None], -(NA_KW - 1), NA_KW - 1) + (NA_KW - 1)
    bias = rpb[dr[:, None, None, :, None], dc[None, :, :, None, :]]
    bias = jnp.transpose(bias, (0, 1, 5, 2, 3, 4)).astype(jnp.float32)
    bias = jnp.where(in_win[None, :, None, :, None, :], bias, NEG_INF)
    bias = bias.reshape(rows, ncb, H, NA_QCB, kh * NA_SPAN)
    p = jax.nn.softmax(s + bias[None], axis=-1)
    o = jnp.einsum('brjhqk,brjkhd->brjqhd', p.astype(v.dtype), vg)
    return o.reshape(B, T, H, D)

def sliding_window_attention(q, k, v, sink, t5_table):
    B, T, H, D = q.shape
    kvh = k.shape[2]
    g = H // kvh
    nb = T // SW_BLOCK
    pad = ((0, 0), (SW_BLOCK, SW_BLOCK), (0, 0), (0, 0))
    kp = jnp.pad(k, pad).reshape(B, nb + 2, SW_BLOCK, kvh, D)
    vp = jnp.pad(v, pad).reshape(B, nb + 2, SW_BLOCK, kvh, D)
    kw = jnp.concatenate([kp[:, :-2], kp[:, 1:-1], kp[:, 2:]], axis=2)
    vw = jnp.concatenate([vp[:, :-2], vp[:, 1:-1], vp[:, 2:]], axis=2)
    qb = q.reshape(B, nb, SW_BLOCK, kvh, g, D)
    s = jnp.einsum('bnqkgd,bnskd->bnkgqs', qb, kw,
                   preferred_element_type=jnp.float32) * (HEAD_DIM ** -0.5)

    rel = np.arange(3 * SW_BLOCK)[None, :] - SW_BLOCK - np.arange(SW_BLOCK)[:, None]
    bias = t5_table[t5_bucket(rel)]
    bias = jnp.transpose(bias, (2, 0, 1)).reshape(kvh, g, SW_BLOCK, 3 * SW_BLOCK).astype(jnp.float32)
    key_pos = np.arange(nb)[:, None] * SW_BLOCK + np.arange(3 * SW_BLOCK)[None, :] - SW_BLOCK
    valid = (np.abs(rel) <= SW_WINDOW)[None] & ((key_pos >= 0) & (key_pos < T))[:, None, :]
    s = jnp.where(valid[None, :, None, None], s + bias[None, None], NEG_INF)

    sk = sink.astype(jnp.float32).reshape(1, 1, kvh, g, 1, 1)
    m = jnp.maximum(jnp.max(s, axis=-1, keepdims=True), sk)
    e = jnp.exp(s - m)
    p = e / (jnp.sum(e, axis=-1, keepdims=True) + jnp.exp(sk - m))
    o = jnp.einsum('bnkgqs,bnskd->bnqkgd', p.astype(v.dtype), vw)
    return o.reshape(B, T, H, D)

def second_inputs(seed: int = 0) -> dict:
    key = jax.random.key(seed)
    ks = jax.random.split(key, 18)
    f32 = jnp.float32

    def w(k, shape, fan_in):
        return jax.random.normal(k, shape, f32) * fan_in ** -0.5

    def gain(k, shape):
        return 1.0 + 0.05 * jax.random.normal(k, shape, f32)

    return {
        "x": jax.random.normal(ks[0], (BATCH, SEQ, D_MODEL), f32),
        "norm_mix": gain(ks[1], (DEPTH, D_MODEL)),
        "w_in": w(ks[2], (DEPTH, D_MODEL, IN_WIDTH), D_MODEL),
        "q_norm_a": gain(ks[3], (DEPTH, HEAD_DIM)),
        "k_norm_a": gain(ks[4], (DEPTH, HEAD_DIM)),
        "rpb_a": 0.1 * jax.random.normal(ks[5], (DEPTH, 2 * NA_KH_MAX - 1, 2 * NA_KW - 1, NA_HEADS), f32),
        "q_norm_b": gain(ks[6], (DEPTH, HEAD_DIM)),
        "k_norm_b": gain(ks[7], (DEPTH, HEAD_DIM)),
        "sink_b": 1.0 + 0.5 * jax.random.normal(ks[8], (DEPTH, SW_HEADS), f32),
        "t5_table": 0.1 * jax.random.normal(ks[9], (T5_BUCKETS, SW_HEADS), f32),
        "w_branch_a": w(ks[10], (DEPTH, A_W, D_MODEL), A_W),
        "w_branch_b": w(ks[11], (DEPTH, B_QW, D_MODEL), B_QW),
        "w_out": w(ks[12], (DEPTH, D_MODEL, D_MODEL), D_MODEL),
        "norm_ffn": gain(ks[13], (DEPTH, D_MODEL)),
        "w_gate": w(ks[14], (DEPTH, D_MODEL, FFN_HIDDEN), D_MODEL),
        "w_up": w(ks[15], (DEPTH, D_MODEL, FFN_HIDDEN), D_MODEL),
        "w_down": w(ks[16], (DEPTH, FFN_HIDDEN, D_MODEL), FFN_HIDDEN),
    }

def second_block(x, norm_mix, w_in, q_norm_a, k_norm_a, rpb_a, q_norm_b, k_norm_b, sink_b,
              t5_table, w_branch_a, w_branch_b, w_out, norm_ffn, w_gate, w_up, w_down):
    B, T, _ = x.shape
    for l in range(DEPTH):
        h = rms_norm_2(x, norm_mix[l])
        proj = jnp.einsum('btd,de->bte', h, w_in[l])
        q_a, k_a, v_a, q_b, k_b, v_b, g_a, g_b = jnp.split(proj, IN_SPLITS, axis=-1)

        q_a = rms_norm_2(q_a.reshape(B, T, NA_HEADS, HEAD_DIM), q_norm_a[l])
        k_a = rms_norm_2(k_a.reshape(B, T, NA_HEADS, HEAD_DIM), k_norm_a[l])
        v_a = v_a.reshape(B, T, NA_HEADS, HEAD_DIM)
        o_a = neighbourhood_attention(q_a, k_a, v_a, rpb_a[l]).reshape(B, T, A_W)

        q_b = rms_norm_2(q_b.reshape(B, T, SW_HEADS, HEAD_DIM), q_norm_b[l])
        k_b = rms_norm_2(k_b.reshape(B, T, SW_KV_HEADS, HEAD_DIM), k_norm_b[l])
        v_b = v_b.reshape(B, T, SW_KV_HEADS, HEAD_DIM)
        o_b = sliding_window_attention(q_b, k_b, v_b, sink_b[l], t5_table).reshape(B, T, B_QW)

        y = (jax.nn.sigmoid(g_a) * jnp.einsum('bte,ed->btd', o_a, w_branch_a[l])
             + jax.nn.sigmoid(g_b) * jnp.einsum('bte,ed->btd', o_b, w_branch_b[l]))
        x = x + jnp.einsum('btd,de->bte', y, w_out[l])

        h = rms_norm_2(x, norm_ffn[l])
        u = jax.nn.silu(jnp.einsum('btd,df->btf', h, w_gate[l])) * jnp.einsum('btd,df->btf', h, w_up[l])
        x = x + jnp.einsum('btf,fd->btd', u, w_down[l])
    return x


def setup_inputs(seed=0):
    out = dict(first_inputs(seed))
    for name, value in second_inputs(seed + 1).items():
        if name != "x":
            out[name + "_2"] = value
    return out


def reference(
    x, mem, norm_mix_g, norm_ffn_g, w_out, w_ff1, w_ff2, mem_norm_g, w_mem_kv, mem_q_norm_g,
    mem_k_norm_g, rw_in, rw_mu, rw_w0, rw_w2, rw_a0, rw_a2, rw_g2, rw_k_k, rw_k_a, rw_r_k,
    rw_lnx_g, rw_lnx_b, df_in, df_q_norm_g, df_k_norm_g, df_lq1, df_lk1, df_lq2, df_lk2,
    df_subln_g, norm_mix_2, w_in_2, q_norm_a_2, k_norm_a_2, rpb_a_2, q_norm_b_2, k_norm_b_2,
    sink_b_2, t5_table_2, w_branch_a_2, w_branch_b_2, w_out_2, norm_ffn_2, w_gate_2, w_up_2,
    w_down_2,
):
    x = first_block(
        x, mem, norm_mix_g, norm_ffn_g, w_out, w_ff1, w_ff2, mem_norm_g, w_mem_kv, mem_q_norm_g,
        mem_k_norm_g, rw_in, rw_mu, rw_w0, rw_w2, rw_a0, rw_a2, rw_g2, rw_k_k, rw_k_a, rw_r_k,
        rw_lnx_g, rw_lnx_b, df_in, df_q_norm_g, df_k_norm_g, df_lq1, df_lk1, df_lq2, df_lk2,
        df_subln_g,
    )
    return second_block(
        x, norm_mix_2, w_in_2, q_norm_a_2, k_norm_a_2, rpb_a_2, q_norm_b_2, k_norm_b_2,
        sink_b_2, t5_table_2, w_branch_a_2, w_branch_b_2, w_out_2, norm_ffn_2, w_gate_2, w_up_2,
        w_down_2,
    )


_drawn_inputs = setup_inputs


def setup_inputs(seed=0):
    import zlib

    import numpy as np

    out = dict(_drawn_inputs(seed))
    spreads = {}
    factors = {'mem_norm_g': 8.0,
     'mem_q_norm_g': 8.0,
     'mem_k_norm_g': 8.0,
     'rw_w2': 5.353,
     'rw_a0': 3.283,
     'rw_k_k': 2.709,
     'rw_lnx_b': 8.0,
     'norm_mix_2': 5.753,
     'q_norm_a_2': 8.0,
     'k_norm_a_2': 8.0,
     'rpb_a_2': 8.0,
     'q_norm_b_2': 8.0,
     'k_norm_b_2': 8.0,
     'sink_b_2': 8.0,
     't5_table_2': 8.0,
     'norm_ffn_2': 8.0}
    for name, (base, spread) in spreads.items():
        noise = np.random.default_rng([zlib.crc32(name.encode()), seed]).standard_normal(out[name].shape)
        drawn = base * np.exp(spread * noise) if base else spread * noise
        out[name] = jnp.asarray(drawn.astype(out[name].dtype))
    for name, factor in factors.items():
        out[name] = (out[name] * factor).astype(out[name].dtype)
    return out
```

```python
import numpy as np

import concourse.bass as bass
from concourse import mybir

F = mybir.dt.float32
R = mybir.dt.float32r
ALU = mybir.AluOpType
ACT = mybir.ActivationFunctionType
AXX = mybir.AxisListType.X

T = 512
NP = 6
NC = 8
LEVELS = (1, 2, 4, 8, 16, 32)
DECAY = 0.6065306597126334
RMS_EPS = 1e-6
GN_EPS = 64e-5

CONSTS = [("bd1", 128), ("bd64", 128), ("mean", 128), ("ident", 128), ("i2", 64), ("bd", 128),
          ("mneg", 128), ("mpos", 128), ("inclneg", 64), ("inclpos", 64), ("level", 64 * 6),
          ("scan", 512), ("one", 1), ("rmseps", 1), ("gneps", 1), ("zero", 1)]
VECS = [("gmem", 8), ("gmix", 8), ("gffn", 8), ("mu", 20), ("w0", 6), ("a0", 6), ("kk", 6),
        ("ka", 6), ("rk", 6), ("lng", 6), ("lnb", 6), ("gmix2", 8), ("gffn2", 8), ("mq", 1),
        ("mk", 1), ("qa", 1), ("ka2", 1), ("qb", 1), ("kb", 1), ("sink", 8)]


def offsets(table):
    at, out = 0, {}
    for name, n in table:
        out[name] = (at, n)
        at += n
    return out, at


C_AT, NCST = offsets(CONSTS)
V_AT, NVEC = offsets(VECS)
NDER = 20 + 6 + 3


class Engine:

    def __init__(self, sem, in_turn=False):
        self.sem, self.ops, self.n, self.seen, self.in_turn = sem, [], 0, {}, in_turn

    def waits(self, need):
        found = {}
        for t in need:
            if t is None:
                continue
            if isinstance(t, list):
                for w in self.waits(t):
                    found[w[0].name] = max(found.get(w[0].name, w), w, key=lambda x: x[1])
            else:
                found[t[0].name] = max(found.get(t[0].name, t), t, key=lambda x: x[1])
        return list(found.values())

    def put(self, fn, need, sem=None, by=1):
        if self.in_turn and self.n:
            need = [*need, (self.sem, self.n)]
        w = [x for x in self.waits(need) if self.seen.get(x[0].name, 0) < x[1]]
        for s, v in w:
            self.seen[s.name] = v
        self.ops.append([w, fn, sem, by])

    def tick(self):
        last = self.ops[-1]
        if last[2] is None:
            last[2] = self.sem
            self.n += 1
        return (self.sem, self.n)

    def step(self, fn, *need):
        self.put(fn, need)
        return self.tick()

    def emit(self, eng):
        for w, fn, sem, by in self.ops:
            for s, v in w:
                eng.wait_ge(s, v)
            ins = fn(eng)
            if sem is not None:
                ins.then_inc(sem, by)


class Ring:

    def __init__(self, items):
        self.items, self.last, self.i = items, [[] for _ in items], 0

    def take(self):
        k = self.i
        self.i = (k + 1) % len(self.items)
        last = self.last[k]
        assert last is not None
        self.last[k] = None
        return k, self.items[k], last

    def free(self, k, *toks):
        self.last[k] = list(toks)


class Act:

    def __init__(self, hi, lo, n):
        self.hi, self.lo, self.tok = hi, lo, [None] * n


def run(gen):
    for _ in gen:
        pass


def block_program(nc, xT, memT, wts, vecs, cst, w2a2, g2, biasA, biasB, out, units):
    sem_of = {}

    def sem(name):
        sem_of[name] = nc.alloc_semaphore(name)
        return sem_of[name]

    pe, dve, act, pool, sp = (Engine(sem("s_" + n), n == "pool")
                              for n in ("pe", "dve", "act", "pool", "sp"))

    base0 = 16640
    top = [base0]

    def sb(name, shape, dt=F):
        n = 4
        for d in shape[1:]:
            n *= d
        n = (n + 31) // 32 * 32
        t = nc.alloc_sbuf_tensor_at(name, list(shape), dt, offset=top[0])
        top[0] += n
        return t

    def sb_at(name, shape, dt, offset):
        return nc.alloc_sbuf_tensor_at(name, list(shape), dt, offset=offset)

    banks = [nc.alloc_psum_tensor(f"bank{i}", [128, 512], F) for i in range(8)]
    D, M, O = Ring(banks[0:2]), Ring(banks[2:7]), Ring(banks[7:8])

    C = sb("C", [128, NCST])
    V = sb("V", [128, NVEC])
    VD = sb("VD", [128, NDER])
    Hhi, Hlo = sb("Hhi", [128, 8, T], R), sb("Hlo", [128, 8, T], R)
    Uhi, Ulo = sb("Uhi", [128, 8, T], R), sb("Ulo", [128, 8, T], R)
    NW = 3
    Wraw = Ring([sb(f"Wraw{i}", [128, 1024]) for i in range(NW)])
    Wsp = Ring([(sb(f"Whi{i}", [128, 1024], R), sb(f"Wlo{i}", [128, 1024], R)) for i in range(NW)])
    SQ = None

    def c(name, a=0, n=None):
        o, w = C_AT[name]
        return C[:, o + a:o + a + (w if n is None else n)]

    def v(name, j=0):
        o, w = V_AT[name]
        return V[:, o + j:o + j + 1]

    def mm(o, lhsT, rhs, start, stop, *need):
        pe.put(lambda e: e.matmul(o, lhsT, rhs, start=start, stop=stop, skip_group_check=True), need)

    def transpose(o, i, ident, *need):
        pe.put(lambda e: e.transpose(o, i, ident), need)

    def tt(E, o, a, b, op, *need):
        return E.step(lambda e: e.tensor_tensor(o, a, b, op), *need)

    def stt(o, a, s, b, op0, op1, *need):
        return dve.step(lambda e: e.scalar_tensor_tensor(o, a, s, b, op0, op1), *need)

    def ts(E, o, a, s1, s2, op0, op1, *need):
        if s2 is None:
            return E.step(lambda e: e.tensor_scalar(o, a, s1, None, op0), *need)
        return E.step(lambda e: e.tensor_scalar(o, a, s1, s2, op0, op1), *need)

    def actf(o, a, f, scale, bias, *need):
        if bias is None:
            return act.step(lambda e: e.activation(o, a, f, scale=scale), *need)
        return act.step(lambda e: e.activation(o, a, f, scale=scale, bias=bias), *need)

    def copy(E, o, a, *need):
        if E is act:
            return act.step(lambda e: e.copy(o, a), *need)
        return E.step(lambda e: e.tensor_copy(o, a), *need)

    def recip(o, a, *need):
        return dve.step(lambda e: e.reciprocal(o, a), *need)

    n_load = [0]

    def load(o, i, *need):
        s = sem(f"ld{n_load[0]}")
        n_load[0] += 1
        sp.put(lambda e: e.dma_start(o, i), need, s, 16)
        return (s, 16)

    def split(hi, lo, src, *need):
        a = copy(act, hi, src, *need)
        b = tt(dve, lo, src, hi.bitcast(F), ALU.subtract, a, *need)
        return [a, b]

    t_c = load(C[:], cst)
    t_v = load(V[:], vecs)

    omu, oka = VD[:, 0:20], VD[:, 20:26]
    mu_all = V[:, V_AT["mu"][0]:V_AT["mu"][0] + 20]
    ka_all = V[:, V_AT["ka"][0]:V_AT["ka"][0] + 6]
    t_vd = [ts(dve, omu, mu_all, -1.0, 1.0, ALU.mult, ALU.add, t_v),
            ts(dve, oka, ka_all, -1.0, 1.0, ALU.mult, ALU.add, t_v)]
    scaled = {}
    for i, name in enumerate(("mq", "qa", "qb")):
        scaled[name] = VD[:, 26 + i:27 + i]
        t_vd.append(ts(dve, scaled[name], v(name), 0.125, None, ALU.mult, None, t_v))

    class Stream:
        def __init__(self):
            self.loads, self.splits, self.got = [], [], 0
            self.sems = [sem(f"w{i}") for i in range(NW)]

        def advance(self, n_split):
            while len(self.splits) < min(n_split, len(units)):
                while len(self.loads) < min(len(self.splits) + NW, len(units)):
                    u = len(self.loads)
                    k, raw, last = Wraw.take()
                    width = units[u][1]
                    s = self.sems[k]
                    sp.put(lambda e, raw=raw, u=u, width=width:
                           e.dma_start(raw[:, 0:width], wts[u, :, 0:width]), [last], s, 16)
                    self.loads.append((k, raw, (s, 16 * (u // NW + 1))))
                u = len(self.splits)
                k, raw, tok = self.loads[u]
                width = units[u][1]
                kk, (hi, lo), last = Wsp.take()
                toks = split(hi[:, 0:width], lo[:, 0:width], raw[:, 0:width], tok, last)
                Wraw.free(k, toks)
                self.splits.append((kk, hi, lo, toks))

        def get(self, name):
            u = self.got
            assert units[u][0] == name, (units[u][0], name)
            self.got += 1
            self.advance(u + NW - 1)
            return self.splits[u]

        def free(self, unit, tok):
            Wsp.free(unit[0], tok)

    W = Stream()

    def mm3(o, whi, wlo, xhi, xlo, first, last, *need):
        mm(o, whi, xhi, first, False, *need)
        mm(o, wlo, xhi, False, False)
        mm(o, whi, xlo, False, last)

    def tile_t(name, a, ks, epi, n=T, j0=0, keep=None, hold=None, bank=None):
        unit = keep if keep is not None else W.get(name)
        if bank is None:
            b, bank, rel = D.take()
        else:
            b, rel = None, None
        for i, k in enumerate(ks):
            j = (j0 + i) * 128
            mm3(bank[:, 0:n], unit[1][:, j:j + 128], unit[2][:, j:j + 128], a.hi[:, k, 0:n],
                a.lo[:, k, 0:n], i == 0, i == len(ks) - 1, unit[3], rel, a.tok[k])
            yield
        t = pe.tick()
        if hold is None:
            W.free(unit, t)
        else:
            hold.append(unit)
        done = epi(bank, t)
        if b is not None:
            D.free(b, done)

    def rms_t(xs, toks, sq, tsq, gname, H, tmp, small, n=T, by_column=False):
        k, bank, rel = M.take()
        mm(bank[:, 0:n], c("mean"), sq, True, True, rel, tsq, t_c)
        t = pe.tick()
        rs = small[:, 0:n]
        a = actf(rs, bank[:, 0:n], ACT.Sqrt, 1.0, c("rmseps"), t)
        M.free(k, a)
        r = recip(rs, rs, a)
        for i, x in enumerate(xs):
            q, tile, last = tmp.take()
            m = stt(tile[:, 0:n], x, v(gname, i), rs, ALU.mult, ALU.mult, r, last, toks[i], t_v)
            hi, lo, src = H.hi[:, i, 0:n], H.lo[:, i, 0:n], tile[:, 0:n]
            if by_column:
                hi, lo, src = columns(hi), columns(lo), rows(src)
            H.tok[i] = split(hi, lo, src, m, hfree[0])
            tmp.free(q, H.tok[i])

    hfree = [[]]

    def rows(ap):
        return ap.rearrange("p (r c) -> p r c", r=8)

    def columns(ap):
        return ap.rearrange("p (c r) -> p r c", r=8)

    def squares(xs, toks, acc, tmp, n=T):
        last = None
        for i, x in enumerate(xs):
            if i == 0:
                last = actf(acc, x, ACT.Square, 1.0, None, toks[i])
                continue
            q, tile, free = tmp.take()
            a = actf(tile[:, 0:n], x, ACT.Square, 1.0, None, toks[i], free)
            last = tt(pool, acc, acc, tile[:, 0:n], ALU.add, a, last)
            tmp.free(q, last)
        return last


    def squares_step(i, x, tok, acc, tmp, last, n=T):
        if i == 0:
            return actf(acc[:, 0:n], x, ACT.Square, 1.0, None, tok, last)
        q, tile, free = tmp.take()
        a = actf(tile[:, 0:n], x, ACT.Square, 1.0, None, tok, free)
        last = tt(pool, acc[:, 0:n], acc[:, 0:n], tile[:, 0:n], ALU.add, a, last)
        tmp.free(q, last)
        return last

    def load_on(E, o, i, s, count, *need):
        E.put(lambda e: e.dma_start(o, i), need, s, 16)
        return (s, 16 * count)

    pend = []

    def flush():
        while pend:
            pend.pop(0)()

    def fence():
        return [e.tick() for e in (pe, dve, act, pool) if e.ops]

    def softmax(bank, n, bias, sink, ring, stats, need):
        q, s, last = ring.take()
        z, st, slast = stats.take()
        s = s[:, 0:n]
        if bias is None:
            src, d = bank, need
        else:
            src = s
            d = tt(dve, s, bank, bias, ALU.add, need, last)
        m = dve.step(lambda e: e.tensor_reduce(st[:, 0:1], src, AXX, ALU.max), d, slast)
        if sink is None:
            m = ts(dve, st[:, 1:2], st[:, 0:1], -1.0, None, ALU.mult, None, m)
        else:
            m = ts(dve, st[:, 1:2], st[:, 0:1], sink, -1.0, ALU.max, ALU.mult, m)
        x = act.step(lambda e: e.activation(s, src, ACT.Exp, scale=1.0, bias=st[:, 1:2],
                                            accum_out=st[:, 2:3]), m, last)
        r = x
        if sink is not None:
            y = actf(st[:, 4:5], sink, ACT.Exp, 1.0, st[:, 1:2], m)
            r = tt(dve, st[:, 2:3], st[:, 2:3], st[:, 4:5], ALU.add, x, y)
        r = recip(st[:, 3:4], st[:, 2:3], r)
        r = ts(dve, s, s, st[:, 3:4], None, ALU.mult, None, r)
        stats.free(z, r)
        return q, s, r, [d, x] if bias is None else [d]

    def pipeline(items, depth):
        items, active = list(items), []
        while items or active:
            if items and len(active) < depth:
                active.append(items.pop(0))
            for g in list(active):
                try:
                    next(g)
                except StopIteration:
                    active.remove(g)
            yield

    def weave(main, filler, per):
        for _ in main:
            for _ in range(per):
                next(filler, None)

    def head_norm(src, dst, view, gain, need, tmp, eps_tok):
        q, raw, last = tmp.take()
        q2, sq, last2 = tmp.take()
        a = copy(dve, raw[:, 0:src.shape[1]], src, need, last)
        b = actf(sq[:, 0:src.shape[1]], raw[:, 0:src.shape[1]], ACT.Square, 1.0, None, a, last2)
        n = src.shape[1]

        def rest():
            k, bank, rel = M.take()
            mm(bank[:, 0:n], c("bd64"), sq[:, 0:n], True, True, rel, b, t_c)
            t = pe.tick()
            x = actf(sq[:, 0:n], bank[:, 0:n], ACT.Sqrt, 1.0, c("rmseps"), t)
            M.free(k, x)
            y = recip(sq[:, 0:n], sq[:, 0:n], x)
            z = dst(raw[:, 0:n], gain, sq[:, 0:n], [y, a])
            tmp.free(q, z)
            tmp.free(q2, z)
        pend.append(rest)
        return [a]

    arena = top[0]
    slab = [sb(f"slab{i}", [128, T]) for i in range(3)]
    WA, GD = sb("WA", [128, T]), sb("GD", [128, T])
    w2s, g2s = sb("w2s", [128, 768]), sb("g2s", [128, 768])
    low = top[0]

    memX = sb("memX", [128, 8, 256])
    memH = Act(sb("memHhi", [128, 8, 256], R), sb("memHlo", [128, 8, 256], R), 8)
    x0 = sb("x0", [128, 8, T])
    tmps = Ring([sb(f"tmp{i}", [128, T]) for i in range(4)])
    acc, small = sb("acc", [128, T]), sb("small", [128, T])
    km, vm = sb("km", [128, 2, 256]), sb("vm", [128, 2, 256])
    qm = sb("qm", [128, 2, T])
    sring = Ring([sb(f"ms{i}", [128, 256]) for i in range(3)])
    mstats = Ring([sb(f"mst{i}", [128, 8]) for i in range(3)])
    pTm = Ring([sb(f"pTm{i}", [128, 2, T]) for i in range(2)])
    assert top[0] <= nc.sbuf_usable_end

    H, U = Act(Hhi, Hlo, 8), Act(Uhi, Ulo, 8)

    t_m = [load(memX[:, 4 * i:4 * i + 4, :], memT[4 * i:4 * i + 4].rearrange("k p n -> p k n"))
           for i in range(2)]
    t_x = [load(x0[:, 2 * i:2 * i + 2, :], xT[2 * i:2 * i + 2].rearrange("k p n -> p k n"))
           for i in range(4)]
    t_w2, t_g2 = load(w2s[:], w2a2), load(g2s[:], g2)
    W.advance(2)

    last = None
    for i in range(8):
        last = squares_step(i, memX[:, i, :], t_m[i // 4], acc, tmps, last, 256)
    rms_t([memX[:, i, :] for i in range(8)], [t_m[i // 4] for i in range(8)], acc[:, 0:256], last,
          "gmem", memH, tmps, small, 256)
    accfree = pe.tick()
    last = None
    for i in range(8):
        last = squares_step(i, x0[:, i, :], t_x[i // 2], acc, tmps, last if i else accfree)
    rms_t([x0[:, i, :] for i in range(8)], [t_x[i // 2] for i in range(8)], acc[:], last, "gmix", H,
          tmps, small)

    t_km = [None, None]

    def km_epi(i):
        def epi(bank, t):
            def dst(raw, gain, rs, need):
                a = tt(dve, km[:, i, :], raw, rs, ALU.mult, need)
                t_km[i] = ts(dve, km[:, i, :], km[:, i, :], gain, None, ALU.mult, None, a)
                return t_km[i]
            return head_norm(bank[:, 0:256], dst, None, v("mk"), t, tmps, None)
        return epi

    for i in range(2):
        run(tile_t(("memk", i), memH, range(8), km_epi(i), n=256))
    got = [M.take(), M.take()]
    for u in range(2):
        unit = W.get(("memv", u))
        for m in range(2):
            k_, bank, rel = got[m]
            for i in range(4):
                k = 4 * u + i
                xh, xl = memH.hi[:, k, 128 * m:128 * m + 128], memH.lo[:, k, 128 * m:128 * m + 128]
                wh, wl = unit[1][:, 256 * i:256 * i + 256], unit[2][:, 256 * i:256 * i + 256]
                o = bank[:, 0:256]
                mm(o, xh, wh, k == 0, False, unit[3], rel, memH.tok[k])
                mm(o, xh, wl, False, False)
                mm(o, xl, wh, False, k == 7)
        W.free(unit, pe.tick())
    t = pe.tick()
    t_vm = []
    for m in range(2):
        t_vm.append(copy(act, vm[:, m, :], got[m][1][:, 0:256], t))
        M.free(got[m][0], t_vm[-1])
    flush()

    t_qm = [None, None]

    def qm_epi(i):
        def epi(bank, t):
            def dst(raw, gain, rs, need):
                t_qm[i] = stt(qm[:, i, :], raw, gain, rs, ALU.mult, ALU.mult, need, t_vd)
                return t_qm[i]
            return head_norm(bank[:], dst, None, scaled["mq"], t, tmps, None)
        return epi

    for i in range(2):
        run(tile_t(("rw", 20 + i), H, range(8), qm_epi(i)))
        flush()

    def transposed(p, n, dst, need, pt_ring_tok):
        k, bank, rel = M.take()
        for b in range(n // 128):
            transpose(bank[:, 128 * b:128 * b + 128], p[:, 128 * b:128 * b + 128], c("ident"),
                      rel, need, t_c)
        t = pe.tick()
        d = copy(dve, dst, bank[:, 0:n].rearrange("p (b x) -> p b x", x=128), t, pt_ring_tok)
        M.free(k, d)
        return t, d

    def mem_head(h, state):
        off, kt = 64 * (h % 2), h // 2
        q, pT, plast = pTm.take()
        pt = []

        def item(j):
            k, bank, rel = M.take()
            mm(bank[:, 0:256], qm[off:off + 64, kt, 128 * j:128 * j + 128], km[off:off + 64, kt, :],
               True, True, rel, t_qm[kt], t_km[kt])
            t = pe.tick()
            z, p, r, free = softmax(bank[:, 0:256], 256, None, None, sring, mstats, t)
            M.free(k, free)
            yield
            yield
            a, d = transposed(p, 256, pT[:, :, 128 * j:128 * j + 128], r, plast)
            sring.free(z, a)
            pt.append(d)

        yield from pipeline([item(j) for j in range(4)], 2)
        if h % 2 == 0:
            state["bank"] = O.take()
        kd, bank, rel = state["bank"]
        for b in range(2):
            mm(bank[off:off + 64, :], vm[:, b, 64 * h:64 * h + 64], pT[:, b, :], b == 0, b == 1,
               rel, t_vm, pt)
        t = pe.tick()
        pTm.free(q, t)
        if h % 2:
            U.tok[6 + kt] = split(Uhi[:, 6 + kt, :], Ulo[:, 6 + kt, :], bank[:], t)
            O.free(kd, U.tok[6 + kt])
        yield

    def mem_attention():
        state = {}
        for h in range(4):
            yield from mem_head(h, state)

    t_lora = {}

    def shift(dst, bank, j, t, *need):
        a = actf(dst[:], bank[:], ACT.Copy, omu[:, j:j + 1], None, t, t_vd, *need)
        return stt(dst[:, 1:T], bank[:, 0:T - 1], v("mu", j), dst[:, 1:T], ALU.mult, ALU.add, a)

    def wa_epi(bank, t):
        d = shift(WA, bank, 18, t)
        t_lora["wa"] = [d, actf(WA[0:64, :], WA[0:64, :], ACT.Tanh, 1.0, None, d)]
        return [d]

    def gd_epi(bank, t):
        d = shift(GD, bank, 19, t)
        t_lora["gd"] = actf(GD[:], GD[:], ACT.Sigmoid, 1.0, None, d)
        return [d]

    t_slab, slab_free = [None] * 3, [[], [], []]

    def slab_epi(i, j):
        def epi(bank, t):
            t_slab[i] = shift(slab[i], bank, j, t, slab_free[i])
            return [t_slab[i]]
        return epi

    def projections(p):
        for i in range(3):
            yield from tile_t(("rw", 6 * i + p), H, range(8), slab_epi(i, 6 * i + p))

    def early():
        yield from tile_t(("rw", 18), H, range(8), wa_epi)
        yield from tile_t(("rw", 19), H, range(8), gd_epi)
        yield from projections(0)

    filler = early()
    weave(mem_attention(), filler, 1)
    run(filler)
    flush()
    old = fence()

    top[0] = low

    def tile2(name):
        return sb(name, [128, T])

    def tile4(name):
        return sb(name, [128, NC, 128])

    sg, cum, Pi, ta, kf, kn, tm, bonus = (tile2(n) for n in
                                          ("sg", "cum", "Pi", "ta", "kf", "kn", "tm", "bonus"))
    Pp = sb("Pp", [128, NC, 65])
    AR, BDb, BDk, BDa, BDv = (tile4(n) for n in ("AR", "BDb", "BDk", "BDa", "BDv"))
    MT, AK, BR, Bnbd, Kbd, Vbd, GA = (tile4(n) for n in
                                      ("MT", "AK", "BR", "Bnbd", "Kbd", "Vbd", "GA"))
    RK, Vs, PD, yc = (sb(n, [128, NC, 64]) for n in ("RK", "Vs", "PD", "yc"))
    XY = sb("XY", [128, 2, 2, 4, 64])
    T1 = sb("T1", [128, NC, 64])
    assert top[0] <= nc.sbuf_usable_end, top[0]
    T1bd, Ybd, U0bd, W1bd, Phi, Sbd, UW = BDb, BDk, BDa, BDv, Kbd, Bnbd, MT
    ysb = T1

    for i, b in enumerate((BDb, BDk, BDa, BDv, Bnbd, Kbd, Vbd)):
        t_z = pool.step(lambda e, b=b: e.memset(b[:], 0.0), old)
    t_z = [t_z, pool.step(lambda e: e.memset(Pp[:, :, 0:1], 1.0), old)]

    def half(bd, h, c0=0, c1=NC):
        return bd[64 * h:64 * h + 64, c0:c1, 64 * h:64 * h + 64]

    def stk(t, h=None, c0=0, c1=NC):
        w = t.rearrange("p (c x) -> p c x", x=64) if len(t.shape) == 2 else t
        return w[:, c0:c1, :] if h is None else w[64 * h:64 * h + 64, c0:c1, :]

    r_, k_, v_ = slab
    war = {"front": [], "pair": []}

    def bcast(ap, n):
        return ap.unsqueeze(1).broadcast_to([ap.shape[0], n, ap.shape[1]])

    def pair(p):
        g = old if p == 0 else []
        free = war["pair"]
        lora = {}
        k1, b1, rel = M.take()
        mm(b1[:], w2s[0:64, 128 * p:128 * p + 128], WA[0:64, :], True, True, rel, t_w2, t_lora["wa"])
        t = pe.tick()
        a = actf(sg[:], b1[:], ACT.Sigmoid, 1.0, v("w0", p), t, g, free)
        M.free(k1, a)
        k1, b1, rel = M.take()
        mm(b1[:], w2s[64:128, 128 * p:128 * p + 128], WA[64:128, :], True, True, rel)
        t = pe.tick()
        a2 = actf(ta[:], b1[:], ACT.Sigmoid, 1.0, v("a0", p), t, g)
        M.free(k1, a2)
        yield
        d = dve.step(lambda e: e.tensor_tensor_scan(cum[:], c("scan"), sg[:], 0.0, ALU.mult, ALU.add),
                     a, g)
        sq = actf(tm[:], k_[:], ACT.Square, v("kk", p), None, t_slab[1], g)
        k1, b1, rel = M.take()
        mm(b1[:], c("bd1"), tm[:], True, True, rel, sq)
        t = pe.tick()
        e1 = actf(Pp[:, :, 1:65], stk(cum), ACT.Exp, -DECAY, None, d, t_z)
        e2 = actf(Pi[:], cum[:], ACT.Exp, DECAY, None, d)
        f = ts(dve, kf[:], ta[:], v("ka", p), oka[:, p:p + 1], ALU.mult, ALU.add, a2, t_vd)
        f = tt(dve, kf[:], kf[:], k_[:], ALU.mult, f, t_slab[1])
        yield
        x = actf(tm[:], b1[:], ACT.Sqrt, 1.0, None, t)
        M.free(k1, x)
        x = ts(dve, tm[:], tm[:], 1e-12, None, ALU.max, None, x)
        x = recip(tm[:], tm[:], x)
        kkt = stt(kn[:], k_[:], v("kk", p), tm[:], ALU.mult, ALU.mult, x)
        bt = tt(pool, ta[:], ta[:], kn[:], ALU.mult, kkt, f)
        rk = stt(tm[:], r_[:], v("rk", p), kf[:], ALU.mult, ALU.mult, kkt, t_slab[0])
        k1, b1, rel = M.take()
        mm(b1[:], c("bd1"), tm[:], True, True, rel, rk)
        t = pe.tick()
        ar = [tt(dve, AR[:, :, 64:128], stk(r_), Pp[:, :, 1:65], ALU.mult, e1, t_slab[0], free),
              tt(dve, AR[:, :, 0:64], stk(kn), Pp[:, :, 0:64], ALU.mult, e1)]
        yield
        bb = [tt(pool, half(BDk, h), stk(kf, h), stk(Pi, h), ALU.mult, e2, f, free, t_z)
              for h in range(2)]
        bb += [tt(dve, half(BDb, h), stk(ta, h), stk(Pi, h), ALU.mult, e2, bt, free, t_z)
               for h in range(2)]
        ba = [copy(act, half(BDa, h), AR[64 * h:64 * h + 64, :, 0:64], ar, free, t_z)
              for h in range(2)]
        bv = [copy(act, half(BDv, h), stk(v_, h), t_slab[2], free, t_z) for h in range(2)]
        bo = tt(dve, bonus[:], b1[:], v_[:], ALU.mult, t, t_slab[2])
        M.free(k1, bo)
        slab_free[0], slab_free[1], slab_free[2] = [ar[0], rk], [kkt, f, sq], [bv, bo]
        yield
        done = []
        for w, full, mask, mask2, o2 in ((BDb, MT, "mneg", "inclneg", BR[:, :, 64:128]),
                                         (BDk, AK, "mpos", "inclpos", RK[:])):
            for hf in range(2):
                k1, b1, rel = M.take()
                for i in range(4):
                    ch = 4 * hf + i
                    mm(b1[:, 128 * i:128 * i + 128], w[:, ch, :], AR[:, ch, :], True, True, rel, ar, bb)
                t = pe.tick()
                src = b1[:].rearrange("p (c x) -> p c x", x=128)
                first = src[:, :, 0:64].unsqueeze(2).broadcast_to([128, 4, 2, 64])
                m4 = c(mask).rearrange("p (h x) -> p h x", h=2).unsqueeze(1).broadcast_to([128, 4, 2, 64])
                o4 = full[:, 4 * hf:4 * hf + 4, :].rearrange("p c (h x) -> p c h x", h=2)
                d1 = tt(dve, o4, first, m4, ALU.mult, t)
                d2 = tt(dve, o2[:, 4 * hf:4 * hf + 4, :], src[:, :, 64:128], bcast(c(mask2), 4),
                        ALU.mult, t)
                M.free(k1, [d1, d2])
                done.append([d1, d2])
                yield
        sc = done
        nat = {}
        for name, w in (("b", BDb), ("v", BDv), ("k", BDk), ("a", BDa), ("c", MT)):
            k1, b1, rel = M.take()
            for ch in range(NC):
                mm(b1[:, 64 * ch:64 * ch + 64], w[:, ch, :], c("i2"), True, True, rel, sc, ba, bv)
            t = pe.tick()
            src = b1[:].rearrange("p (c x) -> p c x", x=64)
            if name == "c":
                d = tt(dve, T1[:], src, bcast(c("level", 0, 64), NC), ALU.mult, t)
                M.free(k1, d)
                t1 = d
                tb = [copy(act, half(T1bd, 0), stk(T1, 0), d), copy(pool, half(T1bd, 1), stk(T1, 1), d)]
            elif name == "b":
                nat["bn"] = ts(dve, BR[:, :, 0:64], src, -1.0, None, ALU.mult, None, t)
                nat["bnbd"] = [copy(pool if h else act, half(Bnbd, h), BR[64 * h:64 * h + 64, :, 0:64],
                                    nat["bn"], t_z) for h in range(2)]
                M.free(k1, nat["bn"])
            elif name == "v":
                nat["v"] = copy(dve, Vs[:], src, t)
                nat["vbd"] = [copy(pool if h else act, half(Vbd, h), stk(Vs, h), nat["v"], t_z)
                              for h in range(2)]
                M.free(k1, nat["v"])
            elif name == "k":
                nat["kbd"] = [copy(act, half(Kbd, h), src[64 * h:64 * h + 64], t, t_z) for h in range(2)]
                M.free(k1, nat["kbd"])
            else:
                nat["a"] = copy(dve, GA[:, :, 64:128], src, t)
                M.free(k1, nat["a"])
            yield

        i2b = bcast(c("i2"), 4)
        xy, ybd, t1h, tbh = [None] * 2, [None] * 2, [t1, t1], [tb, tb]
        nl = len(LEVELS)
        for l in range(nl):
            if l:
                for hf in range(2):
                    k1, b1, rel = M.take()
                    for i in range(4):
                        ch = 4 * hf + i
                        mm(b1[:, 64 * i:64 * i + 64], MT[:, ch, :], XY[:, hf, 0, i, :], True, True, rel,
                           xy[hf])
                    t = pe.tick()
                    o = T1[:, 4 * hf:4 * hf + 4, :]
                    t1h[hf] = tt(dve, o, b1[:, 0:256].rearrange("p (c x) -> p c x", x=64),
                                 bcast(c("level", 64 * l, 64), 4), ALU.mult, t)
                    M.free(k1, t1h[hf])
                    tbh[hf] = [copy(act, half(T1bd, 0, 4 * hf, 4 * hf + 4), stk(T1, 0, 4 * hf, 4 * hf + 4), t1h[hf]),
                               copy(pool, half(T1bd, 1, 4 * hf, 4 * hf + 4), stk(T1, 1, 4 * hf, 4 * hf + 4), t1h[hf])]
                    yield
            for hf in range(2):
                k1, b1, rel = M.take()
                lastl = l == nl - 1
                if l and not lastl:
                    for i in range(4):
                        ch = 4 * hf + i
                        mm(b1[:, 64 * i:64 * i + 64], Ybd[:, ch, :], T1[:, ch, :], True, True, rel,
                           t1h[hf], ybd[hf])
                for i in range(4):
                    ch = 4 * hf + i
                    rhs = XY[:, hf, 1, i, :] if l else c("i2")
                    mm(b1[:, 256 + 64 * i:320 + 64 * i], T1bd[:, ch, :], rhs, True, True, rel, tbh[hf], xy[hf])
                t = pe.tick()
                yv = b1[:, 256:512].rearrange("p (c x) -> p c x", x=64)
                if l == 0:
                    d = [tt(dve, XY[:, hf, 0], T1[:, 4 * hf:4 * hf + 4, :], i2b, ALU.add, t1h[hf]),
                         tt(dve, XY[:, hf, 1], yv, i2b, ALU.add, t)]
                elif not lastl:
                    xf = XY[:, hf].rearrange("p a c x -> p (a c x)")
                    d = [tt(dve, xf, b1[:], xf, ALU.add, t)]
                else:
                    d = [tt(dve, XY[:, hf, 1], yv, XY[:, hf, 1], ALU.add, t)]
                M.free(k1, d)
                xy[hf] = d
                ybd[hf] = [copy(act, half(Ybd, 0, 4 * hf, 4 * hf + 4), XY[0:64, hf, 1], d),
                           copy(pool, half(Ybd, 1, 4 * hf, 4 * hf + 4), XY[64:128, hf, 1], d)]
                yield
            if l == 0:
                k1, b1, rel = M.take()
                for ch in range(NC):
                    mm(b1[:, 64 * ch:64 * ch + 64], AK[:, ch, :], Vs[:, ch, :], True, True, rel, nat["v"])
                t = pe.tick()
                gv = copy(act, GA[:, :, 0:64], b1[:].rearrange("p (c x) -> p c x", x=64), t)
                M.free(k1, gv)
                yield
        uw = []
        for hf in range(2):
            k1, b1, rel = M.take()
            for i in range(4):
                ch = 4 * hf + i
                mm(b1[:, 128 * i:128 * i + 128], Ybd[:, ch, :], GA[:, ch, :], True, True, rel, ybd[hf],
                   gv, nat["a"])
            t = pe.tick()
            src = b1[:].rearrange("p (c x) -> p c x", x=128)
            cc = (4 * hf, 4 * hf + 4)
            x = [copy(dve, UW[:, 4 * hf:4 * hf + 4, :], src, t)]
            M.free(k1, x)
            for w, o in ((W1bd, 64), (U0bd, 0)):
                x += [copy(pool if h else act, half(w, h, *cc),
                           UW[64 * h:64 * h + 64, 4 * hf:4 * hf + 4, o:o + 64], x[0]) for h in range(2)]
            uw.append(x)
            yield
        k1, b1, rel = M.take()
        for ch in range(NC - 1):
            o = b1[:, 64 * ch:64 * ch + 64]
            mm(o, Bnbd[:, ch, :], UW[:, ch, 0:64], True, False, rel, nat["bnbd"], uw[ch // 4])
            mm(o, Kbd[:, ch, :], Vs[:, ch, :], False, True, nat["kbd"])
        t = pe.tick()
        pc = Pp[:, 0:NC - 1, 64:65].broadcast_to([128, NC - 1, 64])
        pd = tt(dve, PD[:, 0:NC - 1, :], b1[:, 0:448].rearrange("p (c x) -> p c x", x=64), pc, ALU.mult, t)
        M.free(k1, pd)
        yield
        ph = []
        for hf in range(2):
            k1, b1, rel = M.take()
            for i in range(4):
                ch = 4 * hf + i
                mm(b1[:, 128 * i:128 * i + 128], W1bd[:, ch, :], BR[:, ch, :], True, True, rel, uw[hf],
                   nat["bn"])
            t = pe.tick()
            src = b1[:].rearrange("p (c x) -> p c x", x=128)
            cc = (4 * hf, 4 * hf + 4)
            x = [tt(dve, half(Phi, h, *cc), src[64 * h:64 * h + 64, :, 0:64],
                    i2b[64 * h:64 * h + 64], ALU.add, t) for h in range(2)]
            o = AR[:, 4 * hf:4 * hf + 4, 64:128]
            x.append(tt(dve, o, src[:, :, 64:128], o, ALU.add, t))
            M.free(k1, x)
            ph.append(x)
            yield
        ky, yb, rel = O.take()
        for ch in range(NC):
            o = yb[:, 64 * ch:64 * ch + 64]
            mm(o, U0bd[:, ch, :], BR[:, ch, 64:128], ch == 0, False, rel)
            mm(o, Vbd[:, ch, :], RK[:, ch, :], False, ch == 0, nat["vbd"])
        st = pd
        k1, b1, rel = M.take()
        for ch in range(1, NC - 1):
            o = b1[:, 64 * ch:64 * ch + 64]
            mm(o, Phi[:, ch, :], PD[:, ch - 1, :], True, True, rel, st, ph[ch // 4])
            t = pe.tick()
            st = stt(PD[:, ch, :], o, Pp[:, ch, 64:65], PD[:, ch, :], ALU.mult, ALU.add, t)
            yield
        M.free(k1, st)
        sb_ = [copy(act if h else pool, half(Sbd, h, 0, NC - 1), PD[64 * h:64 * h + 64, 0:NC - 1, :], st)
               for h in range(2)]
        yield
        for ch in range(1, NC):
            mm(yb[:, 64 * ch:64 * ch + 64], Sbd[:, ch - 1, :], AR[:, ch, 64:128], False, True, sb_)
        t = pe.tick()
        y2 = ysb.rearrange("p c x -> p (c x)")
        z2 = yc.rearrange("p c x -> p (c x)")
        yy = copy(act, y2, yb[:], t)
        O.free(ky, yy)
        k1, b1, rel = M.take()
        mm(b1[:], c("bd64"), y2, True, True, rel, yy)
        t = pe.tick()
        war["pair"] = [t, ph]
        d = tt(dve, y2, y2, b1[:], ALU.subtract, t)
        M.free(k1, d)
        s = actf(z2, y2, ACT.Square, 1.0, None, d)
        yield
        k1, b1, rel = M.take()
        mm(b1[:], c("bd64"), z2, True, True, rel, s)
        t = pe.tick()
        x = actf(z2, b1[:], ACT.Sqrt, 1.0, c("gneps"), t)
        M.free(k1, x)
        x = recip(z2, z2, x)
        x = tt(dve, y2, y2, z2, ALU.mult, x)
        x = ts(dve, y2, y2, v("lng", p), v("lnb", p), ALU.mult, ALU.add, x)
        x = tt(dve, y2, y2, bonus[:], ALU.add, x)
        k1, b1, rel = M.take()
        mm(b1[:], g2s[:, 128 * p:128 * p + 128], GD[:], True, True, rel, t_g2, t_lora["gd"])
        t = pe.tick()
        x = tt(dve, y2, y2, b1[:], ALU.mult, x, t)
        M.free(k1, x)
        U.tok[p] = split(Uhi[:, p, :], Ulo[:, p, :], y2, x)
        war["pair"] = [war["pair"], x, U.tok[p]]
        yield

    for p in range(NP):
        filler = projections(p + 1) if p + 1 < NP else iter(())
        weave(pair(p), filler, 1)
        run(filler)
    old = fence()

    top[0] = arena
    X = sb("X", [128, 8, T])
    tmps = Ring([sb(f"tmpb{i}", [128, T]) for i in range(2)])
    sraw = [sb(f"sr{i}", [128, 384]) for i in range(6)]
    accb, smallb = sb_at("accb", [128, T], F, top[0] - 6 * 1536), sb_at("smallb", [128, T], F, top[0] - 6 * 1536 + 2048)
    xtok = [load(X[:, 4 * i:4 * i + 4, :], xT[4 * i:4 * i + 4].rearrange("k p n -> p k n"), old)
            for i in range(2) for _ in range(1)]
    xtok = [xtok[i // 4] for i in range(8)]
    for r in (tmps,):
        r.last = [[old] for _ in r.last]
    sqlast = [None]

    def residual(i, norm, sqtmp, by_column=False):
        def epi(bank, t):
            x, y = X[:, i, :], bank[:]
            if by_column:
                x, y = rows(x), columns(y)
            d = tt(dve, x, x, y, ALU.add, t, xtok[i])
            xtok[i] = d
            if norm:
                sqlast[0] = squares_step(i, X[:, i, :], d, accb, sqtmp, sqlast[0] if i else old)
            return [d]
        return epi

    def norm_x(gname, by_column=False):
        hfree[0] = pe.tick()
        rms_t([X[:, i, :] for i in range(8)], xtok, accb[:], sqlast[0], gname, H, tmps, smallb,
              by_column=by_column)

    for i in range(8):
        run(tile_t(("wo", i), U, range(8), residual(i, True, tmps)))
    norm_x("gffn")

    def ff1_epi(i):
        def epi(bank, t):
            q, tile, last = tmps.take()
            a = actf(tile[:], bank[:], ACT.Relu, 1.0, None, t, last)
            d = tt(pool, tile[:], tile[:], tile[:], ALU.mult, a)
            U.tok[i] = split(Uhi[:, i, :], Ulo[:, i, :], tile[:], d)
            tmps.free(q, U.tok[i])
            return [a]
        return epi

    for chn in range(4):
        for i in range(8):
            run(tile_t(("f1", 8 * chn + i), H, range(8), ff1_epi(i)))
        for i in range(8):
            run(tile_t(("f2", chn, i), U, range(8), residual(i, chn == 3, tmps)))
    norm_x("gmix2", True)

    qa, ka = sb("qa", [128, 4, T]), sb("ka", [128, 4, T])
    va = [sb(f"va{i}", [128, T]) for i in range(4)]
    vs = [sb(f"vs{i}", [128, T]) for i in range(3)]
    qb, kbr, vb = sb("qb", [128, 4, T]), sb("kbr", [128, 2, T]), sb("vb", [128, 4, 128])
    ga = sb("ga", [128, 8, T])
    gbt = [qa[:, i, :] for i in range(4)] + [ka[:, i, :] for i in range(4)]
    bA = Ring([sb(f"bA{i}", [128, 3, 256]) for i in range(2)])
    bB = Ring([sb(f"bB{i}", [128, 384]) for i in range(2)])
    assert top[0] <= nc.sbuf_usable_end, top[0]
    sring, pT = Ring([x for x in sraw[0:3]]), Ring([x for x in sraw[3:6]])
    stats = Ring([sb_at(f"st{i}", [128, 8], F, base0 - 256 + 32 * i) for i in range(3)])
    sem_bA, sem_bB = [sem("bA0"), sem("bA1")], [sem("bB0"), sem("bB1")]
    tq = {}

    def qk_epi(name, i, dst_tile, gain, by_row):
        def epi(bank, t):
            def dst(raw, g, rs, need):
                if by_row:
                    o, a, b = rows(dst_tile), columns(raw), columns(rs)
                else:
                    o, a, b = dst_tile, raw, rs
                d = stt(o, a, g, b, ALU.mult, ALU.mult, need, t_vd, old)
                tq[(name, i)] = d
                return d
            return head_norm(bank[:], dst, None, gain, t, tmps, None)
        return epi

    for i in range(4):
        run(tile_t(("wi", i), H, range(8), qk_epi("qa", i, qa[:, i, :], scaled["qa"], False)))
        flush()
    for i in range(4):
        run(tile_t(("wi", 4 + i), H, range(8), qk_epi("ka", i, ka[:, i, :], v("ka2"), False)))
        flush()
    got = [M.take() for _ in range(4)]
    for u in range(4):
        unit = W.get(("va", u))
        for j in range(4):
            k_b, bank, rel = got[j]
            for i in range(2):
                k = 2 * u + i
                xh, xl = (z[:, k, 128 * j:128 * j + 128] for z in (Hhi, Hlo))
                wh, wl = unit[1][:, 512 * i:512 * i + 512], unit[2][:, 512 * i:512 * i + 512]
                mm(bank[:], xh, wh, k == 0, False, unit[3], rel, H.tok[k])
                mm(bank[:], xh, wl, False, False)
                mm(bank[:], xl, wh, False, k == 7)
        W.free(unit, pe.tick())
    t = pe.tick()
    t_va = []
    for j in range(4):
        b = got[j][1]
        E = dve if j % 2 else act
        x = [copy(E, va[j][:], b[:], t, old)]
        if j < 3:
            x.append(copy(E, vs[j][0:64, :], b[64:128, :], t, old))
        if j:
            x.append(copy(E, vs[j - 1][64:128, :], b[0:64, :], t, old))
        M.free(got[j][0], x)
        t_va.append(x)

    def kb_epi(bank, t):
        def dst(raw, g, rs, need):
            x = stt(raw, raw, g, rs, ALU.mult, ALU.mult, need)
            tq["kb"] = [copy(act, rows(kbr[64 * a:64 * a + 64, b, :]), columns(raw[64 * b:64 * b + 64, :]), x, old)
                        for a in range(2) for b in range(2)]
            return tq["kb"]
        return head_norm(bank[:], dst, None, v("kb"), t, tmps, None)

    t_g = {}

    def gate_epi(i, dst, *need):
        def epi(bank, t):
            t_g[i] = actf(dst, bank[:], ACT.Sigmoid, 1.0, None, t, old, *need)
            return [t_g[i]]
        return epi

    def side_a():
        for i in range(4):
            yield from tile_t(("wi", 12 + i), H, range(8), qk_epi("qb", i, qb[:, i, :], scaled["qb"], True))
            flush()
        yield from tile_t(("wi", 16), H, range(8), kb_epi)
        flush()
        yield from tile_t(("wi", 17), H, range(8), vb_epi)
        flush()
        for i in range(8):
            yield from tile_t(("wi", 18 + i), H, range(8), gate_epi(i, ga[:, i, :]))

    def vb_epi(bank, t):
        q, tile, last = tmps.take()
        a = copy(act, rows(tile[:]), columns(bank[:]), t, last)

        def rest():
            k, b1, rel = M.take()
            for n in range(4):
                transpose(b1[:, 128 * n:128 * n + 128], tile[:, 128 * n:128 * n + 128], c("ident"), rel, a)
            t = pe.tick()
            tq["vb"] = copy(dve, vb[:], b1[:].rearrange("p (n x) -> p n x", x=128), t, old)
            M.free(k, tq["vb"])
            tmps.free(q, t)
        pend.append(rest)
        return [a]

    A_SPAN, A_KIND = (0, 64, 192, 256), (0, 1, 1, 2)
    A_V = ((va[0], va[1]), (vs[0], vs[1]), (vs[1], vs[2]), (va[2], va[3]))

    def scores_item(q, k, n, bias, sink, need, values, o_of, vneed):
        kk, bank, rel = M.take()
        mm(bank[:, 0:n], q, k, True, True, rel, need)
        t = pe.tick()
        z, p, r, free = softmax(bank[:, 0:n], n, bias, sink, sring, stats, t)
        M.free(kk, free)
        yield
        qq, pt, plast = pT.take()
        ptv = pt.rearrange("p (b x) -> p b x", x=128)[:, 0:n // 128, :]
        a, d = transposed(p, n, ptv, r, plast)
        sring.free(z, a)
        yield
        o, orel = o_of()
        nb = n // 128
        for b in range(nb):
            mm(o, values[b], ptv[:, b, :], b == 0, b == nb - 1, d, orel, vneed)
        t = pe.tick()
        pT.free(qq, t)
        yield t, free

    def attention(pairs, n_items, make, bias_load, finish):
        for hp in range(4):
            hold = {}

            def o_of(off, j, hold=hold):
                if "b" not in hold:
                    hold["b"] = O.take()
                kd, bank, rel = hold["b"]
                return bank[off:off + 64, 128 * j:128 * j + 128], rel

            toks = []
            for h in (2 * hp, 2 * hp + 1):
                kb_, bias, bt = bias_load(h)
                fr = []

                def item(j, h=h, bias=bias, bt=bt, fr=fr):
                    g = make(h, j, bias, bt, o_of)
                    for x in g:
                        if x is not None:
                            toks.append(x[0])
                            fr.append(x[1])
                        yield

                yield from pipeline([item(j) for j in range(4)], 2)
                bias_free(kb_, fr)
            kd, bank, rel = hold["b"]
            finish(hp, kd, bank, pe.tick())

    n_b = {"A": 0, "B": 0}
    bias_now = {}

    def bias_loader(which, ring, sems, src):
        def issue(h):
            k, tile, last = ring.take()
            i = n_b[which]
            n_b[which] += 1
            t = load_on(pool, tile[:], src[h], sems[i % 2], i // 2 + 1, last, old)
            bias_now[(which, h)] = (k, tile, t)

        def get(h):
            if (which, h) not in bias_now:
                issue(h)
            if h + 1 < 8 and (which, h + 1) not in bias_now:
                issue(h + 1)
            k, tile, t = bias_now[(which, h)]
            current["ring"] = ring
            return k, tile, t
        return get

    current = {}

    def bias_free(k, fr):
        current["ring"].free(k, fr)

    def make_a(h, j, bias, bt, o_of):
        off, kt = 64 * (h % 2), h // 2
        return scores_item(qa[off:off + 64, kt, 128 * j:128 * j + 128],
                           ka[off:off + 64, kt, A_SPAN[j]:A_SPAN[j] + 256], 256,
                           bias[:, A_KIND[j], :], None, [tq[("qa", kt)], tq[("ka", kt)], bt],
                           [z[:, 64 * h:64 * h + 64] for z in A_V[j]], lambda: o_of(off, j), t_va)

    def finish_a(hp, kd, bank, t):
        U.tok[hp] = split(Uhi[:, hp, :], Ulo[:, hp, :], bank[:], t)
        O.free(kd, U.tok[hp])

    def make_b(h, n, bias, bt, o_of):
        off, kt, kv = 64 * (h % 2), h // 2, h // 4
        a, b = max(0, n - 1), min(4, n + 2)
        w = 128 * (b - a)
        o = 128 * (a - n + 1)
        return scores_item(qb[off:off + 64, kt, 128 * n:128 * n + 128],
                           kbr[off:off + 64, kv, 128 * a:128 * b], w, bias[:, o:o + w],
                           v("sink", h), [tq[("qb", kt)], tq["kb"], bt],
                           [vb[:, i, 64 * kv:64 * kv + 64] for i in range(a, b)],
                           lambda: o_of(off, n), tq["vb"])

    def finish_b(hp, kd, bank, t):
        hi, lo = columns(Uhi[:, 4 + hp, :]), columns(Ulo[:, 4 + hp, :])
        U.tok[4 + hp] = split(hi, lo, rows(bank[:]), t)
        O.free(kd, U.tok[4 + hp])

    filler = side_a()
    weave(attention(4, 4, make_a, bias_loader("A", bA, sem_bA, biasA), finish_a), filler, 3)
    run(filler)
    a_done = [pe.tick(), U.tok[0:4]]

    def side_b():
        for i in range(8):
            yield from tile_t(("wi", 26 + i), H, range(8), gate_epi(8 + i, gbt[i], a_done))

    filler = side_b()
    weave(attention(4, 4, make_b, bias_loader("B", bB, sem_bB, biasB), finish_b), filler, 2)
    run(filler)
    flush()

    hfree[0] = pe.tick()
    branch = {}

    def keep(i, which):
        def epi(bank, t):
            q, tile, last = tmps.take()
            g = ga[:, i, :] if which == 0 else gbt[i]
            d = tt(dve, tile[:], bank[:], g, ALU.mult, t, last, t_g[8 * which + i])
            branch[which] = (q, tile, d)
            return [d]
        return epi

    for m in range(4):
        hold_a, hold_b = [], []
        for i in (2 * m, 2 * m + 1):
            j0 = 4 * (i % 2)
            ua = hold_a[-1] if hold_a else None
            ub = hold_b[-1] if hold_b else None
            last_one = i % 2 == 1
            run(tile_t(("ba", m), U, range(4), keep(i, 0), j0=j0, keep=ua, hold=None if last_one else hold_a))
            run(tile_t(("bb", m), U, range(4, 8), keep(i, 1), j0=j0, keep=ub, hold=None if last_one else hold_b))
            (qa_, ta_, da_), (qb_, tb_, db_) = branch[0], branch[1]
            d = tt(pool, ta_[:], ta_[:], tb_[:], ALU.add, da_, db_)
            H.tok[i] = split(Hhi[:, i, :], Hlo[:, i, :], ta_[:], d, hfree[0])
            tmps.free(qa_, H.tok[i])
            tmps.free(qb_, d)
    for i in range(8):
        run(tile_t(("wo2", i), H, range(8), residual(i, True, tmps, True)))
    norm_x("gffn2")

    glu = {}

    def gate1(bank, t):
        q, tile, last = tmps.take()
        a = actf(tile[:], bank[:], ACT.Sigmoid, 1.0, None, t, last)
        d = tt(dve, tile[:], tile[:], bank[:], ALU.mult, a)
        glu["x"] = (q, tile, d)
        return [a, d]

    def up1(i):
        def epi(bank, t):
            q, tile, d = glu["x"]
            d = tt(dve, tile[:], tile[:], bank[:], ALU.mult, d, t)
            U.tok[i] = split(Uhi[:, i, :], Ulo[:, i, :], tile[:], d)
            tmps.free(q, U.tok[i])
            return [d]
        return epi

    s_out = sem("s_out")

    def final(i):
        r = residual(i, False, tmps)

        def epi(bank, t):
            d = r(bank, t)
            sp_out.append((i, d))
            return d
        return epi

    sp_out = []
    for chn, n in enumerate((8, 8, 6)):
        for i in range(n):
            run(tile_t(("fg", 8 * chn + i), H, range(8), gate1))
            run(tile_t(("fu", 8 * chn + i), H, range(8), up1(i)))
        for i in range(8):
            run(tile_t(("fd", chn, i), U, range(n), final(i) if chn == 2 else residual(i, False, tmps)))
            while sp_out:
                k, d = sp_out.pop(0)
                load_on(sp, out[k], X[:, k, :], s_out, k + 1, d)
    assert W.got == len(units), (W.got, len(units))

    with nc.Block() as block:
        @block.sync
        def _(e):
            sp.emit(e)
            e.wait_ge(s_out, 16 * 8)

        @block.gpsimd
        def _(e):
            pool.emit(e)

        @block.scalar
        def _(e):
            act.emit(e)

        @block.vector
        def _(e):
            dve.emit(e)

        @block.tensor
        def _(e):
            pe.emit(e)


def unit_list():
    u = [(("memk", i), 1024) for i in range(2)] + [(("memv", i), 1024) for i in range(2)]
    u += [(("rw", m), 1024) for m in (20, 21, 18, 19)]
    u += [(("rw", 6 * i + p), 1024) for p in range(NP) for i in range(3)]
    u += [(("wo", i), 1024) for i in range(8)]
    for ch in range(4):
        u += [(("f1", 8 * ch + i), 1024) for i in range(8)] + [(("f2", ch, i), 1024) for i in range(8)]
    u += [(("wi", i), 1024) for i in range(8)] + [(("va", i), 1024) for i in range(4)]
    u += [(("wi", i), 1024) for i in range(12, 18)]
    u += [(("wi", i), 1024) for i in range(18, 34)]
    for m in range(4):
        u += [(("ba", m), 1024), (("bb", m), 1024)]
    u += [(("wo2", i), 1024) for i in range(8)]
    for ch, n in enumerate((8, 8, 6)):
        for i in range(n):
            u += [(("fg", 8 * ch + i), 1024), (("fu", 8 * ch + i), 1024)]
        u += [(("fd", ch, i), 128 * n) for i in range(8)]
    return u


def constants():
    out = np.zeros((128, NCST), np.float32)

    def put(name, a):
        o, n = C_AT[name]
        out[:, o:o + n] = a

    p = np.arange(128)
    same = (p[:, None] // 64 == p[None, :] // 64).astype(np.float32)
    s, t = p[:, None] % 64, np.arange(64)[None, :]
    both = lambda a: np.concatenate([a, a], 1) * same
    put("bd1", same)
    put("bd64", same / 64.0)
    put("mean", np.full((128, 128), 1.0 / 1024))
    put("ident", np.eye(128))
    put("i2", (s == t))
    put("bd", same)
    put("mneg", both(-1.0 * (s < t)))
    put("mpos", both(1.0 * (s < t)))
    put("inclneg", -1.0 * (s <= t))
    put("inclpos", 1.0 * (s <= t))
    put("level", np.concatenate([((s // m) % 2 == 1) & (t // m == s // m - 1) for m in LEVELS], 1))
    put("scan", np.broadcast_to((np.arange(512) % 64 != 0), (128, 512)))
    put("one", 1.0)
    put("rmseps", RMS_EPS)
    put("gneps", GN_EPS)
    return out


def t5_buckets():
    rel = np.arange(384)[None, :] - 128 - np.arange(128)[:, None]
    half, exact = 16, 8
    n = np.abs(rel)
    large = exact + (np.log(np.maximum(n, 1) / exact) / np.log(128 / exact) * (half - exact)).astype(np.int32)
    return (rel > 0) * half + np.where(n < exact, n, np.minimum(large, half - 1)), n <= 128


def kernel(**inputs):
    import concourse.bacc as _bacc
    from concourse.bass_utils import run_bass_kernel_spmd as _run

    a = {k: np.asarray(x) for k, x in inputs.items()}
    f32 = np.float32

    def tiles(w, m, ks):
        x = w[ks[0] * 128:(ks[-1] + 1) * 128, 128 * m:128 * m + 128]
        return x.reshape(len(ks), 128, 128).transpose(1, 0, 2).reshape(128, -1)

    k8 = range(8)
    wi = a["w_in_2"][0]

    def unit(name):
        kind = name[0]
        if kind == "memk":
            return tiles(a["w_mem_kv"], name[1], k8)
        if kind == "memv":
            x = a["w_mem_kv"][512 * name[1]:512 * name[1] + 512, 256:512]
            return x.reshape(4, 128, 256).transpose(1, 0, 2).reshape(128, 1024)
        if kind == "rw":
            return tiles(a["rw_in"][0], name[1], k8)
        if kind == "wo":
            return tiles(a["w_out"][0], name[1], k8)
        if kind == "f1":
            return tiles(a["w_ff1"][0], name[1], k8)
        if kind == "f2":
            return tiles(a["w_ff2"][0], name[2], range(8 * name[1], 8 * name[1] + 8))
        if kind == "wi":
            return tiles(wi, name[1], k8)
        if kind == "va":
            x = wi[256 * name[1]:256 * name[1] + 256, 1024:1536]
            return x.reshape(2, 128, 512).transpose(1, 0, 2).reshape(128, 1024)
        if kind in ("ba", "bb"):
            w = a["w_branch_a_2" if kind == "ba" else "w_branch_b_2"][0]
            return np.concatenate([tiles(w, 2 * name[1] + i, range(4)) for i in range(2)], 1)
        if kind == "wo2":
            return tiles(a["w_out_2"][0], name[1], k8)
        if kind in ("fg", "fu"):
            return tiles(a["w_gate_2" if kind == "fg" else "w_up_2"][0], name[1], k8)
        return tiles(a["w_down_2"][0], name[2], range(8 * name[1], min(22, 8 * name[1] + 8)))

    units = unit_list()
    wts = np.zeros((len(units), 128, 1024), f32)
    for i, (name, n) in enumerate(units):
        wts[i, :, 0:n] = unit(name)

    def cols(x):
        return np.asarray(x, f32).reshape(-1, 128).T

    def twice(x):
        return np.concatenate([x.reshape(64), x.reshape(64)]).reshape(128, 1)

    vec = {"gmem": cols(a["mem_norm_g"]), "gmix": cols(a["norm_mix_g"]), "gffn": cols(a["norm_ffn_g"]),
           "mu": cols(a["rw_mu"]), "w0": cols(a["rw_w0"]), "a0": cols(a["rw_a0"]), "kk": cols(a["rw_k_k"]),
           "ka": cols(a["rw_k_a"]), "rk": cols(a["rw_r_k"]), "lng": cols(a["rw_lnx_g"]),
           "lnb": cols(a["rw_lnx_b"]), "gmix2": cols(a["norm_mix_2"]), "gffn2": cols(a["norm_ffn_2"]),
           "mq": twice(a["mem_q_norm_g"]), "mk": twice(a["mem_k_norm_g"]), "qa": twice(a["q_norm_a_2"]),
           "ka2": twice(a["k_norm_a_2"]), "qb": twice(a["q_norm_b_2"]), "kb": twice(a["k_norm_b_2"]),
           "sink": np.broadcast_to(a["sink_b_2"].reshape(1, 8), (128, 8))}
    vecs = np.concatenate([vec[n] for n, _ in VECS], 1)

    rpb, t5 = a["rpb_a_2"][0], a["t5_table_2"]
    col, row = np.arange(16), np.arange(8)
    bias_a = np.empty((8, 128, 3, 256), f32)
    for kind, (q0, k0) in enumerate(((0, 0), (16, 8), (48, 32))):
        qc, kc = q0 + col, k0 + np.arange(32)
        win = np.clip(qc - 8, 0, 48)
        ok = (kc[None, :] >= win[:, None]) & (kc[None, :] < win[:, None] + 16)
        dc = np.clip(kc[None, :] - qc[:, None], -15, 15) + 15
        dr = row[None, :] - row[:, None] + 7
        g = rpb[dr[None, :, None, :], dc[:, None, :, None]]
        g = np.where(ok[:, None, :, None, None], g, f32(-1e30))
        bias_a[:, :, kind, :] = g.reshape(128, 256, 8).transpose(2, 0, 1)
    bucket, ok = t5_buckets()
    bias_b = np.where(ok[:, :, None], t5[bucket], f32(-1e30)).transpose(2, 0, 1)

    arrays = {
        "xT": a["x"][0].T.reshape(8, 128, 512), "memT": a["mem"][0].T.reshape(8, 128, 256),
        "wts": wts, "vecs": vecs, "cst": constants(),
        "w2a2": np.concatenate([a["rw_w2"][0], a["rw_a2"][0]], 0), "g2": a["rw_g2"][0],
        "biasA": bias_a, "biasB": bias_b,
    }
    arrays = {f"in_{k}": np.ascontiguousarray(x, dtype=x.dtype) for k, x in arrays.items()}
    nc = _bacc.Bacc("TRN2", target_bir_lowering=False, num_devices=1)
    args = [nc.dram_tensor(k, x.shape, mybir.dt.from_np(x.dtype), kind="ExternalInput").ap()
            for k, x in arrays.items()]
    o = nc.dram_tensor("out", (8, 128, 512), F, kind="ExternalOutput").ap()
    block_program(nc, *args, o, units)
    r = _run(nc, [arrays], core_ids=[0])
    y = np.asarray(r.results[0]["out"])
    return y.reshape(1024, 512).T.reshape(1, 512, 1024).copy()
```

```python
import numpy as np

import concourse.bass as bass
from concourse import mybir

F = mybir.dt.float32
R = mybir.dt.float32r
ALU = mybir.AluOpType
ACT = mybir.ActivationFunctionType
AXX = mybir.AxisListType.X

T = 512
NP = 6
NC = 8
LEVELS = (1, 2, 4, 8, 16, 32)
DECAY = 0.6065306597126334
RMS_EPS = 1e-6
GN_EPS = 64e-5

CONSTS = [("bd64", 128), ("mean", 128), ("ident", 128), ("i2", 64),
          ("mneg", 128), ("mpos", 128), ("inclneg", 128), ("inclnegs", 64), ("inclpos", 128),
          ("level", 128 * 5), ("level1t", 128), ("scan", 512), ("one", 1), ("rmseps", 1), ("gneps", 1), ("zero", 1)]
VECS = [("gmem", 8), ("gmix", 8), ("gffn", 8), ("mu", 20), ("w0", 6), ("a0", 6), ("kk", 6),
        ("ka", 6), ("rk", 6), ("lng", 6), ("lnb", 6), ("gmix2", 8), ("gffn2", 8), ("mq", 1),
        ("mk", 1), ("qa", 1), ("ka2", 1), ("qb", 1), ("kb", 1), ("sink", 8)]


def offsets(table):
    at, out = 0, {}
    for name, n in table:
        out[name] = (at, n)
        at += n
    return out, at


C_AT, NCST = offsets(CONSTS)
V_AT, NVEC = offsets(VECS)
NDER = 20 + 6 + 3


class Engine:

    def __init__(self, sem, in_turn=False):
        self.sem, self.ops, self.n, self.seen, self.in_turn = sem, [], 0, {}, in_turn

    def waits(self, need):
        found = {}
        for t in need:
            if t is None:
                continue
            if isinstance(t, list):
                for w in self.waits(t):
                    found[w[0].name] = max(found.get(w[0].name, w), w, key=lambda x: x[1])
            else:
                found[t[0].name] = max(found.get(t[0].name, t), t, key=lambda x: x[1])
        return list(found.values())

    def put(self, fn, need, sem=None, by=1):
        if self.in_turn and self.n:
            need = [*need, (self.sem, self.n)]
        w = [x for x in self.waits(need) if self.seen.get(x[0].name, 0) < x[1]]
        for s, v in w:
            self.seen[s.name] = v
        self.ops.append([w, fn, sem, by])

    def tick(self):
        last = self.ops[-1]
        if last[2] is None:
            last[2] = self.sem
            self.n += 1
        return (self.sem, self.n)

    def step(self, fn, *need):
        self.put(fn, need)
        return self.tick()

    def emit(self, eng):
        for w, fn, sem, by in self.ops:
            for s, v in w:
                eng.wait_ge(s, v)
            ins = fn(eng)
            if sem is not None:
                ins.then_inc(sem, by)


class Ring:

    def __init__(self, items):
        self.items, self.last, self.i = items, [[] for _ in items], 0

    def take(self):
        k = self.i
        self.i = (k + 1) % len(self.items)
        last = self.last[k]
        assert last is not None
        self.last[k] = None
        return k, self.items[k], last

    def free(self, k, *toks):
        self.last[k] = list(toks)


class Act:

    def __init__(self, hi, lo, n):
        self.hi, self.lo, self.tok = hi, lo, [None] * n


def run(gen):
    for _ in gen:
        pass


def block_program(nc, xT, memT, wts, vecs, cst, w2a2, g2, biasA, biasB, out, units):
    sem_of = {}

    def sem(name):
        sem_of[name] = nc.alloc_semaphore(name)
        return sem_of[name]

    pe, dve, act, pool, sp = (Engine(sem("s_" + n), n == "pool")
                              for n in ("pe", "dve", "act", "pool", "sp"))

    base0 = 16512
    top = [base0]

    def sb(name, shape, dt=F):
        n = 4
        for d in shape[1:]:
            n *= d
        n = (n + 31) // 32 * 32
        t = nc.alloc_sbuf_tensor_at(name, list(shape), dt, offset=top[0])
        top[0] += n
        return t

    def sb_at(name, shape, dt, offset):
        return nc.alloc_sbuf_tensor_at(name, list(shape), dt, offset=offset)

    banks = [nc.alloc_psum_tensor(f"bank{i}", [128, 512], F) for i in range(8)]
    D, M, O, Y = Ring(banks[0:2]), Ring(banks[2:6]), Ring(banks[6:7]), Ring(banks[7:8])

    C = sb("C", [128, NCST])
    V = sb("V", [128, NVEC])
    VD = sb("VD", [128, NDER])
    Hhi, Hlo = sb("Hhi", [128, 8, T], R), sb("Hlo", [128, 8, T], R)
    Uhi, Ulo = sb("Uhi", [128, 8, T], R), sb("Ulo", [128, 8, T], R)
    NW = 3
    Wraw = Ring([sb(f"Wraw{i}", [128, 1024]) for i in range(NW)])
    Wsp = Ring([(sb(f"Whi{i}", [128, 1024], R), sb(f"Wlo{i}", [128, 1024], R)) for i in range(NW)])
    SQ = None

    def c(name, a=0, n=None):
        o, w = C_AT[name]
        return C[:, o + a:o + a + (w if n is None else n)]

    def v(name, j=0):
        o, w = V_AT[name]
        return V[:, o + j:o + j + 1]

    def mm(o, lhsT, rhs, start, stop, *need):
        pe.put(lambda e: e.matmul(o, lhsT, rhs, start=start, stop=stop, skip_group_check=True), need)

    def transpose(o, i, ident, *need):
        pe.put(lambda e: e.transpose(o, i, ident), need)

    def tt(E, o, a, b, op, *need):
        return E.step(lambda e: e.tensor_tensor(o, a, b, op), *need)

    def stt(o, a, s, b, op0, op1, *need):
        return dve.step(lambda e: e.scalar_tensor_tensor(o, a, s, b, op0, op1), *need)

    def ts(E, o, a, s1, s2, op0, op1, *need):
        if s2 is None:
            return E.step(lambda e: e.tensor_scalar(o, a, s1, None, op0), *need)
        return E.step(lambda e: e.tensor_scalar(o, a, s1, s2, op0, op1), *need)

    def actf(o, a, f, scale, bias, *need):
        if bias is None:
            return act.step(lambda e: e.activation(o, a, f, scale=scale), *need)
        return act.step(lambda e: e.activation(o, a, f, scale=scale, bias=bias), *need)

    def copy(E, o, a, *need):
        if E is act:
            return act.step(lambda e: e.copy(o, a), *need)
        return E.step(lambda e: e.tensor_copy(o, a), *need)

    def recip(o, a, *need):
        return dve.step(lambda e: e.reciprocal(o, a), *need)

    n_load = [0]

    def load(o, i, *need):
        s = sem(f"ld{n_load[0]}")
        n_load[0] += 1
        sp.put(lambda e: e.dma_start(o, i), need, s, 16)
        return (s, 16)

    def split(hi, lo, src, *need):
        a = copy(act, hi, src, *need)
        b = tt(dve, lo, src, hi.bitcast(F), ALU.subtract, a, *need)
        return [a, b]

    t_c = load(C[:], cst)
    t_v = load(V[:], vecs)

    omu, oka = VD[:, 0:20], VD[:, 20:26]
    mu_all = V[:, V_AT["mu"][0]:V_AT["mu"][0] + 20]
    ka_all = V[:, V_AT["ka"][0]:V_AT["ka"][0] + 6]
    t_vd = [ts(dve, omu, mu_all, -1.0, 1.0, ALU.mult, ALU.add, t_v),
            ts(dve, oka, ka_all, -1.0, 1.0, ALU.mult, ALU.add, t_v)]
    scaled = {}
    for i, name in enumerate(("mq", "qa", "qb")):
        scaled[name] = VD[:, 26 + i:27 + i]
        t_vd.append(ts(dve, scaled[name], v(name), 0.125, None, ALU.mult, None, t_v))

    class Stream:
        def __init__(self):
            self.loads, self.splits, self.got = [], [], 0
            self.sems = [sem(f"w{i}") for i in range(NW)]

        def load_ahead(self, n):
            while len(self.loads) < n:
                u = len(self.loads)
                k, raw, last = Wraw.take()
                width = units[u][1]
                s = self.sems[k]
                sp.put(lambda e, raw=raw, u=u, width=width: e.dma_start(raw[:, 0:width], wts[u, :, 0:width]),
                       [last], s, 16)
                self.loads.append((k, raw, (s, 16 * (u // NW + 1))))

        def advance(self, n_split):
            while len(self.splits) < min(n_split, len(units)):
                self.load_ahead(min(len(self.splits) + NW, len(units)))
                u = len(self.splits)
                k, raw, tok = self.loads[u]
                width = units[u][1]
                kk, (hi, lo), last = Wsp.take()
                toks = split(hi[:, 0:width], lo[:, 0:width], raw[:, 0:width], tok, last)
                Wraw.free(k, toks)
                self.splits.append((kk, hi, lo, toks))

        def get(self, name):
            u = self.got
            assert units[u][0] == name, (units[u][0], name)
            self.got += 1
            self.advance(u + NW - 1)
            return self.splits[u]

        def free(self, unit, tok):
            Wsp.free(unit[0], tok)

    W = Stream()

    def mm3(o, whi, wlo, xhi, xlo, first, last, *need):
        mm(o, whi, xhi, first, False, *need)
        mm(o, wlo, xhi, False, False)
        mm(o, whi, xlo, False, last)

    def tile_t(name, a, ks, epi, n=T, j0=0, keep=None, hold=None, bank=None):
        unit = keep if keep is not None else W.get(name)
        if bank is None:
            b, bank, rel = D.take()
        else:
            b, rel = None, None
        for i, k in enumerate(ks):
            j = (j0 + i) * 128
            mm3(bank[:, 0:n], unit[1][:, j:j + 128], unit[2][:, j:j + 128], a.hi[:, k, 0:n],
                a.lo[:, k, 0:n], i == 0, i == len(ks) - 1, unit[3], rel, a.tok[k])
            if i == 2:
                flush()
            yield
        t = pe.tick()
        if hold is None:
            W.free(unit, t)
        else:
            hold.append(unit)
        done = epi(bank, t)
        if b is not None:
            D.free(b, done)

    def gained(i, x, tok, gname, a, n, *need, by_column=False):
        hi, lo = a.hi[:, i, 0:n], a.lo[:, i, 0:n]
        if by_column:
            hi, lo, x = columns(hi), columns(lo), rows(x)
        h = actf(hi, x, ACT.Copy, v(gname, i), None, tok, t_v, *need)
        a.tok[i] = [h, stt(lo, x, v(gname, i), hi.bitcast(F), ALU.mult, ALU.subtract, h, tok, t_v, *need)]
        return a.tok[i]

    def inverse_rms(sq, tsq, rs, *need, n=T, by_column=False):
        k, bank, rel = M.take()
        mm(bank[:, 0:n], c("mean"), sq, True, True, rel, tsq, t_c)
        t = pe.tick()
        o, b = rs[:, 0:n], bank[:, 0:n]
        if by_column:
            o, b = columns(o), rows(b)
        a = actf(o, b, ACT.Sqrt, 1.0, c("rmseps"), t, *need)
        M.free(k, a)
        return recip(rs[:, 0:n], rs[:, 0:n], a)

    def by_partition(rs, t_rs, dst, n, *need):
        k, bank, rel = M.take()
        for j in range(n):
            transpose(bank[:, 128 * j:128 * j + 128], rs[:, 128 * j:128 * j + 128], c("ident"), rel,
                      t_rs, t_c)
        t = pe.tick()
        d = copy(dve, dst.unsqueeze(2), bank[:, 0:128 * n].rearrange("p (j x) -> p j x", x=128)[:, :, 0:1], t,
                 *need)
        M.free(k, d)
        return d

    def rows(ap):
        return ap.rearrange("p (r c) -> p r c", r=8)

    def columns(ap):
        return ap.rearrange("p (c r) -> p r c", r=8)

    def squares_step(i, x, tok, acc, tmp, last, n=T):
        if i == 0:
            return actf(acc[:, 0:n], x, ACT.Square, 1.0, None, tok, last)
        q, tile, free = tmp.take()
        a = actf(tile[:, 0:n], x, ACT.Square, 1.0, None, tok, free)
        last = tt(pool, acc[:, 0:n], acc[:, 0:n], tile[:, 0:n], ALU.add, a, last)
        tmp.free(q, last)
        return last

    def load_on(E, o, i, s, count, *need):
        E.put(lambda e: e.dma_start(o, i), need, s, 16)
        return (s, 16 * count)

    pend = []

    def flush():
        while pend:
            pend.pop(0)()

    def fence():
        return [e.tick() for e in (pe, dve, act, pool) if e.ops]

    def softmax(bank, n, bias, sink, ring, stats, need):
        q, s, last = ring.take()
        z, st, slast = stats.take()
        s = s[:, 0:n]
        if bias is None:
            src, d = bank, need
        else:
            src = s
            d = tt(dve, s, bank, bias, ALU.add, need, last)
        m = dve.step(lambda e: e.tensor_reduce(st[:, 0:1], src, AXX, ALU.max), d, slast)
        if sink is None:
            m = ts(dve, st[:, 1:2], st[:, 0:1], -1.0, None, ALU.mult, None, m)
        else:
            m = ts(dve, st[:, 1:2], st[:, 0:1], sink, -1.0, ALU.max, ALU.mult, m)
        x = act.step(lambda e: e.activation(s, src, ACT.Exp, scale=1.0, bias=st[:, 1:2],
                                            accum_out=st[:, 2:3]), m, last)
        r = x
        if sink is not None:
            y = actf(st[:, 4:5], sink, ACT.Exp, 1.0, st[:, 1:2], m)
            r = tt(dve, st[:, 2:3], st[:, 2:3], st[:, 4:5], ALU.add, x, y)
        r = recip(st[:, 3:4], st[:, 2:3], r)
        r = ts(dve, s, s, st[:, 3:4], None, ALU.mult, None, r)
        stats.free(z, r)
        return q, s, r, [d, x] if bias is None else [d]

    def pipeline(items, depth):
        items, active = list(items), []
        while items or active:
            if items and len(active) < depth:
                active.append(items.pop(0))
            for g in list(active):
                try:
                    next(g)
                except StopIteration:
                    active.remove(g)
            yield

    def weave(main, filler, per):
        due = 0.0
        for _ in main:
            due += per
            while due >= 1:
                due -= 1
                next(filler, None)

    def head_norm(src, rs, dst, need, tmp):
        q, raw, last = tmp.take()
        q2, sq, last2 = tmp.take()
        n = src.shape[1]
        a = tt(dve, raw[:, 0:n], src, rs, ALU.mult, need, last)
        b = actf(sq[:, 0:n], raw[:, 0:n], ACT.Square, 1.0, None, a, last2)

        def rest():
            k, bank, rel = M.take()
            mm(bank[:, 0:n], c("bd64"), sq[:, 0:n], True, True, rel, b, t_c)
            t = pe.tick()
            x = actf(sq[:, 0:n], bank[:, 0:n], ACT.Sqrt, 1.0, c("rmseps"), t)
            M.free(k, x)
            y = recip(sq[:, 0:n], sq[:, 0:n], x)
            z = dst(raw[:, 0:n], sq[:, 0:n], [y, a])
            tmp.free(q, z)
            tmp.free(q2, z)
        pend.append(rest)
        return [a]

    arena = top[0]
    slab = [sb(f"slab{i}", [128, T]) for i in range(3)]
    WA, GD = sb("WA", [128, T]), sb("GD", [128, T])
    w2s, g2s = sb("w2s", [128, 768]), sb("g2s", [128, 768])
    RS = sb("RS", [128, T])
    ftmp = Ring([sb(f"ftmp{i}", [128, T]) for i in range(2)])
    sg, Pi, ta, kf, kn = (sb(n, [128, T]) for n in ("sg", "Pi", "ta", "kf", "kn"))
    Pp = sb("Pp", [128, NC, 65])
    bonus2 = [sb(f"bonus{i}", [128, T]) for i in range(2)]
    PC2 = [sb(f"PC{i}", [128, NC]) for i in range(2)]
    low = top[0]

    memX = sb("memX", [128, 8, 256])
    memH = Act(sb("memHhi", [128, 8, 256], R), sb("memHlo", [128, 8, 256], R), 8)
    x0 = Ring([sb(f"x0{i}", [128, T]) for i in range(4)])
    acc, accm, RSm = sb("acc", [128, T]), sb("accm", [128, 256]), sb("RSm", [128, 256])
    rsn = sb("rsn", [128, 2])
    km, vm = sb("km", [128, 2, 256]), sb("vm", [128, 2, 256])
    qm = sb("qm", [128, 2, T])
    sring = Ring([sb(f"ms{i}", [128, 256]) for i in range(4)])
    mstats = Ring([sb(f"mst{i}", [128, 8]) for i in range(4)])
    pTm = Ring([sb(f"pTm{i}", [128, 2, T]) for i in range(2)])
    assert top[0] <= nc.sbuf_usable_end, top[0]

    H, U = Act(Hhi, Hlo, 8), Act(Uhi, Ulo, 8)

    W.load_ahead(2)
    last = None
    sem_x = [sem(f"x{i}") for i in range(4)]
    for i in range(8):
        q, tile, free = x0.take()
        t_x = load_on(sp, tile[:], xT[i], sem_x[i % 4], i // 4 + 1, free)
        g = gained(i, tile[:], t_x, "gmix", H, T)
        last = squares_step(i, tile[:], t_x, acc, ftmp, last)
        x0.free(q, g, last)
        if i == 3:
            W.advance(1)
    W.advance(2)
    t_rs = inverse_rms(acc[:], last, RS)
    t_w2, t_g2 = load(w2s[:], w2a2), load(g2s[:], g2)
    t_m = [load(memX[:, 4 * i:4 * i + 4, :], memT[4 * i:4 * i + 4].rearrange("k p n -> p k n"))
           for i in range(2)]

    t_lora = {}

    def shift(dst, bank, j, t, *need):
        q, z, last = ftmp.take()
        m = tt(dve, z[:], bank[:], RS[:], ALU.mult, t, last, t_rs)
        a = actf(dst[:], z[:], ACT.Copy, omu[:, j:j + 1], None, m, t_vd, *need)
        d = stt(dst[:, 1:T], z[:, 0:T - 1], v("mu", j), dst[:, 1:T], ALU.mult, ALU.add, a)
        ftmp.free(q, d)
        return m, d

    def wa_epi(bank, t):
        m, d = shift(WA, bank, 18, t)
        t_lora["wa"] = [d, actf(WA[0:64, :], WA[0:64, :], ACT.Tanh, 1.0, None, d)]
        return [m]

    def gd_epi(bank, t):
        m, d = shift(GD, bank, 19, t)
        t_lora["gd"] = actf(GD[:], GD[:], ACT.Sigmoid, 1.0, None, d)
        return [m]

    run(tile_t(("rw", 18), H, range(8), wa_epi))
    run(tile_t(("rw", 19), H, range(8), gd_epi))

    last = None
    for i in range(8):
        gained(i, memX[:, i, :], t_m[i // 4], "gmem", memH, 256)
        last = squares_step(i, memX[:, i, :], t_m[i // 4], accm, ftmp, last, 256)
    t_qm, t_km = [None, None], [None, None]

    def qm_epi(i):
        def epi(bank, t):
            def dst(raw, rs, need):
                t_qm[i] = stt(qm[:, i, :], raw, scaled["mq"], rs, ALU.mult, ALU.mult, need, t_vd)
                return t_qm[i]
            return head_norm(bank[:], RS[:], dst, [t, t_rs], x0)
        return epi

    for i in range(2):
        run(tile_t(("rw", 20 + i), H, range(8), qm_epi(i)))
    t_rsm = inverse_rms(accm[:], last, RSm, n=256)
    t_rsn = by_partition(RSm, t_rsm, rsn[:], 2)

    def km_epi(i):
        def epi(bank, t):
            def dst(raw, rs, need):
                a = tt(dve, km[:, i, :], raw, rs, ALU.mult, need)
                t_km[i] = ts(dve, km[:, i, :], km[:, i, :], v("mk"), None, ALU.mult, None, a)
                return t_km[i]
            return head_norm(bank[:, 0:256], RSm[:], dst, [t, t_rsm], x0)
        return epi

    for i in range(2):
        run(tile_t(("memk", i), memH, range(8), km_epi(i), n=256))
    got = [M.take(), M.take()]
    for u in range(2):
        unit = W.get(("memv", u))
        for m in range(2):
            k_, bank, rel = got[m]
            for i in range(4):
                k = 4 * u + i
                xh, xl = memH.hi[:, k, 128 * m:128 * m + 128], memH.lo[:, k, 128 * m:128 * m + 128]
                wh, wl = unit[1][:, 256 * i:256 * i + 256], unit[2][:, 256 * i:256 * i + 256]
                o = bank[:, 0:256]
                mm(o, xh, wh, k == 0, False, unit[3], rel, memH.tok[k])
                mm(o, xh, wl, False, False)
                mm(o, xl, wh, False, k == 7)
        W.free(unit, pe.tick())
    t = pe.tick()
    t_vm = []
    for m in range(2):
        t_vm.append(actf(vm[:, m, :], got[m][1][:, 0:256], ACT.Copy, rsn[:, m:m + 1], None, t, t_rsn))
        M.free(got[m][0], t_vm[-1])
    flush()

    def transposed(p, n, dst, need, pt_ring_tok):
        k, bank, rel = M.take()
        for b in range(n // 128):
            transpose(bank[:, 128 * b:128 * b + 128], p[:, 128 * b:128 * b + 128], c("ident"),
                      rel, need, t_c)
        t = pe.tick()
        d = copy(dve, dst, bank[:, 0:n].rearrange("p (b x) -> p b x", x=128), t, pt_ring_tok)
        M.free(k, d)
        return t, d

    def mem_head(h, state):
        off, kt = 64 * (h % 2), h // 2
        q, pT, plast = pTm.take()
        pt = []

        def item(j):
            k, bank, rel = M.take()
            mm(bank[:, 0:256], qm[off:off + 64, kt, 128 * j:128 * j + 128], km[off:off + 64, kt, :],
               True, True, rel, t_qm[kt], t_km[kt])
            t = pe.tick()
            z, p, r, free = softmax(bank[:, 0:256], 256, None, None, sring, mstats, t)
            M.free(k, free)
            yield
            yield
            a, d = transposed(p, 256, pT[:, :, 128 * j:128 * j + 128], r, plast)
            sring.free(z, a)
            pt.append(d)

        yield from pipeline([item(j) for j in range(4)], 3)
        if h % 2 == 0:
            state["bank"] = O.take()
        kd, bank, rel = state["bank"]
        for b in range(2):
            mm(bank[off:off + 64, :], vm[:, b, 64 * h:64 * h + 64], pT[:, b, :], b == 0, b == 1,
               rel, t_vm, pt)
        t = pe.tick()
        pTm.free(q, t)
        if h % 2:
            U.tok[6 + kt] = split(Uhi[:, 6 + kt, :], Ulo[:, 6 + kt, :], bank[:], t)
            O.free(kd, U.tok[6 + kt])
        yield

    def mem_attention():
        state = {}
        for h in range(4):
            yield from mem_head(h, state)

    t_slab, slab_free = [None] * 3, [[], [], []]

    def slab_epi(i, j):
        def epi(bank, t):
            m, t_slab[i] = shift(slab[i], bank, j, t, slab_free[i])
            return [m]
        return epi

    def projections(p):
        for i in range(3):
            yield from tile_t(("rw", 6 * i + p), H, range(8), slab_epi(i, 6 * i + p))

    def half(bd, h, c0=0, c1=NC):
        return bd[64 * h:64 * h + 64, c0:c1, 64 * h:64 * h + 64]

    def stk(t, h=None, c0=0, c1=NC):
        w = t.rearrange("p (c x) -> p c x", x=64) if len(t.shape) == 2 else t
        return w[:, c0:c1, :] if h is None else w[64 * h:64 * h + 64, c0:c1, :]

    def bcast(ap, n):
        return ap.unsqueeze(1).broadcast_to([ap.shape[0], n, ap.shape[1]])

    r_, k_, v_ = slab
    t_one = pool.step(lambda e: e.memset(Pp[:, :, 0:1], 1.0))
    front_free, fr, bonus_free = [[]], {}, [None]

    def front(p):
        free = front_free[0]
        bonus, PC = bonus2[p % 2], PC2[p % 2]
        k1, b1, rel = M.take()
        mm(b1[:], w2s[0:64, 128 * p:128 * p + 128], WA[0:64, :], True, True, rel, t_w2, t_lora["wa"])
        t = pe.tick()
        a = actf(sg[:], b1[:], ACT.Sigmoid, 1.0, v("w0", p), t, free)
        M.free(k1, a)
        yield
        k1, b1, rel = M.take()
        mm(b1[:], w2s[64:128, 128 * p:128 * p + 128], WA[64:128, :], True, True, rel)
        t = pe.tick()
        a2 = actf(ta[:], b1[:], ACT.Sigmoid, 1.0, v("a0", p), t, free)
        M.free(k1, a2)
        d = dve.step(lambda e: e.tensor_tensor_scan(sg[:], c("scan"), sg[:], 0.0, ALU.mult, ALU.add), a)
        q, tm, last = ftmp.take()
        sq = actf(tm[:], k_[:], ACT.Square, v("kk", p), None, t_slab[1], last)
        yield
        k1, b1, rel = M.take()
        mm(b1[:], c("bd64"), tm[:], True, True, rel, sq)
        t = pe.tick()
        e1 = actf(Pp[:, :, 1:65], stk(sg), ACT.Exp, -DECAY, None, d, t_one, free)
        e2 = actf(Pi[:], sg[:], ACT.Exp, DECAY, None, d, free)
        fr["pc"] = copy(pool, PC[:].unsqueeze(2), Pp[:, :, 64:65], e1, free)
        x = actf(tm[:], b1[:], ACT.Sqrt, 64.0, None, t)
        M.free(k1, x)
        f = ts(dve, kf[:], ta[:], v("ka", p), oka[:, p:p + 1], ALU.mult, ALU.add, a2, t_vd, free)
        f = tt(pool, kf[:], kf[:], k_[:], ALU.mult, f, t_slab[1])
        yield
        x = ts(dve, tm[:], tm[:], 1e-12, None, ALU.max, None, x)
        x = recip(tm[:], tm[:], x)
        kkt = stt(kn[:], k_[:], v("kk", p), tm[:], ALU.mult, ALU.mult, x, free)
        bt = tt(pool, ta[:], ta[:], kn[:], ALU.mult, kkt, f)
        rk = stt(tm[:], r_[:], v("rk", p), kf[:], ALU.mult, ALU.mult, kkt, f, t_slab[0])
        yield
        k1, b1, rel = M.take()
        mm(b1[:], c("bd64"), tm[:], True, True, rel, rk)
        t = pe.tick()
        bo = stt(bonus[:], b1[:], 64.0, v_[:], ALU.mult, ALU.mult, t, t_slab[2], free, bonus_free[0])
        M.free(k1, bo)
        ftmp.free(q, t)
        fr.update(e1=e1, e2=e2, f=f, kkt=kkt, bt=bt, bo=bo, rk=rk, t_slab=list(t_slab), bonus=bonus,
                  PC=PC)
        yield

    def ahead(p):
        yield from projections(p)
        yield from front(p)

    filler = ahead(0)
    weave(mem_attention(), filler, 0.5)
    run(filler)
    flush()
    old = fence()

    top[0] = low

    def tile4(name):
        return sb(name, [128, NC, 128])

    AR, BDb, BDk, BDa, BDv = (tile4(n) for n in ("AR", "BDb", "BDk", "BDa", "BDv"))
    MT, AK, RB, RK, BR, GA = (tile4(n) for n in ("MT", "AK", "RB", "RK", "BR", "GA"))
    Bn, Kn, Vn = (tile4(n) for n in ("Bn", "Kn", "Vn"))
    y2, z2 = sb("y2", [128, T])[:], sb("z2", [128, T])[:]
    assert top[0] <= nc.sbuf_usable_end, top[0]
    Xb, T1, Yb, U0, W1, Phi, Rt, PD = BDb, BDk, BDa, BDv, AK, Kn, MT, Bn

    for b in (BDb, BDk, BDa, BDv, MT, AK, RB, RK, Bn, Kn, Vn):
        t_z = pool.step(lambda e, b=b: e.memset(b[:], 0.0), old)

    war = [[]]
    CC = ((0, 4), (4, 8))

    def chunks(bank):
        return bank[:].rearrange("p (c x) -> p c x", x=128)

    def masked(name, n=4):
        return bcast(c(name), n)

    def products(w, rhs, need, hf, w2=None, rhs2=None, need2=None, chs=None):
        k1, b1, rel = M.take()
        for i in range(4):
            ch = 4 * hf + i
            if chs is not None and ch not in chs:
                continue
            o = b1[:, 128 * i:128 * i + 128]
            mm(o, w[:, ch, :], rhs[:, ch, :], True, w2 is None, rel, need)
            if w2 is not None:
                mm(o, w2[:, ch, :], rhs2[:, ch, :], False, True, need2)
        return k1, b1, pe.tick()

    def transposes(w, need, hf):
        k1, b1, rel = M.take()
        for i in range(4):
            transpose(b1[:, 128 * i:128 * i + 128], w[:, 4 * hf + i, :], c("ident"), rel, need, t_c)
        return k1, b1, pe.tick()

    def pair(p):
        free = war[0]
        f_ = dict(fr)
        ts_ = f_["t_slab"]
        ar = [tt(dve, AR[:, :, 0:64], stk(kn), Pp[:, :, 0:64], ALU.mult, f_["e1"], f_["kkt"], free, old)]
        bb = [tt(dve, half(BDb, h), stk(ta, h), stk(Pi, h), ALU.mult, f_["e2"], f_["bt"], t_z, free)
              for h in range(2)]
        ar.append(tt(dve, AR[:, :, 64:128], stk(r_), Pp[:, :, 1:65], ALU.mult, ts_[0]))
        bk = [tt(pool, half(BDk, h), stk(kf, h), stk(Pi, h), ALU.mult, f_["e2"], f_["f"], t_z, free)
              for h in range(2)]
        ba = [copy(act, half(BDa, h), AR[64 * h:64 * h + 64, :, 0:64], ar[0], t_z, free)
              for h in range(2)]
        bv = [copy(act, half(BDv, h), stk(v_, h), ts_[2], t_z, free) for h in range(2)]
        slab_free[0] = [ar[1], f_["rk"]]
        slab_free[1] = [f_["kkt"], f_["f"]]
        slab_free[2] = [bv, f_["bo"]]
        front_free[0] = [ar, bb, bk]
        yield

        def score(w, need, full, mask, full2, mask2, keep2, hf):
            k1, b1, t = products(w, AR, [ar, need], hf)
            src = chunks(b1)
            c0, c1 = CC[hf]
            done = []
            for o, x, m in ((full, 0, mask), (full2, 64, mask2)):
                s4 = src[:, :, x:x + 64].unsqueeze(2).broadcast_to([128, 4, 2, 64])
                m4 = c(m).rearrange("p (h x) -> p h x", h=2).unsqueeze(1).broadcast_to([128, 4, 2, 64])
                o4 = o[:, c0:c1, :].rearrange("p c (h x) -> p c h x", h=2)
                done.append(tt(dve, o4, s4, m4, ALU.mult, t))
            if keep2 is not None:
                done.append(tt(dve, keep2[:, c0:c1, 64:128], src[:, :, 64:128], bcast(c(mask2 + "s"), 4),
                               ALU.mult, t))
            M.free(k1, done)
            return done

        sb1, sk1 = [None] * 2, [None] * 2
        for hf in range(2):
            sb1[hf] = score(BDb, bb, MT, "mneg", RB, "inclneg", BR, hf)
            yield
        nbs, na, nv, nk = {}, {}, {}, {}
        nb = {}
        for hf in range(2):
            c0, c1 = CC[hf]
            k1, b1, t = transposes(BDb, bb, hf)
            nb[hf] = actf(Bn[:, c0:c1, :], chunks(b1), ACT.Copy, -1.0, None, t, free)
            M.free(k1, nb[hf])
            nbs[hf] = [copy(pool, BR[64 * h:64 * h + 64, c0:c1, 0:64], half(Bn, h, c0, c1), nb[hf], free)
                       for h in range(2)]
            k1, b1, t = transposes(BDa, ba, hf)
            na[hf] = [copy(act, GA[64 * h:64 * h + 64, c0:c1, 64:128],
                           chunks(b1)[64 * h:64 * h + 64, :, 64 * h:64 * h + 64], t, free)
                      for h in range(2)]
            M.free(k1, na[hf])
            yield
        y, x = [None] * 2, [None] * 2
        for hf in range(2):
            c0, c1 = CC[hf]
            d = tt(pool, Yb[:, c0:c1, :], MT[:, c0:c1, :], masked("level1t"), ALU.mult, sb1[hf][0], t)
            y[hf] = tt(pool, Yb[:, c0:c1, :], Yb[:, c0:c1, :], masked("ident"), ALU.add, d)
        for hf in range(2):
            sk1[hf] = score(BDk, bk, AK, "mpos", RK, "inclpos", None, hf)
            yield
        for hf in range(2):
            c0, c1 = CC[hf]
            k1, b1, t = transposes(BDv, bv, hf)
            nv[hf] = copy(act, Vn[:, c0:c1, :], chunks(b1), t, free)
            M.free(k1, nv[hf])
            k1, b1, t = transposes(BDk, bk, hf)
            nk[hf] = copy(act, Kn[:, c0:c1, :], chunks(b1), t, free)
            M.free(k1, nk[hf])
            yield
        for hf in range(2):
            c0, c1 = CC[hf]
            k1, b1, t = transposes(Yb, y[hf], hf)
            x[hf] = copy(act, Xb[:, c0:c1, :], chunks(b1), t)
            M.free(k1, x[hf])
        gv = [None] * 2
        for l in range(1, len(LEVELS)):
            t1 = [None] * 2
            for hf in range(2):
                c0, c1 = CC[hf]
                k1, b1, t = products(MT, Xb, [x[hf], sb1[hf]], hf)
                t1[hf] = tt(dve, T1[:, c0:c1, :], chunks(b1), bcast(c("level", 128 * (l - 1), 128), 4),
                            ALU.mult, t)
                M.free(k1, t1[hf])
                yield
            if l == 1:
                for hf in range(2):
                    c0, c1 = CC[hf]
                    k1, b1, t = products(AK, Vn, [nv[hf], sk1[hf]], hf)
                    gv[hf] = [copy(act, GA[64 * h:64 * h + 64, c0:c1, 0:64],
                                   chunks(b1)[64 * h:64 * h + 64, :, 64 * h:64 * h + 64], t, free)
                              for h in range(2)]
                    M.free(k1, gv[hf])
                yield
            if l < len(LEVELS) - 1:
                for hf in range(2):
                    c0, c1 = CC[hf]
                    k1, b1, t = products(Yb, T1, [y[hf], t1[hf]], hf)
                    x[hf] = tt(dve, Xb[:, c0:c1, :], chunks(b1), Xb[:, c0:c1, :], ALU.add, t)
                    M.free(k1, x[hf])
                    yield
                for hf in range(2):
                    c0, c1 = CC[hf]
                    k1, b1, t = transposes(Xb, x[hf], hf)
                    y[hf] = copy(act, Yb[:, c0:c1, :], chunks(b1), t)
                    M.free(k1, y[hf])
                    yield
            else:
                for hf in range(2):
                    c0, c1 = CC[hf]
                    k1, b1, t = products(T1, Yb, [y[hf], t1[hf]], hf)
                    y[hf] = tt(dve, Yb[:, c0:c1, :], chunks(b1), Yb[:, c0:c1, :], ALU.add, t)
                    M.free(k1, y[hf])
                    yield
        uw = [None] * 2
        for hf in range(2):
            k1, b1, t = products(Yb, GA, [y[hf], gv[hf], na[hf]], hf)
            E = act if hf else dve
            uw[hf] = [copy(E, half(w, h, *CC[hf]), chunks(b1)[64 * h:64 * h + 64, :, o:o + 64], t)
                      for w, o in ((U0, 0), (W1, 64)) for h in range(2)]
            M.free(k1, uw[hf])
            yield
        st, PC = [None] * NC, f_["PC"]
        for hf in range(2):
            c0, c1 = CC[hf]
            n = min(c1, NC - 1) - c0
            k1, b1, t = products(Bn, U0, [nb[hf], uw[hf]], hf, Kn, Vn, nk[hf], range(NC - 1))
            pc = PC[:, c0:c0 + n].unsqueeze(2).broadcast_to([128, n, 128])
            d = tt(dve, PD[:, c0:c0 + n, :], chunks(b1)[:, 0:n, :], pc, ALU.mult, t, fr_pc, free)
            M.free(k1, d)
            for i in range(c0, c0 + n):
                st[i] = d
            yield
        ph = [None] * 2
        for hf in range(2):
            c0, c1 = CC[hf]
            k1, b1, t = products(W1, BR, [uw[hf], nbs[hf]], hf)
            src = chunks(b1)
            ph[hf] = [tt(dve, half(Phi, h, c0, c1), src[64 * h:64 * h + 64, :, 0:64],
                         bcast(c("i2"), 4)[64 * h:64 * h + 64], ALU.add, t) for h in range(2)]
            ph[hf] += [tt(dve, half(Rt, h, c0, c1), src[64 * h:64 * h + 64, :, 64:128],
                          AR[64 * h:64 * h + 64, c0:c1, 64:128], ALU.add, t) for h in range(2)]
            M.free(k1, ph[hf])
            yield
        ko, ob, orel = O.take()
        ke = None
        yy = []
        for ch in range(NC):
            if 1 <= ch < NC - 1:
                o = ob[:, 128 * (ch % 4):128 * (ch % 4) + 128]
                mm(o, Phi[:, ch, :], PD[:, ch - 1, :], True, True, orel, st[ch - 1], ph[ch // 4])
                t = pe.tick()
                st[ch] = stt(PD[:, ch, :], o, PC[:, ch:ch + 1], PD[:, ch, :], ALU.mult, ALU.add, t)
            if ch % 4 == 0:
                ke, yb, rel = Y.take()
            o = yb[:, 128 * (ch % 4):128 * (ch % 4) + 128]
            mm(o, U0[:, ch, :], RB[:, ch, :], True, False, rel)
            mm(o, Vn[:, ch, :], RK[:, ch, :], False, ch == 0)
            if ch:
                mm(o, PD[:, ch - 1, :], Rt[:, ch, :], False, True, st[ch - 1], ph[ch // 4])
            if ch % 4 == 3:
                t = pe.tick()
                x_ = [copy(act, stk(y2, h, ch - 3, ch + 1),
                           chunks(yb)[64 * h:64 * h + 64, :, 64 * h:64 * h + 64], t, y2_free[0])
                      for h in range(2)]
                Y.free(ke, x_)
                yy.append(x_)
            yield
        O.free(ko, st[NC - 2])
        war[0] = [t]
        f_["yy"] = yy
        done_[p] = f_

    done_ = {}
    y2_free = [old]

    def tail(p):
        f_ = done_[p]
        k1, b1, rel = M.take()
        mm(b1[:], c("bd64"), y2, True, True, rel, f_["yy"])
        t = pe.tick()
        d = tt(dve, y2, y2, b1[:], ALU.subtract, t)
        M.free(k1, d)
        s = actf(z2, y2, ACT.Square, 1.0, None, d, y2_free[0])
        yield
        yield
        k1, b1, rel = M.take()
        mm(b1[:], c("bd64"), z2, True, True, rel, s)
        t = pe.tick()
        x = actf(z2, b1[:], ACT.Sqrt, 1.0, c("gneps"), t)
        M.free(k1, x)
        yield
        x = recip(z2, z2, x)
        x = tt(dve, y2, y2, z2, ALU.mult, x)
        x = ts(dve, y2, y2, v("lng", p), v("lnb", p), ALU.mult, ALU.add, x)
        x = tt(pool, y2, y2, f_["bonus"][:], ALU.add, x)
        bonus_free[0] = x
        yield
        k1, b1, rel = M.take()
        mm(b1[:], g2s[:, 128 * p:128 * p + 128], GD[:], True, True, rel, t_g2, t_lora["gd"])
        t = pe.tick()
        x = tt(dve, y2, y2, b1[:], ALU.mult, x, t)
        M.free(k1, x)
        U.tok[p] = split(Uhi[:, p, :], Ulo[:, p, :], y2, x)
        y2_free[0] = [x, U.tok[p]]
        yield

    def turns(*gens):
        gens = list(gens)
        while gens:
            for g in list(gens):
                try:
                    next(g)
                    yield
                except StopIteration:
                    gens.remove(g)

    for p in range(NP):
        fr_pc = fr["pc"]
        gens = []
        if p:
            gens.append(tail(p - 1))
        if p + 1 < NP:
            gens.append(ahead(p + 1))
        filler = turns(*gens)
        weave(pair(p), filler, 0.7)
        run(filler)
    run(tail(NP - 1))
    old = fence()

    top[0] = arena
    X = sb("X", [128, 8, T])
    RSb, accb, rsnb = sb("RSb", [128, T]), sb("accb", [128, T]), sb("rsnb", [128, 4])
    tmps = Ring([sb(f"tmpb{i}", [128, T]) for i in range(4)])
    xtok = [load(X[:, 4 * i:4 * i + 4, :], xT[4 * i:4 * i + 4].rearrange("k p n -> p k n"), old)
            for i in range(2)]
    xtok = [xtok[i // 4] for i in range(8)]
    tmps.last = [[old] for _ in tmps.last]
    sqlast = [None]

    def residual(i, gname=None, to=None, by_column=False):
        def epi(bank, t):
            x, y = X[:, i, :], bank[:]
            if by_column:
                x, y = rows(x), columns(y)
            d = tt(dve, x, x, y, ALU.add, t, xtok[i])
            xtok[i] = d
            if gname is not None:
                gained(i, X[:, i, :], d, gname, to, T, by_column=gname == "gmix2")
                sqlast[0] = squares_step(i, X[:, i, :], d, accb, tmps, sqlast[0] if i else sq_free[0])
            return [d]
        return epi

    sq_free = [old]

    def norm_x(by_column=False):
        t = inverse_rms(accb[:], sqlast[0], RSb, rs_free[0], by_column=by_column)
        sq_free[0] = pe.tick()
        return t

    rs_free = [old]
    for i in range(8):
        run(tile_t(("wo", i), U, range(8), residual(i, "gffn", H)))
    t_rs = norm_x()

    def ff1_epi(i):
        def epi(bank, t):
            q, tile, last = tmps.take()
            a = stt(tile[:], bank[:], 0.0, RSb[:], ALU.max, ALU.mult, t, t_rs, last)
            d = tt(pool, tile[:], tile[:], tile[:], ALU.mult, a)
            U.tok[i] = split(Uhi[:, i, :], Ulo[:, i, :], tile[:], d)
            tmps.free(q, U.tok[i])
            rs_free[0] = a
            return [a]
        return epi

    for chn in range(4):
        for i in range(8):
            run(tile_t(("f1", 8 * chn + i), H, range(8), ff1_epi(i)))
        for i in range(8):
            run(tile_t(("f2", chn, i), U, range(8), residual(i, "gmix2" if chn == 3 else None, H)))
    t_rs = norm_x(True)
    t_rsn = by_partition(RSb, t_rs, rsnb[:], 4, old)

    qa, ka = sb("qa", [128, 4, T]), sb("ka", [128, 4, T])
    va = [sb(f"va{i}", [128, T]) for i in range(4)]
    vs = [sb(f"vs{i}", [128, T]) for i in range(3)]
    qb, kbr, vb = sb("qb", [128, 4, T]), sb("kbr", [128, 2, T]), sb("vb", [128, 4, 128])
    ga = sb("ga", [128, 4, T])
    gates = [ga[:, i, :] for i in range(4)] + [z[:, i, :] for z in (qa, ka) for i in range(4)]
    gates += [z[:] for z in va]
    bA = Ring([sb(f"bA{i}", [128, 3, 256])[:] for i in range(2)])
    bB = Ring([z[:, 0:2, :].rearrange("p a x -> p (a x)")[:, 0:384] for z in bA.items])
    assert top[0] <= nc.sbuf_usable_end, top[0]
    sring, pT = Ring([sb(f"sr{i}", [128, 384]) for i in range(4)]), Ring([sb(f"pT{i}", [128, 384]) for i in range(3)])
    stats = Ring([sb(f"st{i}", [128, 8]) for i in range(4)])
    for r in (sring, pT, stats):
        r.last = [[old] for _ in r.last]
    sem_bA, sem_bB = [sem("bA0"), sem("bA1")], [sem("bB0"), sem("bB1")]
    tq = {}

    def qk_epi(name, i, dst_tile, gain, by_row):
        def epi(bank, t):
            def dst(raw, rs, need):
                if by_row:
                    o, a, b = rows(dst_tile), columns(raw), columns(rs)
                else:
                    o, a, b = dst_tile, raw, rs
                d = stt(o, a, gain, b, ALU.mult, ALU.mult, need, t_vd, old)
                tq[(name, i)] = d
                return d
            return head_norm(bank[:], RSb[:], dst, [t, t_rs], tmps)
        return epi

    for i in range(4):
        run(tile_t(("wi", i), H, range(8), qk_epi("qa", i, qa[:, i, :], scaled["qa"], False)))
    for i in range(4):
        run(tile_t(("wi", 4 + i), H, range(8), qk_epi("ka", i, ka[:, i, :], v("ka2"), False)))
    got = [M.take() for _ in range(4)]
    for u in range(4):
        unit = W.get(("va", u))
        for j in range(4):
            k_b, bank, rel = got[j]
            for i in range(2):
                k = 2 * u + i
                xh, xl = (z[:, k, 128 * j:128 * j + 128] for z in (Hhi, Hlo))
                wh, wl = unit[1][:, 512 * i:512 * i + 512], unit[2][:, 512 * i:512 * i + 512]
                mm(bank[:], xh, wh, k == 0, False, unit[3], rel, H.tok[k])
                mm(bank[:], xh, wl, False, False)
                mm(bank[:], xl, wh, False, k == 7)
        W.free(unit, pe.tick())
    t = pe.tick()
    t_va = []
    for j in range(4):
        b = got[j][1]
        outs = [(va[j][:], 0, 128)]
        if j < 3:
            outs.append((vs[j][0:64, :], 64, 128))
        if j:
            outs.append((vs[j - 1][64:128, :], 0, 64))
        if j % 2:
            x = [ts(dve, o, b[lo:hi, :], rsnb[lo:hi, j:j + 1], None, ALU.mult, None, t, t_rsn, old)
                 for o, lo, hi in outs]
        else:
            x = [actf(o, b[lo:hi, :], ACT.Copy, rsnb[lo:hi, j:j + 1], None, t, t_rsn, old)
                 for o, lo, hi in outs]
        M.free(got[j][0], x)
        t_va.append(x)

    def kb_epi(bank, t):
        def dst(raw, rs, need):
            x = stt(raw, raw, v("kb"), rs, ALU.mult, ALU.mult, need)
            tq["kb"] = [copy(act, rows(kbr[64 * a:64 * a + 64, b, :]), columns(raw[64 * b:64 * b + 64, :]), x, old)
                        for a in range(2) for b in range(2)]
            return tq["kb"]
        return head_norm(bank[:], RSb[:], dst, [t, t_rs], tmps)

    t_g = {}

    def gate_epi(i, dst, *need):
        def epi(bank, t):
            d = tt(dve, dst, bank[:], RSb[:], ALU.mult, t, t_rs, old, *need)
            t_g[i] = actf(dst, dst, ACT.Sigmoid, 1.0, None, d)
            rs_free[0] = d
            return [d]
        return epi

    def side_a():
        for i in range(4):
            yield from tile_t(("wi", 12 + i), H, range(8), qk_epi("qb", i, qb[:, i, :], scaled["qb"], True))
        yield from tile_t(("wi", 16), H, range(8), kb_epi)
        yield from tile_t(("wi", 17), H, range(8), vb_epi)
        for i in range(4):
            yield from tile_t(("wi", 18 + i), H, range(8), gate_epi(i, gates[i]))

    def vb_epi(bank, t):
        q, tile, last = tmps.take()
        a = tt(dve, rows(tile[:]), columns(bank[:]), columns(RSb[:]), ALU.mult, t, last, t_rs)

        def rest():
            k, b1, rel = M.take()
            for n in range(4):
                transpose(b1[:, 128 * n:128 * n + 128], tile[:, 128 * n:128 * n + 128], c("ident"), rel, a)
            t = pe.tick()
            tq["vb"] = copy(dve, vb[:], b1[:].rearrange("p (n x) -> p n x", x=128), t, old)
            M.free(k, tq["vb"])
            tmps.free(q, t)
        pend.append(rest)
        return [a]

    A_SPAN, A_KIND = (0, 64, 192, 256), (0, 1, 1, 2)
    A_V = ((va[0], va[1]), (vs[0], vs[1]), (vs[1], vs[2]), (va[2], va[3]))

    def scores_item(q, k, n, bias, sink, need, values, o_of, vneed):
        kk, bank, rel = M.take()
        mm(bank[:, 0:n], q, k, True, True, rel, need)
        t = pe.tick()
        z, p, r, free = softmax(bank[:, 0:n], n, bias, sink, sring, stats, t)
        M.free(kk, free)
        yield
        qq, pt, plast = pT.take()
        ptv = pt.rearrange("p (b x) -> p b x", x=128)[:, 0:n // 128, :]
        a, d = transposed(p, n, ptv, r, plast)
        sring.free(z, a)
        yield
        o, orel = o_of()
        nb = n // 128
        for b in range(nb):
            mm(o, values[b], ptv[:, b, :], b == 0, b == nb - 1, d, orel, vneed)
        t = pe.tick()
        pT.free(qq, t)
        yield t, free

    def attention(pairs, n_items, make, bias_load, finish):
        for hp in range(4):
            hold = {}

            def o_of(off, j, hold=hold):
                if "b" not in hold:
                    hold["b"] = O.take()
                kd, bank, rel = hold["b"]
                return bank[off:off + 64, 128 * j:128 * j + 128], rel

            toks = []
            for h in (2 * hp, 2 * hp + 1):
                kb_, bias, bt = bias_load(h)
                fr = []

                def item(j, h=h, bias=bias, bt=bt, fr=fr):
                    g = make(h, j, bias, bt, o_of)
                    for x in g:
                        if x is not None:
                            toks.append(x[0])
                            fr.append(x[1])
                        yield

                yield from pipeline([item(j) for j in range(4)], 3)
                bias_free(kb_, fr)
            kd, bank, rel = hold["b"]
            finish(hp, kd, bank, pe.tick())

    n_b = {"A": 0, "B": 0}
    bias_now = {}

    def bias_loader(which, ring, sems, src):
        def issue(h):
            k, tile, last = ring.take()
            i = n_b[which]
            n_b[which] += 1
            t = load_on(pool, tile, src[h], sems[i % 2], i // 2 + 1, last, old)
            bias_now[(which, h)] = (k, tile, t)

        def get(h):
            if (which, h) not in bias_now:
                issue(h)
            if h + 1 < 8 and (which, h + 1) not in bias_now:
                issue(h + 1)
            k, tile, t = bias_now[(which, h)]
            current["ring"] = ring
            return k, tile, t
        return get

    current = {}

    def bias_free(k, fr):
        current["ring"].free(k, fr)

    def make_a(h, j, bias, bt, o_of):
        off, kt = 64 * (h % 2), h // 2
        return scores_item(qa[off:off + 64, kt, 128 * j:128 * j + 128],
                           ka[off:off + 64, kt, A_SPAN[j]:A_SPAN[j] + 256], 256,
                           bias[:, A_KIND[j], :], None, [tq[("qa", kt)], tq[("ka", kt)], bt],
                           [z[:, 64 * h:64 * h + 64] for z in A_V[j]], lambda: o_of(off, j), t_va)

    def finish_a(hp, kd, bank, t):
        U.tok[hp] = split(Uhi[:, hp, :], Ulo[:, hp, :], bank[:], t)
        O.free(kd, U.tok[hp])

    def make_b(h, n, bias, bt, o_of):
        off, kt, kv = 64 * (h % 2), h // 2, h // 4
        a, b = max(0, n - 1), min(4, n + 2)
        w = 128 * (b - a)
        o = 128 * (a - n + 1)
        return scores_item(qb[off:off + 64, kt, 128 * n:128 * n + 128],
                           kbr[off:off + 64, kv, 128 * a:128 * b], w, bias[:, o:o + w],
                           v("sink", h), [tq[("qb", kt)], tq["kb"], bt],
                           [vb[:, i, 64 * kv:64 * kv + 64] for i in range(a, b)],
                           lambda: o_of(off, n), tq["vb"])

    def finish_b(hp, kd, bank, t):
        hi, lo = columns(Uhi[:, 4 + hp, :]), columns(Ulo[:, 4 + hp, :])
        U.tok[4 + hp] = split(hi, lo, rows(bank[:]), t)
        O.free(kd, U.tok[4 + hp])

    filler = side_a()
    weave(attention(4, 4, make_a, bias_loader("A", bA, sem_bA, biasA), finish_a), filler, 2)
    run(filler)
    a_done = [pe.tick(), U.tok[0:4]]

    def side_b():
        for i in range(4, 16):
            yield from tile_t(("wi", 18 + i), H, range(8), gate_epi(i, gates[i], a_done))

    bB.last = [a_done, a_done]
    filler = side_b()
    weave(attention(4, 4, make_b, bias_loader("B", bB, sem_bB, biasB), finish_b), filler, 1.5)
    run(filler)
    flush()

    hfree = pe.tick()
    branch = {}

    def keep(i, which):
        def epi(bank, t):
            q, tile, last = tmps.take()
            g = gates[8 * which + i]
            d = tt(dve, tile[:], bank[:], g, ALU.mult, t, last, t_g[8 * which + i])
            branch[which] = (q, tile, d)
            return [d]
        return epi

    for m in range(4):
        hold_a, hold_b = [], []
        for i in (2 * m, 2 * m + 1):
            j0 = 4 * (i % 2)
            ua = hold_a[-1] if hold_a else None
            ub = hold_b[-1] if hold_b else None
            last_one = i % 2 == 1
            run(tile_t(("ba", m), U, range(4), keep(i, 0), j0=j0, keep=ua, hold=None if last_one else hold_a))
            run(tile_t(("bb", m), U, range(4, 8), keep(i, 1), j0=j0, keep=ub, hold=None if last_one else hold_b))
            (qa_, ta_, da_), (qb_, tb_, db_) = branch[0], branch[1]
            d = tt(pool, ta_[:], ta_[:], tb_[:], ALU.add, da_, db_)
            H.tok[i] = split(Hhi[:, i, :], Hlo[:, i, :], ta_[:], d, hfree)
            tmps.free(qa_, H.tok[i])
            tmps.free(qb_, d)
    for i in range(8):
        run(tile_t(("wo2", i), H, range(8), residual(i, "gffn2", U, True)))
    t_rs = norm_x()

    glu = {}

    def gate1(bank, t):
        q, tile, last = tmps.take()
        z, sig, last2 = tmps.take()
        d = tt(dve, tile[:], bank[:], RSb[:], ALU.mult, t, last, t_rs)
        a = actf(sig[:], tile[:], ACT.Sigmoid, 1.0, None, d, last2)
        m = tt(pool, tile[:], tile[:], sig[:], ALU.mult, a)
        glu["x"] = (q, tile, m, z, sig)
        return [d]

    def up1(i):
        def epi(bank, t):
            q, tile, m, z, up = glu["x"]
            d = tt(dve, up[:], bank[:], RSb[:], ALU.mult, m, t)
            m = tt(pool, up[:], up[:], tile[:], ALU.mult, d)
            H.tok[i] = split(Hhi[:, i, :], Hlo[:, i, :], up[:], m)
            tmps.free(q, m)
            tmps.free(z, H.tok[i])
            return [d]
        return epi

    s_out = sem("s_out")

    def final(i):
        r = residual(i)

        def epi(bank, t):
            d = r(bank, t)
            sp_out.append((i, d))
            return d
        return epi

    sp_out = []
    for chn, n in enumerate((8, 8, 6)):
        for i in range(n):
            run(tile_t(("fg", 8 * chn + i), U, range(8), gate1))
            run(tile_t(("fu", 8 * chn + i), U, range(8), up1(i)))
        for i in range(8):
            run(tile_t(("fd", chn, i), H, range(n), final(i) if chn == 2 else residual(i)))
            while sp_out:
                k, d = sp_out.pop(0)
                load_on(sp, out[k], X[:, k, :], s_out, k + 1, d)
    assert W.got == len(units), (W.got, len(units))

    with nc.Block() as block:
        @block.sync
        def _(e):
            sp.emit(e)
            e.wait_ge(s_out, 16 * 8)

        @block.gpsimd
        def _(e):
            pool.emit(e)

        @block.scalar
        def _(e):
            act.emit(e)

        @block.vector
        def _(e):
            dve.emit(e)

        @block.tensor
        def _(e):
            pe.emit(e)


def unit_list():
    u = [(("rw", m), 1024) for m in (18, 19, 20, 21)]
    u += [(("memk", i), 1024) for i in range(2)] + [(("memv", i), 1024) for i in range(2)]
    u += [(("rw", 6 * i + p), 1024) for p in range(NP) for i in range(3)]
    u += [(("wo", i), 1024) for i in range(8)]
    for ch in range(4):
        u += [(("f1", 8 * ch + i), 1024) for i in range(8)] + [(("f2", ch, i), 1024) for i in range(8)]
    u += [(("wi", i), 1024) for i in range(8)] + [(("va", i), 1024) for i in range(4)]
    u += [(("wi", i), 1024) for i in range(12, 18)]
    u += [(("wi", i), 1024) for i in range(18, 34)]
    for m in range(4):
        u += [(("ba", m), 1024), (("bb", m), 1024)]
    u += [(("wo2", i), 1024) for i in range(8)]
    for ch, n in enumerate((8, 8, 6)):
        for i in range(n):
            u += [(("fg", 8 * ch + i), 1024), (("fu", 8 * ch + i), 1024)]
        u += [(("fd", ch, i), 128 * n) for i in range(8)]
    return u


def constants():
    out = np.zeros((128, NCST), np.float32)

    def put(name, a):
        o, n = C_AT[name]
        out[:, o:o + n] = a

    p = np.arange(128)
    same = (p[:, None] // 64 == p[None, :] // 64).astype(np.float32)
    s, t = p[:, None] % 64, np.arange(64)[None, :]
    both = lambda a: np.concatenate([a, a], 1) * same
    put("bd64", same / 64.0)
    put("mean", np.full((128, 128), 1.0 / 1024))
    put("ident", np.eye(128))
    put("i2", (s == t))
    put("mneg", both(-1.0 * (s < t)))
    put("mpos", both(1.0 * (s < t)))
    put("inclneg", both(-1.0 * (s <= t)))
    put("inclnegs", -1.0 * (s <= t))
    put("inclpos", both(1.0 * (s <= t)))
    level = lambda m, a, b: ((a // m) % 2 == 1) & (b // m == a // m - 1)
    put("level", np.concatenate([both(level(m, s, t)) for m in LEVELS[1:]], 1))
    put("level1t", both(level(1, t, s)))
    put("scan", np.broadcast_to((np.arange(512) % 64 != 0), (128, 512)))
    put("one", 1.0)
    put("rmseps", RMS_EPS)
    put("gneps", GN_EPS)
    return out


def t5_buckets():
    rel = np.arange(384)[None, :] - 128 - np.arange(128)[:, None]
    half, exact = 16, 8
    n = np.abs(rel)
    large = exact + (np.log(np.maximum(n, 1) / exact) / np.log(128 / exact) * (half - exact)).astype(np.int32)
    return (rel > 0) * half + np.where(n < exact, n, np.minimum(large, half - 1)), n <= 128


def kernel(**inputs):
    import concourse.bacc as _bacc
    from concourse.bass_utils import run_bass_kernel_spmd as _run

    a = {k: np.asarray(x) for k, x in inputs.items()}
    f32 = np.float32

    def tiles(w, m, ks):
        x = w[ks[0] * 128:(ks[-1] + 1) * 128, 128 * m:128 * m + 128]
        return x.reshape(len(ks), 128, 128).transpose(1, 0, 2).reshape(128, -1)

    k8 = range(8)
    wi = a["w_in_2"][0]

    def unit(name):
        kind = name[0]
        if kind == "memk":
            return tiles(a["w_mem_kv"], name[1], k8)
        if kind == "memv":
            x = a["w_mem_kv"][512 * name[1]:512 * name[1] + 512, 256:512]
            return x.reshape(4, 128, 256).transpose(1, 0, 2).reshape(128, 1024)
        if kind == "rw":
            return tiles(a["rw_in"][0], name[1], k8)
        if kind == "wo":
            return tiles(a["w_out"][0], name[1], k8)
        if kind == "f1":
            return tiles(a["w_ff1"][0], name[1], k8)
        if kind == "f2":
            return tiles(a["w_ff2"][0], name[2], range(8 * name[1], 8 * name[1] + 8))
        if kind == "wi":
            return tiles(wi, name[1], k8)
        if kind == "va":
            x = wi[256 * name[1]:256 * name[1] + 256, 1024:1536]
            return x.reshape(2, 128, 512).transpose(1, 0, 2).reshape(128, 1024)
        if kind in ("ba", "bb"):
            w = a["w_branch_a_2" if kind == "ba" else "w_branch_b_2"][0]
            return np.concatenate([tiles(w, 2 * name[1] + i, range(4)) for i in range(2)], 1)
        if kind == "wo2":
            return tiles(a["w_out_2"][0], name[1], k8)
        if kind in ("fg", "fu"):
            return tiles(a["w_gate_2" if kind == "fg" else "w_up_2"][0], name[1], k8)
        return tiles(a["w_down_2"][0], name[2], range(8 * name[1], min(22, 8 * name[1] + 8)))

    units = unit_list()
    wts = np.zeros((len(units), 128, 1024), f32)
    for i, (name, n) in enumerate(units):
        wts[i, :, 0:n] = unit(name)

    def cols(x):
        return np.asarray(x, f32).reshape(-1, 128).T

    def twice(x):
        return np.concatenate([x.reshape(64), x.reshape(64)]).reshape(128, 1)

    vec = {"gmem": cols(a["mem_norm_g"]), "gmix": cols(a["norm_mix_g"]), "gffn": cols(a["norm_ffn_g"]),
           "mu": cols(a["rw_mu"]), "w0": cols(a["rw_w0"]), "a0": cols(a["rw_a0"]), "kk": cols(a["rw_k_k"]),
           "ka": cols(a["rw_k_a"]), "rk": cols(a["rw_r_k"]), "lng": cols(a["rw_lnx_g"]),
           "lnb": cols(a["rw_lnx_b"]), "gmix2": cols(a["norm_mix_2"]), "gffn2": cols(a["norm_ffn_2"]),
           "mq": twice(a["mem_q_norm_g"]), "mk": twice(a["mem_k_norm_g"]), "qa": twice(a["q_norm_a_2"]),
           "ka2": twice(a["k_norm_a_2"]), "qb": twice(a["q_norm_b_2"]), "kb": twice(a["k_norm_b_2"]),
           "sink": np.broadcast_to(a["sink_b_2"].reshape(1, 8), (128, 8))}
    vecs = np.concatenate([vec[n] for n, _ in VECS], 1)

    rpb, t5 = a["rpb_a_2"][0], a["t5_table_2"]
    col, row = np.arange(16), np.arange(8)
    bias_a = np.empty((8, 128, 3, 256), f32)
    for kind, (q0, k0) in enumerate(((0, 0), (16, 8), (48, 32))):
        qc, kc = q0 + col, k0 + np.arange(32)
        win = np.clip(qc - 8, 0, 48)
        ok = (kc[None, :] >= win[:, None]) & (kc[None, :] < win[:, None] + 16)
        dc = np.clip(kc[None, :] - qc[:, None], -15, 15) + 15
        dr = row[None, :] - row[:, None] + 7
        g = rpb[dr[None, :, None, :], dc[:, None, :, None]]
        g = np.where(ok[:, None, :, None, None], g, f32(-1e30))
        bias_a[:, :, kind, :] = g.reshape(128, 256, 8).transpose(2, 0, 1)
    bucket, ok = t5_buckets()
    bias_b = np.where(ok[:, :, None], t5[bucket], f32(-1e30)).transpose(2, 0, 1)

    arrays = {
        "xT": a["x"][0].T.reshape(8, 128, 512), "memT": a["mem"][0].T.reshape(8, 128, 256),
        "wts": wts, "vecs": vecs, "cst": constants(),
        "w2a2": np.concatenate([a["rw_w2"][0], a["rw_a2"][0]], 0), "g2": a["rw_g2"][0],
        "biasA": bias_a, "biasB": bias_b,
    }
    arrays = {f"in_{k}": np.ascontiguousarray(x, dtype=x.dtype) for k, x in arrays.items()}
    nc = _bacc.Bacc("TRN2", target_bir_lowering=False, num_devices=1)
    args = [nc.dram_tensor(k, x.shape, mybir.dt.from_np(x.dtype), kind="ExternalInput").ap()
            for k, x in arrays.items()]
    o = nc.dram_tensor("out", (8, 128, 512), F, kind="ExternalOutput").ap()
    block_program(nc, *args, o, units)
    r = _run(nc, [arrays], core_ids=[0])
    y = np.asarray(r.results[0]["out"])
    return y.reshape(1024, 512).T.reshape(1, 512, 1024).copy()
```

```python
import itertools

import numpy as np

import concourse.bass as bass
from concourse import mybir

F = mybir.dt.float32
R = mybir.dt.float32r
ALU = mybir.AluOpType
ACT = mybir.ActivationFunctionType
AXX = mybir.AxisListType.X

T = 512
NP = 6
NC = 8

FILL_FRONT, FILL_PAIR_FIRST, FILL_PAIR, FILL_PAIR_LAST, FILL_TAIL = 0.2, 1, 1.2, 0.5, 2
FILL_A, FILL_B = 1, 3.5
STATE_WEIGHT = 1.5
MEM_STEPS = 20
SOFT_ROUNDS = 2
LEVELS = (1, 2, 4, 8, 16, 32)
DECAY = 0.6065306597126334
RMS_EPS = 1e-6
GN_EPS = 64e-5

CONSTS = [("bd64", 128), ("mean", 128), ("ident", 128),
          ("mneg", 128), ("mpos", 128), ("inclneg", 128), ("inclnegs", 64), ("inclpos", 128),
          ("level", 128 * 5), ("level1t", 128), ("scan", 512), ("rmseps", 1), ("gneps", 1)]
VECS = [("gmem", 8), ("gmix", 8), ("gffn", 8), ("mu", 20), ("w0", 6), ("a0", 6), ("kk", 6),
        ("ka", 6), ("rk", 6), ("lng", 6), ("lnb", 6), ("gmix2", 8), ("gffn2", 8), ("mq", 1),
        ("mk", 1), ("qa", 1), ("ka2", 1), ("qb", 1), ("kb", 1), ("sink", 8)]


def offsets(table):
    at, out = 0, {}
    for name, n in table:
        out[name] = (at, n)
        at += n
    return out, at


C_AT, NCST = offsets(CONSTS)
V_AT, NVEC = offsets(VECS)
NDER = 20 + 6 + 3 + 12


class Engine:

    def __init__(self, sem, in_turn=False):
        self.sem, self.ops, self.n, self.seen, self.in_turn = sem, [], 0, {}, in_turn

    def waits(self, need):
        found = {}
        for t in need:
            if t is None:
                continue
            if isinstance(t, list):
                for w in self.waits(t):
                    found[w[0].name] = max(found.get(w[0].name, w), w, key=lambda x: x[1])
            else:
                found[t[0].name] = max(found.get(t[0].name, t), t, key=lambda x: x[1])
        return list(found.values())

    def put(self, fn, need, sem=None, by=1):
        if self.in_turn and self.n:
            need = [*need, (self.sem, self.n)]
        w = [x for x in self.waits(need) if self.seen.get(x[0].name, 0) < x[1]]
        for s, v in w:
            self.seen[s.name] = v
        self.ops.append([w, fn, sem, by])

    def tick(self):
        last = self.ops[-1]
        if last[2] is None:
            last[2] = self.sem
            self.n += 1
        return (self.sem, self.n)

    def step(self, fn, *need):
        self.put(fn, need)
        return self.tick()

    def emit(self, eng):
        for w, fn, sem, by in self.ops:
            for s, v in w:
                eng.wait_ge(s, v)
            ins = fn(eng)
            if sem is not None:
                ins.then_inc(sem, by)


class Ring:

    def __init__(self, items):
        self.items, self.last, self.i = items, [[] for _ in items], 0

    def take(self):
        k = self.i
        while self.last[k] is None:
            k = (k + 1) % len(self.items)
            assert k != self.i
        self.i = (k + 1) % len(self.items)
        last = self.last[k]
        self.last[k] = None
        return k, self.items[k], last

    def free(self, k, *toks):
        self.last[k] = list(toks)


class Act:

    def __init__(self, hi, lo, n):
        self.hi, self.lo, self.tok = hi, lo, [None] * n


def run(gen):
    for _ in gen:
        pass


def block_program(nc, xT, memT, wts, vecs, cst, w2a2, g2, biasA, biasB, out, units):
    sem_of = {}

    def sem(name):
        sem_of[name] = nc.alloc_semaphore(name)
        return sem_of[name]

    pe, dve, act, pool, sp = (Engine(sem("s_" + n), n == "pool")
                              for n in ("pe", "dve", "act", "pool", "sp"))

    base0 = 16512
    top = [base0]

    def sb(name, shape, dt=F):
        n = 4
        for d in shape[1:]:
            n *= d
        n = (n + 31) // 32 * 32
        t = nc.alloc_sbuf_tensor_at(name, list(shape), dt, offset=top[0])
        top[0] += n
        return t

    def sb_at(name, shape, dt, offset):
        return nc.alloc_sbuf_tensor_at(name, list(shape), dt, offset=offset)

    banks = [nc.alloc_psum_tensor(f"bank{i}", [128, 512], F) for i in range(8)]
    D, M, O, Y = Ring(banks[0:2]), Ring(banks[2:6]), Ring(banks[6:7]), Ring(banks[7:8])

    C = sb("C", [128, NCST])
    V = sb("V", [128, NVEC])
    VD = sb("VD", [128, NDER])
    H_AT = top[0]
    Hhi, Hlo = sb("Hhi", [128, 8, T], R), sb("Hlo", [128, 8, T], R)
    U_AT = (top[0], top[0] + 16384)
    Uhi, Ulo = sb("Uhi", [128, 8, T], R), sb("Ulo", [128, 8, T], R)
    NW = 3
    Wraw = Ring([sb(f"Wraw{i}", [128, 1024]) for i in range(NW)])
    Wsp = Ring([(sb(f"Whi{i}", [128, 1024], R), sb(f"Wlo{i}", [128, 1024], R)) for i in range(NW)])

    def c(name, a=0, n=None):
        o, w = C_AT[name]
        return C[:, o + a:o + a + (w if n is None else n)]

    def v(name, j=0):
        o, w = V_AT[name]
        return V[:, o + j:o + j + 1]

    def mm(o, lhsT, rhs, start, stop, *need):
        pe.put(lambda e: e.matmul(o, lhsT, rhs, start=start, stop=stop, skip_group_check=True), need)

    def transpose(o, i, ident, *need):
        pe.put(lambda e: e.transpose(o, i, ident), need)

    def tt(E, o, a, b, op, *need):
        return E.step(lambda e: e.tensor_tensor(o, a, b, op), *need)

    def stt(o, a, s, b, op0, op1, *need):
        return dve.step(lambda e: e.scalar_tensor_tensor(o, a, s, b, op0, op1), *need)

    def ts(E, o, a, s1, s2, op0, op1, *need):
        if s2 is None:
            return E.step(lambda e: e.tensor_scalar(o, a, s1, None, op0), *need)
        return E.step(lambda e: e.tensor_scalar(o, a, s1, s2, op0, op1), *need)

    def actf(o, a, f, scale, bias, *need):
        if bias is None:
            return act.step(lambda e: e.activation(o, a, f, scale=scale), *need)
        return act.step(lambda e: e.activation(o, a, f, scale=scale, bias=bias), *need)

    def copy(E, o, a, *need):
        if E is act:
            return act.step(lambda e: e.copy(o, a), *need)
        return E.step(lambda e: e.tensor_copy(o, a), *need)

    def recip(o, a, *need):
        return dve.step(lambda e: e.reciprocal(o, a), *need)

    def sigmoid(o, a, half_bias, *need):
        return actf(o, a, ACT.Tanh, 0.5, half_bias, *need)

    n_load = [0]

    def load(o, i, *need):
        s = sem(f"ld{n_load[0]}")
        n_load[0] += 1
        sp.put(lambda e: e.dma_start(o, i), need, s, 16)
        return (s, 16)

    st8 = [sb(f"st8{i}", [128, 8])[:] for i in range(2)]
    small = Ring(st8)

    def split(hi, lo, src, *need, E=dve):
        a = copy(act, hi, src, *need)
        b = tt(E, lo, src, hi.bitcast(F), ALU.subtract, a, *need)
        return [a, b]

    t_v = load(V[:], vecs)
    t_c = []

    omu, oka = VD[:, 0:20], VD[:, 20:26]
    mu_all = V[:, V_AT["mu"][0]:V_AT["mu"][0] + 20]
    ka_all = V[:, V_AT["ka"][0]:V_AT["ka"][0] + 6]
    t_vd = [ts(dve, omu, mu_all, -1.0, 1.0, ALU.mult, ALU.add, t_v),
            ts(dve, oka, ka_all, -1.0, 1.0, ALU.mult, ALU.add, t_v)]
    hw0, ha0 = VD[:, 29:35], VD[:, 35:41]
    for half_of, name in ((hw0, "w0"), (ha0, "a0")):
        full = V[:, V_AT[name][0]:V_AT[name][0] + 6]
        t_vd.append(ts(dve, half_of, full, 0.5, None, ALU.mult, None, t_v))
    scaled = {}
    for i, name in enumerate(("mq", "qa", "qb")):
        scaled[name] = VD[:, 26 + i:27 + i]
        t_vd.append(ts(dve, scaled[name], v(name), 0.125, None, ALU.mult, None, t_v))

    class Stream:
        def __init__(self):
            self.loads, self.splits, self.got = [], [], 0
            self.sems = [sem(f"w{i}") for i in range(NW)]

        def load_ahead(self, n):
            while len(self.loads) < n:
                u = len(self.loads)
                k, raw, last = Wraw.take()
                width = units[u][1]
                s = self.sems[k]
                sp.put(lambda e, raw=raw, u=u, width=width: e.dma_start(raw[:, 0:width], wts[u, :, 0:width]),
                       [last], s, 16)
                self.loads.append((k, raw, (s, 16 * (u // NW + 1))))

        def advance(self, n_split):
            while len(self.splits) < min(n_split, len(units)):
                self.load_ahead(min(len(self.splits) + NW, len(units)))
                u = len(self.splits)
                k, raw, tok = self.loads[u]
                width = units[u][1]
                kk, (hi, lo), last = Wsp.take()
                toks = split(hi[:, 0:width], lo[:, 0:width], raw[:, 0:width], tok, last,
                             E=lows[0])
                Wraw.free(k, toks)
                self.splits.append((kk, hi, lo, toks))

        def get(self, name):
            u = self.got
            assert units[u][0] == name, (units[u][0], name)
            self.got += 1
            self.advance(u + NW - 1)
            return self.splits[u]

        def free(self, unit, tok):
            Wsp.free(unit[0], tok)

    lows = [dve]
    W = Stream()

    def mm3(o, whi, wlo, xhi, xlo, first, last, *need):
        mm(o, whi, xhi, first, False, *need)
        mm(o, wlo, xhi, False, False)
        mm(o, whi, xlo, False, last)

    def tile_t(name, a, ks, epi, n=T, j0=0, keep=None, hold=None, js=None):
        unit = keep if keep is not None else W.get(name)
        b, bank, rel = D.take()
        for i, k in enumerate(ks):
            j = (j0 + (i if js is None else js[i])) * 128
            mm3(bank[:, 0:n], unit[1][:, j:j + 128], unit[2][:, j:j + 128], a.hi[:, k, 0:n],
                a.lo[:, k, 0:n], i == 0, i == len(ks) - 1, unit[3], rel, a.tok[k])
            if i in (2, 5):
                flush()
            yield
        t = pe.tick()
        if hold is None:
            W.free(unit, t)
        else:
            hold.append(unit)
        done = epi(bank, t)
        D.free(b, done)

    def gained(i, x, tok, gname, a, n, *need, by_column=False):
        hi, lo = a.hi[:, i, 0:n], a.lo[:, i, 0:n]
        if by_column:
            hi, lo, x = columns(hi), columns(lo), rows(x)
        h = actf(hi, x, ACT.Copy, v(gname, i), None, tok, t_v, *need)
        a.tok[i] = [h, stt(lo, x, v(gname, i), hi.bitcast(F), ALU.mult, ALU.subtract, h, tok, t_v, *need)]
        return a.tok[i]

    def roots(sq, n, mat, scale, bias, floor, *need):
        k, bank, rel = M.take()
        for j in range(n // 128):
            mm(bank[:, 128 * j:128 * j + 128], sq[:, 128 * j:128 * j + 128], c(mat), True, True, rel,
               list(need), t_c)
        t = pe.tick()
        z, st, last = small.take()
        st = st[:, 0:n // 64]
        one = bank[:, 0:n].rearrange("p (j x) -> p j x", x=64)[:, :, 0:1]
        x = actf(st.unsqueeze(2), one, ACT.Sqrt, scale, bias, t, last)
        M.free(k, x)
        if floor is not None:
            x = ts(dve, st, st, floor, None, ALU.max, None, x)
        x = recip(st, st, x)
        wide = sq[:, 0:n].rearrange("p (j x) -> p j x", x=64)
        d = copy(dve, wide, st.unsqueeze(2).broadcast_to([128, n // 64, 64]), x, t)
        small.free(z, d)
        return st, x, d

    def spread(sq, n, need):
        k, bank, rel = M.take()
        for j in range(n // 128):
            transpose(bank[:, 128 * j:128 * j + 128], sq[:, 128 * j:128 * j + 128], c("ident"), rel, need)
        return k, bank, pe.tick()

    def inverse_rms(sq, tsq, rs, done, *need, n=T, rsn=None):
        st, x, d = roots(sq, n, "mean", 1.0, c("rmseps"), None, tsq)
        if rsn is not None:
            done.append(copy(dve, rsn.unsqueeze(2), st.rearrange("p (j h) -> p j h", h=2)[:, :, 0:1], x,
                             *need))
        yield
        k, bank, t = spread(sq, n, d)
        y = copy(dve, rs[:, 0:n], bank[:, 0:n], t, *need)
        M.free(k, y)
        done.append(y)

    def around(g1, g2, norm):
        for _ in range(8):
            next(g1)
        next(norm)
        for _ in range(3):
            next(g2)
        run(norm)
        run(g1)
        run(g2)

    def rows(ap):
        return ap.rearrange("p (r c) -> p r c", r=8)

    def columns(ap):
        return ap.rearrange("p (c r) -> p r c", r=8)

    def squares_step(i, x, tok, acc, tmp, last, n=T, by_column=False):
        turn = columns if by_column else (lambda ap: ap)
        if by_column:
            x = rows(x)
        if i == 0:
            return actf(turn(acc[:, 0:n]), x, ACT.Square, 1.0, None, tok, last)
        q, tile, free = tmp.take()
        a = actf(turn(tile[:, 0:n]), x, ACT.Square, 1.0, None, tok, free)
        last = tt(pool, acc[:, 0:n], acc[:, 0:n], tile[:, 0:n], ALU.add, a, last)
        tmp.free(q, last)
        return last

    def load_on(E, o, i, s, count, *need):
        E.put(lambda e: e.dma_start(o, i), need, s, 16)
        return (s, 16 * count)

    pend = []

    def flush():
        now, pend[:] = pend[:], []
        for f in now:
            f()

    def fence():
        return [e.tick() for e in (pe, dve, act, pool) if e.ops]

    def softmax(bank, n, bias, sink, ring, stats, need):
        q, s, last = ring.take()
        z, st, slast = stats.take()
        s = s[:, 0:n]
        if bias is None:
            src, d = bank, need
        else:
            src = s
            d = tt(dve, s, bank, bias, ALU.add, need, last)
        m = dve.step(lambda e: e.tensor_reduce(st[:, 0:1], src, AXX, ALU.max), d, slast)
        if sink is None:
            m = ts(dve, st[:, 1:2], st[:, 0:1], -1.0, None, ALU.mult, None, m)
        else:
            m = ts(dve, st[:, 1:2], st[:, 0:1], sink, -1.0, ALU.max, ALU.mult, m)
        x = act.step(lambda e: e.activation(s, src, ACT.Exp, scale=1.0, bias=st[:, 1:2],
                                            accum_out=st[:, 2:3]), m, last)
        yield [d, x] if bias is None else [d]
        r = x
        if sink is not None:
            y = actf(st[:, 4:5], sink, ACT.Exp, 1.0, st[:, 1:2], m)
            r = tt(dve, st[:, 2:3], st[:, 2:3], st[:, 4:5], ALU.add, x, y)
        r = recip(st[:, 3:4], st[:, 2:3], r)
        r = actf(s, s, ACT.Copy, st[:, 3:4], None, r)
        stats.free(z, r)
        yield q, s, r

    def pipeline(items):
        items, active = list(items), []
        while items or active:
            if items:
                active.append(items.pop(0))
            for g in list(active):
                if next(g, False) is False:
                    active.remove(g)
            yield

    def rounds(n):
        for _ in range(n):
            yield

    def weave(main, filler, per):
        due = 0.0
        for weight in main:
            due += per * (weight or 1)
            while due >= 1:
                due -= 1
                next(filler, None)

    def head_norm(src, rs, dst, need, tmp):
        q, raw, last = tmp.take()
        q2, sq, last2 = tmp.take()
        n = src.shape[1]
        a = tt(dve, raw[:, 0:n], src, rs, ALU.mult, need, last)
        b = actf(sq[:, 0:n], raw[:, 0:n], ACT.Square, 1.0, None, a, last2)

        def rest():
            st, x, d = roots(sq, n, "bd64", 1.0, c("rmseps"), None, b)

            def then():
                k, bank, t = spread(sq, n, d)
                z = dst(raw[:, 0:n], bank[:, 0:n], [t, a])
                M.free(k, z)
                tmp.free(q, z)
                tmp.free(q2, t)
            pend.append(then)
        pend.append(rest)
        return [a]

    arena = top[0]
    slab = [sb(f"slab{i}", [128, T]) for i in range(3)]
    WA, GD = sb("WA", [128, T]), sb("GD", [128, T])
    w2s, g2s = sb("w2s", [128, 768]), sb("g2s", [128, 768])
    RS = sb("RS", [128, T])
    ftmp = Ring([sb(f"ftmp{i}", [128, T]) for i in range(2)])
    sg, Pi, ta, kf, kn = (sb(n, [128, T]) for n in ("sg", "Pi", "ta", "kf", "kn"))
    Pp = sb("Pp", [128, NC, 65])
    bonus2 = [sb(f"bonus{i}", [128, T]) for i in range(2)]
    PC2 = [sb(f"PC{i}", [128, NC]) for i in range(2)]
    mst = sb("mst", [128, 16])
    mstats = Ring([mst[:, 4 * i:4 * i + 4] for i in range(4)])
    low = top[0]

    memX = sb("memX", [128, 8, 256])
    memH = Act(sb("memHhi", [128, 8, 256], R), sb("memHlo", [128, 8, 256], R), 8)
    x0 = Ring([sb(f"x0{i}", [128, T]) for i in range(4)])
    acc, accm, RSm = sb("acc", [128, T]), sb("accm", [128, 256]), sb("RSm", [128, 256])
    rsn = sb("rsn", [128, 2])
    uhi, ulo = U_AT[0] + 2048, U_AT[1] + 2048
    qm = sb_at("qm", [128, 2, T], F, uhi)
    pTm = Ring([sb_at(f"pTm{i}", [128, 2, T], F, a) for i, a in enumerate((uhi + 4096, ulo))])
    sring = Ring([sb_at(f"ms{i}", [128, 256], F, ulo + 4096 + 1024 * i) for i in range(4)])
    km, vm = (sb_at(n, [128, 2, 256], F, a) for n, a in (("km", uhi + 8192), ("vm", ulo + 8192)))
    low_end = (nc.sbuf_usable_end - 5 * 4096) // 32 * 32
    assert top[0] <= low_end, top[0]
    top[0] = low_end
    BDb, BDk, BDa, BDv, AR = (sb(n, [128, NC, 128]) for n in ("BDb", "BDk", "BDa", "BDv", "AR"))
    t_z = [pool.step(lambda e, b=b: e.memset(b[:], 0.0)) for b in (BDb, BDk, BDa, BDv)]
    assert top[0] <= nc.sbuf_usable_end, top[0]

    H, U = Act(Hhi, Hlo, 8), Act(Uhi, Ulo, 8)

    last = None
    sem_x = [sem(f"x{i}") for i in range(4)]
    for i in range(8):
        q, tile, free = x0.take()
        t_x = load_on(sp, tile[:], xT[i], sem_x[i % 4], i // 4 + 1, free)
        if i < 2:
            W.load_ahead(i + 1)
        if i == 3:
            t_c.append(load(C[:], cst))
        g = gained(i, tile[:], t_x, "gmix", H, T)
        last = squares_step(i, tile[:], t_x, acc, ftmp, last)
        x0.free(q, g, last)
        if i == 0:
            W.advance(1)
    W.advance(2)
    t_w2, t_g2 = load(w2s[:], w2a2), load(g2s[:], g2)
    t_m = [load(memX[:, 4 * i:4 * i + 4, :], memT[4 * i:4 * i + 4].rearrange("k p n -> p k n"))
           for i in range(2)]

    t_lora, t_rs = {}, []

    def shift(dst, bank, j, t, *need):
        q, z, last = ftmp.take()
        m = tt(dve, z[:], bank[:], RS[:], ALU.mult, t, last, t_rs)
        a = actf(dst[:], z[:], ACT.Copy, omu[:, j:j + 1], None, m, t_vd, *need)
        d = stt(dst[:, 1:T], z[:, 0:T - 1], v("mu", j), dst[:, 1:T], ALU.mult, ALU.add, a)
        ftmp.free(q, d)
        return m, d

    def wa_epi(bank, t):
        m, d = shift(WA, bank, 18, t)
        t_lora["wa"] = [d, actf(WA[0:64, :], WA[0:64, :], ACT.Tanh, 1.0, None, d)]
        return [m]

    def gd_epi(bank, t):
        m, d = shift(GD, bank, 19, t)
        t_lora["gd"] = actf(GD[:], GD[:], ACT.Sigmoid, 1.0, None, d)
        return [m]

    around(tile_t(("rw", 18), H, range(8), wa_epi), tile_t(("rw", 19), H, range(8), gd_epi),
           inverse_rms(acc[:], last, RS, t_rs))

    t_qm, t_km = [None, None], [None, None]

    def qm_epi(i):
        def epi(bank, t):
            def dst(raw, rs, need):
                t_qm[i] = stt(qm[:, i, :], raw, scaled["mq"], rs, ALU.mult, ALU.mult, need, t_vd)
                return t_qm[i]
            return head_norm(bank[:], RS[:], dst, [t, t_rs], x0)
        return epi

    tm = {}

    def km_epi(i):
        def epi(bank, t):
            def dst(raw, rs, need):
                a = tt(dve, km[:, i, :], raw, rs, ALU.mult, need)
                t_km[i] = ts(dve, km[:, i, :], km[:, i, :], v("mk"), None, ALU.mult, None, a)
                return t_km[i]
            return head_norm(bank[:, 0:256], RSm[:], dst, [t, tm["rs"]], x0)
        return epi

    def mem_norm():
        last = None
        for i in range(8):
            gained(i, memX[:, i, :], t_m[i // 4], "gmem", memH, 256)
            last = squares_step(i, memX[:, i, :], t_m[i // 4], accm, ftmp, last, 256)
            yield
        tm["sq"] = last

    def mem_projections():
        tm["rs"] = []
        norm = inverse_rms(accm[:], tm["sq"], RSm, tm["rs"], n=256, rsn=rsn[:])
        next(norm)
        yield from tile_t(("rw", 20), H, range(8), qm_epi(0))
        run(norm)
        yield from tile_t(("rw", 21), H, range(8), qm_epi(1))
        for i in range(2):
            yield from tile_t(("memk", i), memH, range(8), km_epi(i), n=256)
        got = [D.take(), D.take()]
        for u in range(2):
            unit = W.get(("memv", u))
            for m in range(2):
                k_, bank, rel = got[m]
                for i in range(4):
                    k = 4 * u + i
                    xh, xl = memH.hi[:, k, 128 * m:128 * m + 128], memH.lo[:, k, 128 * m:128 * m + 128]
                    wh, wl = unit[1][:, 256 * i:256 * i + 256], unit[2][:, 256 * i:256 * i + 256]
                    o = bank[:, 0:256]
                    mm(o, xh, wh, k == 0, False, unit[3], rel, memH.tok[k])
                    mm(o, xh, wl, False, False)
                    mm(o, xl, wh, False, k == 7)
                yield
                flush()
            W.free(unit, pe.tick())
        t = pe.tick()
        for m in range(2):
            t_vm.append(actf(vm[:, m, :], got[m][1][:, 0:256], ACT.Copy, rsn[:, m:m + 1], None, t, tm["rs"]))
            D.free(got[m][0], t_vm[-1])

    t_vm = []

    def transposed(p, n, dst, need, pt_ring_tok):
        k, bank, rel = M.take()
        for b in range(n // 128):
            transpose(bank[:, 128 * b:128 * b + 128], p[:, 128 * b:128 * b + 128], c("ident"),
                      rel, need, t_c)
        t = pe.tick()
        d = copy(dve, dst, bank[:, 0:n].rearrange("p (b x) -> p b x", x=128), t, pt_ring_tok)
        M.free(k, d)
        return t, d

    def mem_head(h):
        off, kt = 64 * (h % 2), h // 2
        q, pT, plast = pTm.take()
        pt = []

        def item(j):
            k, bank, rel = M.take()
            mm(bank[:, 0:256], qm[off:off + 64, kt, 128 * j:128 * j + 128], km[off:off + 64, kt, :],
               True, True, rel, t_qm[kt], t_km[kt])
            t = pe.tick()
            soft = softmax(bank[:, 0:256], 256, None, None, sring, mstats, t)
            M.free(k, next(soft))
            yield
            z, p, r = next(soft)
            yield from rounds(SOFT_ROUNDS)
            a, d = transposed(p, 256, pT[:, :, 128 * j:128 * j + 128], r, plast)
            sring.free(z, a)
            pt.append(d)

        yield from pipeline([item(j) for j in range(4)])
        k, bank, rel = M.take()
        rows_ = slice(off, off + 64)
        for b in range(2):
            mm(bank[rows_, :], vm[:, b, 64 * h:64 * h + 64], pT[:, b, :], b == 0, b == 1, rel, t_vm, pt)
        t = pe.tick()
        pTm.free(q, t)
        hi, lo = Uhi[rows_, 6 + kt, :], Ulo[rows_, 6 + kt, :]
        a = copy(act, hi, bank[rows_, :], t)
        yield
        d = tt(dve, lo, bank[rows_, :], hi.bitcast(F), ALU.subtract, a)
        M.free(k, d)
        U.tok[6 + kt] = [U.tok[6 + kt], a, d]
        yield

    def mem_attention():
        for h in range(4):
            yield from mem_head(h)

    t_slab, slab_free = [None] * 3, [[], [], []]

    def slab_epi(i, j):
        def epi(bank, t):
            m, t_slab[i] = shift(slab[i], bank, j, t, slab_free[i])
            return [m]
        return epi

    def projections(p):
        for i in range(3):
            yield from tile_t(("rw", 6 * i + p), H, range(8), slab_epi(i, 6 * i + p))

    def half(bd, h, c0=0, c1=NC):
        return bd[64 * h:64 * h + 64, c0:c1, 64 * h:64 * h + 64]

    def stk(t, h=None, c0=0, c1=NC):
        w = t.rearrange("p (c x) -> p c x", x=64) if len(t.shape) == 2 else t
        return w[:, c0:c1, :] if h is None else w[64 * h:64 * h + 64, c0:c1, :]

    def bcast(ap, n):
        return ap.unsqueeze(1).broadcast_to([ap.shape[0], n, ap.shape[1]])

    r_, k_, v_ = slab
    t_one = pool.step(lambda e: e.memset(Pp[:, :, 0:1], 1.0))
    front_free, fr, bonus_free = [[]], {}, [None]

    def rates(p):
        free = front_free[0]
        PC = PC2[p % 2]
        k1, b1, rel = M.take()
        mm(b1[:], w2s[0:64, 128 * p:128 * p + 128], WA[0:64, :], True, True, rel, t_w2, t_lora["wa"])
        t = pe.tick()
        a = sigmoid(sg[:], b1[:], hw0[:, p:p + 1], t, t_vd, free)
        M.free(k1, a)
        a = ts(pool, sg[:], sg[:], 0.5, 0.5, ALU.mult, ALU.add, a)
        yield
        k1, b1, rel = M.take()
        mm(b1[:], w2s[64:128, 128 * p:128 * p + 128], WA[64:128, :], True, True, rel)
        t = pe.tick()
        a2 = sigmoid(ta[:], b1[:], ha0[:, p:p + 1], t, free)
        M.free(k1, a2)
        a2 = ts(pool, ta[:], ta[:], 0.5, 0.5, ALU.mult, ALU.add, a2)
        yield
        d = dve.step(lambda e: e.tensor_tensor_scan(sg[:], c("scan"), sg[:], 0.0, ALU.mult, ALU.add), a)
        f = ts(dve, kf[:], ta[:], v("ka", p), oka[:, p:p + 1], ALU.mult, ALU.add, a2, t_vd, free)
        yield
        e1 = actf(Pp[:, :, 1:65], stk(sg), ACT.Exp, -DECAY, None, d, t_one, free)
        e2 = actf(Pi[:], sg[:], ACT.Exp, DECAY, None, d, free)
        rt.update(f=f, e1=e1, e2=e2, PC=PC, pc=copy(pool, PC[:].unsqueeze(2), Pp[:, :, 64:65], e1, free))
        yield

    rt = {}

    def front(p):
        free = front_free[0]
        bonus = bonus2[p % 2]
        q, tm, last = ftmp.take()
        sq = actf(tm[:], k_[:], ACT.Square, v("kk", p), None, t_slab[1], last)
        f = tt(pool, kf[:], kf[:], k_[:], ALU.mult, rt["f"], t_slab[1])
        yield from rounds(2)
        st, x, nrm = roots(tm, T, "bd64", 64.0, None, 1e-12, sq)
        yield from rounds(2)
        k1, b1, t = spread(tm, T, nrm)
        kkt = stt(kn[:], k_[:], v("kk", p), b1[:], ALU.mult, ALU.mult, t, free)
        M.free(k1, kkt)
        bt = tt(pool, ta[:], ta[:], kn[:], ALU.mult, kkt, f)
        rk = stt(tm[:], r_[:], v("rk", p), kf[:], ALU.mult, ALU.mult, kkt, f, t_slab[0])
        yield from rounds(2)
        k1, b1, rel = M.take()
        mm(b1[:], c("bd64"), tm[:], True, True, rel, rk)
        t = pe.tick()
        bo = stt(bonus[:], b1[:], 64.0, v_[:], ALU.mult, ALU.mult, t, t_slab[2], free, bonus_free[0])
        M.free(k1, bo)
        ftmp.free(q, t)
        fr.update(rt)
        fr.update(f=f, kkt=kkt, bt=bt, bo=bo, rk=rk, t_slab=list(t_slab), bonus=bonus)
        yield

    def ahead(p):
        yield from rates(p)
        yield from projections(p)
        yield from front(p)

    top[0] = low

    def tile4(name):
        return sb(name, [128, NC, 128])

    MT, AK, RB, RK, BR, GA = (tile4(n) for n in ("MT", "AK", "RB", "RK", "BR", "GA"))
    Bn, Kn, Vn = (tile4(n) for n in ("Bn", "Kn", "Vn"))
    y2, z2 = sb("y2", [128, T])[:], sb("z2", [128, T])[:]
    assert top[0] <= low_end, top[0]
    Xb, T1, Yb, U0, W1, Phi, Rt, PD = BDb, BDk, BDa, BDv, AK, Kn, MT, Bn

    war = [[]]
    CC = ((0, 4), (4, 8))

    def chunks(bank):
        return bank[:].rearrange("p (c x) -> p c x", x=128)

    def masked(name, n=4):
        return bcast(c(name), n)

    def products(w, rhs, need, hf, w2=None, rhs2=None, need2=None, chs=None):
        k1, b1, rel = M.take()
        for i in range(4):
            ch = 4 * hf + i
            if chs is not None and ch not in chs:
                continue
            o = b1[:, 128 * i:128 * i + 128]
            mm(o, w[:, ch, :], rhs[:, ch, :], True, w2 is None, rel, need)
            if w2 is not None:
                mm(o, w2[:, ch, :], rhs2[:, ch, :], False, True, need2)
        return k1, b1, pe.tick()

    def transposes(w, need, hf):
        k1, b1, rel = M.take()
        for i in range(4):
            transpose(b1[:, 128 * i:128 * i + 128], w[:, 4 * hf + i, :], c("ident"), rel, need, t_c)
        return k1, b1, pe.tick()

    def pair(p):
        free = war[0]
        f_ = dict(fr)
        ts_ = f_["t_slab"]
        ar = [tt(dve, AR[:, :, 0:64], stk(kn), Pp[:, :, 0:64], ALU.mult, f_["e1"], f_["kkt"], free)]
        bb = [tt(dve, half(BDb, h), stk(ta, h), stk(Pi, h), ALU.mult, f_["e2"], f_["bt"], t_z, free)
              for h in range(2)]
        ar.append(tt(dve, AR[:, :, 64:128], stk(r_), Pp[:, :, 1:65], ALU.mult, ts_[0]))
        bk = [tt(pool, half(BDk, h), stk(kf, h), stk(Pi, h), ALU.mult, f_["e2"], f_["f"], t_z, free)
              for h in range(2)]
        ba = [copy(act, half(BDa, h), AR[64 * h:64 * h + 64, :, 0:64], ar[0], t_z, free)
              for h in range(2)]
        bv = [copy(act, half(BDv, h), stk(v_, h), ts_[2], t_z, free) for h in range(2)]
        slab_free[0] = [ar[1], f_["rk"]]
        slab_free[1] = [f_["kkt"], f_["f"]]
        slab_free[2] = [bv, f_["bo"]]
        front_free[0] = [ar, bb, bk]
        yield 1
        free = war[0]

        def score(w, need, full, mask, full2, mask2, keep2, hf):
            k1, b1, t = products(w, AR, [ar, need], hf)
            src = chunks(b1)
            c0, c1 = CC[hf]
            done = []
            for o, x, m in ((full, 0, mask), (full2, 64, mask2)):
                s4 = src[:, :, x:x + 64].unsqueeze(2).broadcast_to([128, 4, 2, 64])
                m4 = c(m).rearrange("p (h x) -> p h x", h=2).unsqueeze(1).broadcast_to([128, 4, 2, 64])
                o4 = o[:, c0:c1, :].rearrange("p c (h x) -> p c h x", h=2)
                done.append(tt(dve, o4, s4, m4, ALU.mult, t, free))
            if keep2 is not None:
                done.append(tt(dve, keep2[:, c0:c1, 64:128], src[:, :, 64:128], bcast(c(mask2 + "s"), 4),
                               ALU.mult, t))
            M.free(k1, done)
            return done

        sb1, sk1 = [None] * 2, [None] * 2
        for hf in range(2):
            sb1[hf] = score(BDb, bb, MT, "mneg", RB, "inclneg", BR, hf)
            yield
        nbs, na, nv, nk = {}, {}, {}, {}
        nb = {}
        y, x = [None] * 2, [None] * 2
        for hf in range(2):
            c0, c1 = CC[hf]
            k1, b1, t = transposes(BDa, ba, hf)
            na[hf] = [copy(act, GA[64 * h:64 * h + 64, c0:c1, 64:128],
                           chunks(b1)[64 * h:64 * h + 64, :, 64 * h:64 * h + 64], t, free)
                      for h in range(2)]
            M.free(k1, na[hf])
            d = tt(pool, Yb[:, c0:c1, :], MT[:, c0:c1, :], masked("level1t"), ALU.mult, sb1[hf][0], t)
            y[hf] = tt(pool, Yb[:, c0:c1, :], Yb[:, c0:c1, :], masked("ident"), ALU.add, d)
            yield
        for hf in range(2):
            c0, c1 = CC[hf]
            k1, b1, t = transposes(BDb, bb, hf)
            nb[hf] = actf(Bn[:, c0:c1, :], chunks(b1), ACT.Copy, -1.0, None, t, free)
            M.free(k1, nb[hf])
            yield
        for hf in range(2):
            sk1[hf] = score(BDk, bk, AK, "mpos", RK, "inclpos", None, hf)
            yield
        for hf in range(2):
            c0, c1 = CC[hf]
            k1, b1, t = transposes(BDv, bv, hf)
            nv[hf] = copy(act, Vn[:, c0:c1, :], chunks(b1), t, free)
            M.free(k1, nv[hf])
            k1, b1, t = transposes(BDk, bk, hf)
            nk[hf] = copy(act, Kn[:, c0:c1, :], chunks(b1), t, free)
            M.free(k1, nk[hf])
            yield
        for hf in range(2):
            c0, c1 = CC[hf]
            k1, b1, t = transposes(Yb, y[hf], hf)
            x[hf] = copy(act, Xb[:, c0:c1, :], chunks(b1), t)
            M.free(k1, x[hf])
        for hf in range(2):
            c0, c1 = CC[hf]
            nbs[hf] = [copy(act, BR[64 * h:64 * h + 64, c0:c1, 0:64], half(Bn, h, c0, c1), nb[hf], free)
                       for h in range(2)]
        gv = [None] * 2
        for l in range(1, len(LEVELS)):
            t1 = [None] * 2
            for hf in range(2):
                c0, c1 = CC[hf]
                k1, b1, t = products(MT, Xb, [x[hf], sb1[hf]], hf)
                t1[hf] = tt(dve, T1[:, c0:c1, :], chunks(b1), bcast(c("level", 128 * (l - 1), 128), 4),
                            ALU.mult, t)
                M.free(k1, t1[hf])
                yield
            if l == 1:
                for hf in range(2):
                    c0, c1 = CC[hf]
                    k1, b1, t = products(AK, Vn, [nv[hf], sk1[hf]], hf)
                    gv[hf] = [copy(act, GA[64 * h:64 * h + 64, c0:c1, 0:64],
                                   chunks(b1)[64 * h:64 * h + 64, :, 64 * h:64 * h + 64], t, free)
                              for h in range(2)]
                    M.free(k1, gv[hf])
                yield
            if l < len(LEVELS) - 1:
                for hf in range(2):
                    c0, c1 = CC[hf]
                    k1, b1, t = products(Yb, T1, [y[hf], t1[hf]], hf)
                    x[hf] = tt(dve, Xb[:, c0:c1, :], chunks(b1), Xb[:, c0:c1, :], ALU.add, t)
                    M.free(k1, x[hf])
                    yield
                for hf in range(2):
                    c0, c1 = CC[hf]
                    k1, b1, t = transposes(Xb, x[hf], hf)
                    y[hf] = copy(act, Yb[:, c0:c1, :], chunks(b1), t)
                    M.free(k1, y[hf])
                    yield
            else:
                for hf in range(2):
                    c0, c1 = CC[hf]
                    k1, b1, t = products(T1, Yb, [y[hf], t1[hf]], hf)
                    y[hf] = tt(dve, Yb[:, c0:c1, :], chunks(b1), Yb[:, c0:c1, :], ALU.add, t)
                    M.free(k1, y[hf])
                    yield
        uw = [None] * 2
        for hf in range(2):
            k1, b1, t = products(Yb, GA, [y[hf], gv[hf], na[hf]], hf)
            uw[hf] = [copy(act, half(w, h, *CC[hf]), chunks(b1)[64 * h:64 * h + 64, :, o:o + 64], t)
                      for w, o in ((U0, 0), (W1, 64)) for h in range(2)]
            M.free(k1, uw[hf])
            yield
        st, PC = [None] * NC, f_["PC"]
        for hf in range(2):
            c0, c1 = CC[hf]
            n = min(c1, NC - 1) - c0
            k1, b1, t = products(Bn, U0, [nb[hf], uw[hf]], hf, Kn, Vn, nk[hf], range(NC - 1))
            pc = PC[:, c0:c0 + n].unsqueeze(2).broadcast_to([128, n, 128])
            d = tt(dve, PD[:, c0:c0 + n, :], chunks(b1)[:, 0:n, :], pc, ALU.mult, t, fr_pc, free, nbs[hf])
            M.free(k1, d)
            for i in range(c0, c0 + n):
                st[i] = d
            yield
        ph = [None] * 2
        for hf in range(2):
            c0, c1 = CC[hf]
            k1, b1, t = products(W1, BR, [uw[hf], nbs[hf]], hf)
            src = chunks(b1)
            ph[hf] = [tt(dve, half(Phi, h, c0, c1), src[64 * h:64 * h + 64, :, 0:64],
                         bcast(c("ident", 64 * h, 64), 4)[64 * h:64 * h + 64], ALU.add, t) for h in range(2)]
            ph[hf] += [tt(dve, half(Rt, h, c0, c1), src[64 * h:64 * h + 64, :, 64:128],
                          AR[64 * h:64 * h + 64, c0:c1, 64:128], ALU.add, t) for h in range(2)]
            M.free(k1, ph[hf])
            yield
        ko, ob, orel = O.take()
        ke = None
        yy = []
        for ch in range(NC):
            if 1 <= ch < NC - 1:
                o = ob[:, 128 * (ch % 4):128 * (ch % 4) + 128]
                mm(o, Phi[:, ch, :], PD[:, ch - 1, :], True, True, orel, st[ch - 1], ph[ch // 4])
                t = pe.tick()
                st[ch] = stt(PD[:, ch, :], o, PC[:, ch:ch + 1], PD[:, ch, :], ALU.mult, ALU.add, t)
            if ch % 4 == 0:
                ke, yb, rel = Y.take()
            o = yb[:, 128 * (ch % 4):128 * (ch % 4) + 128]
            mm(o, U0[:, ch, :], RB[:, ch, :], True, False, rel)
            mm(o, Vn[:, ch, :], RK[:, ch, :], False, ch == 0)
            if ch:
                mm(o, PD[:, ch - 1, :], Rt[:, ch, :], False, True, st[ch - 1], ph[ch // 4])
            if ch % 4 == 3:
                t = pe.tick()
                x_ = [copy(act, stk(y2, h, ch - 3, ch + 1),
                           chunks(yb)[64 * h:64 * h + 64, :, 64 * h:64 * h + 64], t, y2_free[0])
                      for h in range(2)]
                Y.free(ke, x_)
                yy.append(x_)
            yield STATE_WEIGHT
        O.free(ko, st[NC - 2])
        war[0] = [t]
        f_["yy"] = yy
        done_[p] = f_

    done_, mem_done, fr_pc = {}, [], []
    y2_free = [war]

    def tail(p):
        f_ = done_[p]
        k1, b1, rel = M.take()
        mm(b1[:], c("bd64"), y2, True, True, rel, f_["yy"])
        t = pe.tick()
        d = tt(dve, y2, y2, b1[:], ALU.subtract, t)
        M.free(k1, d)
        s = actf(z2, y2, ACT.Square, 1.0, None, d, y2_free[0])
        yield
        yield
        st, x, d = roots(z2, T, "bd64", 1.0, c("gneps"), None, s)
        yield
        yield
        k1, b1, t = spread(z2, T, d)
        x = tt(dve, y2, y2, b1[:], ALU.mult, t)
        M.free(k1, x)
        z_free = t
        x = ts(dve, y2, y2, v("lng", p), v("lnb", p), ALU.mult, ALU.add, x)
        x = tt(pool, y2, y2, f_["bonus"][:], ALU.add, x)
        bonus_free[0] = x
        yield
        k1, b1, rel = M.take()
        mm(b1[:], g2s[:, 128 * p:128 * p + 128], GD[:], True, True, rel, t_g2, t_lora["gd"])
        t = pe.tick()
        x = tt(dve, y2, y2, b1[:], ALU.mult, x, t)
        M.free(k1, x)
        U.tok[p] = split(Uhi[:, p, :], Ulo[:, p, :], y2, x, mem_done)
        y2_free[0] = [x, U.tok[p], z_free]
        yield

    def turns(*gens):
        gens = list(gens)
        while gens:
            for g in list(gens):
                try:
                    next(g)
                    yield
                except StopIteration:
                    gens.remove(g)

    normed = mem_norm()
    early = turns(normed, rates(0))
    weave(projections(0), early, 0.5)
    run(early)
    pair0 = pair(0)

    def front0():
        yield from front(0)
        fr_pc.append(fr["pc"])
        yield next(pair0)

    filler = front0()
    weave(mem_projections(), filler, FILL_FRONT)
    run(filler)
    flush()
    flush()
    war[0] = fence()

    lows[0] = pool
    mem_att = mem_attention()
    WO = (0, 1, 2, 3, 6, 7, 4, 5)
    def residual(i, gname=None, to=None, by_column=False):
        def epi(bank, t):
            x, y = X[:, i, :], bank[:]
            if by_column:
                x, y = rows(x), columns(y)
            d = tt(dve, x, x, y, ALU.add, t, xtok[i])
            xtok[i] = d
            if gname is not None:
                gained(i, X[:, i, :], d, gname, to, T, by_column=gname == "gmix2")
                sqlast[0] = squares_step(i, X[:, i, :], d, accb, tmps, sqlast[0] if i else sq_free[0],
                                         by_column=gname == "gmix2")
            return [d]
        return epi

    for p in range(NP):
        fr_pc[:] = [fr["pc"]]
        gens = []
        if p == 0:
            gens.append(itertools.islice(mem_att, MEM_STEPS))
        if p == 1:
            gens.append(mem_att)
        if p == 2:
            mem_done.append(fence())
        if p:
            gens.append(tail(p - 1))
        if p + 1 < NP:
            gens.append(ahead(p + 1))
        else:
            X = sb_at("X", [128, 8, T], F, H_AT)
            xtok = [load(X[:, 4 * i:4 * i + 4, :], xT[4 * i:4 * i + 4].rearrange("k p n -> p k n"), fence())
                    for i in range(2)]
            xtok = [xtok[i // 4] for i in range(8)]
            outs = [tile_t(("wo", i), U, WO, residual(i, "gffn", H), js=WO) for i in range(2)]
            gens = [itertools.chain(*gens, *(itertools.islice(g, 7) for g in outs))]
        filler = turns(*gens)
        weave(pair(p) if p else pair0, filler,
              FILL_PAIR_LAST if p == NP - 1 else FILL_PAIR if p > 1 else FILL_PAIR_FIRST)
        if p < NP - 1:
            run(filler)
    lows[0] = dve
    weave(tail(NP - 1), filler, FILL_TAIL)
    run(filler)
    old = fence()

    top[0] = arena
    Hhi = sb("Hhi2", [128, 8, T], R)
    H.hi = Hhi
    RSb, accb, rsnb = sb("RSb", [128, T]), sb("accb", [128, T]), sb("rsnb", [128, 4])
    tmps = Ring([sb(f"tmpb{i}", [128, T]) for i in range(4)])
    tmps.last = [[old] for _ in tmps.last]
    sqlast = [None]

    sq_free = [old]

    def norm_x(done, rsn=None):
        yield from inverse_rms(accb[:], sqlast[0], RSb, done, rs_free[0], rsn=rsn)
        sq_free[0] = pe.tick()

    rs_free = [old]
    for i in range(8):
        run(outs[i] if i < 2 else tile_t(("wo", i), U, range(8), residual(i, "gffn", H)))
    t_rs = []
    ahead_of = [norm_x(t_rs)]

    def tiles(gens):
        gens = list(gens)
        if ahead_of:
            around(gens.pop(0), gens.pop(0), ahead_of.pop())
        for g in gens:
            run(g)

    def ff1_epi(i):
        def epi(bank, t):
            q, tile, last = tmps.take()
            a = stt(tile[:], bank[:], 0.0, RSb[:], ALU.max, ALU.mult, t, t_rs, last)
            d = tt(dve, tile[:], tile[:], tile[:], ALU.mult, a)
            U.tok[i] = split(Uhi[:, i, :], Ulo[:, i, :], tile[:], d)
            tmps.free(q, U.tok[i])
            rs_free[0] = a
            return [a]
        return epi

    for chn in range(4):
        tiles(tile_t(("f1", 8 * chn + i), H, range(8), ff1_epi(i)) for i in range(8))
        for i in range(8):
            run(tile_t(("f2", chn, i), U, range(8), residual(i, "gmix2" if chn == 3 else None, H)))
    t_rs = []
    ahead_of.append(norm_x(t_rs, rsnb[:]))

    qa, ka = sb("qa", [128, 4, T]), sb("ka", [128, 4, T])
    va = [sb(f"va{i}", [128, T]) for i in range(4)]
    vs = [sb(f"vs{i}", [128, T]) for i in range(3)]
    qb, kbr, vb = sb("qb", [128, 4, T]), sb("kbr", [128, 2, T]), sb("vb", [128, 4, 128])
    ga = sb("ga", [128, 4, T])
    gates = [ga[:, i, :] for i in range(4)] + [z[:, i, :] for z in (qa, ka) for i in range(4)]
    gates += [z[:] for z in va]
    bA = Ring([sb(f"bA{i}", [128, 3, 256])[:] for i in range(2)])
    bB = Ring([z[:, 0:2, :].rearrange("p a x -> p (a x)")[:, 0:384] for z in bA.items])
    assert top[0] <= nc.sbuf_usable_end, top[0]
    sring, pT = Ring([sb(f"sr{i}", [128, 384]) for i in range(4)]), Ring([sb(f"pT{i}", [128, 384]) for i in range(3)])
    stats = Ring([sb(f"st{i}", [128, 8]) for i in range(4)])
    for r in (sring, pT, stats):
        r.last = [[old] for _ in r.last]
    sem_bA, sem_bB = [sem("bA0"), sem("bA1")], [sem("bB0"), sem("bB1")]
    tq = {}

    def qk_epi(name, i, dst_tile, gain, by_row):
        def epi(bank, t):
            def dst(raw, rs, need):
                if by_row:
                    o, a, b = rows(dst_tile), columns(raw), columns(rs)
                else:
                    o, a, b = dst_tile, raw, rs
                d = stt(o, a, gain, b, ALU.mult, ALU.mult, need, t_vd, old)
                tq[(name, i)] = d
                return d
            return head_norm(bank[:], RSb[:], dst, [t, t_rs], tmps)
        return epi

    tiles(tile_t(("wi", i), H, range(8), qk_epi("qa", i, qa[:, i, :], scaled["qa"], False))
          for i in range(4))
    for i in range(4):
        run(tile_t(("wi", 4 + i), H, range(8), qk_epi("ka", i, ka[:, i, :], v("ka2"), False)))
    got = [M.take() for _ in range(4)]
    for u in range(4):
        unit = W.get(("va", u))
        for j in range(4):
            k_b, bank, rel = got[j]
            for i in range(2):
                k = 2 * u + i
                xh, xl = (z[:, k, 128 * j:128 * j + 128] for z in (Hhi, Hlo))
                wh, wl = unit[1][:, 512 * i:512 * i + 512], unit[2][:, 512 * i:512 * i + 512]
                mm(bank[:], xh, wh, k == 0, False, unit[3], rel, H.tok[k])
                mm(bank[:], xh, wl, False, False)
                mm(bank[:], xl, wh, False, k == 7)
        W.free(unit, pe.tick())
    t = pe.tick()
    t_va = []
    for j in range(4):
        b = got[j][1]
        outs = [(va[j][:], 0, 128)]
        if j < 3:
            outs.append((vs[j][0:64, :], 64, 128))
        if j:
            outs.append((vs[j - 1][64:128, :], 0, 64))
        if j % 2:
            x = [ts(dve, o, b[lo:hi, :], rsnb[lo:hi, j:j + 1], None, ALU.mult, None, t, t_rs, old)
                 for o, lo, hi in outs]
        else:
            x = [actf(o, b[lo:hi, :], ACT.Copy, rsnb[lo:hi, j:j + 1], None, t, t_rs, old)
                 for o, lo, hi in outs]
        M.free(got[j][0], x)
        t_va.append(x)

    def kb_epi(bank, t):
        def dst(raw, rs, need):
            x = stt(raw, raw, v("kb"), rs, ALU.mult, ALU.mult, need)
            tq["kb"] = [copy(act, rows(kbr[64 * a:64 * a + 64, b, :]), columns(raw[64 * b:64 * b + 64, :]), x, old)
                        for a in range(2) for b in range(2)]
            return tq["kb"]
        return head_norm(bank[:], RSb[:], dst, [t, t_rs], tmps)

    t_g = {}

    def gate_epi(i, *need):
        def epi(bank, t):
            dst = gates[i]
            d = tt(dve, dst, bank[:], RSb[:], ALU.mult, t, t_rs, old, *need)
            t_g[i] = sigmoid(dst, dst, None, d)
            rs_free[0] = d
            return [d]
        return epi

    def vb_epi(bank, t):
        q, tile, last = tmps.take()
        a = tt(dve, rows(tile[:]), columns(bank[:]), columns(RSb[:]), ALU.mult, t, last, t_rs)

        def rest():
            k, b1, rel = M.take()
            for n in range(4):
                transpose(b1[:, 128 * n:128 * n + 128], tile[:, 128 * n:128 * n + 128], c("ident"), rel, a)
            t = pe.tick()
            tq["vb"] = copy(dve, vb[:], b1[:].rearrange("p (n x) -> p n x", x=128), t, old)
            M.free(k, tq["vb"])
            tmps.free(q, t)
        pend.append(rest)
        return [a]

    for i in range(4):
        run(tile_t(("wi", 12 + i), H, range(8), qk_epi("qb", i, qb[:, i, :], scaled["qb"], True)))
    run(tile_t(("wi", 16), H, range(8), kb_epi))
    run(tile_t(("wi", 17), H, range(8), vb_epi))

    A_SPAN, A_KIND = (0, 64, 192, 256), (0, 1, 1, 2)
    A_V = ((va[0], va[1]), (vs[0], vs[1]), (vs[1], vs[2]), (va[2], va[3]))

    def scores_item(q, k, n, bias, sink, need, values, o_of, vneed):
        kk, bank, rel = M.take()
        mm(bank[:, 0:n], q, k, True, True, rel, need)
        t = pe.tick()
        soft = softmax(bank[:, 0:n], n, bias, sink, sring, stats, t)
        free = next(soft)
        M.free(kk, free)
        yield
        z, p, r = next(soft)
        yield from rounds(SOFT_ROUNDS)
        qq, pt, plast = pT.take()
        ptv = pt.rearrange("p (b x) -> p b x", x=128)[:, 0:n // 128, :]
        a, d = transposed(p, n, ptv, r, plast)
        sring.free(z, a)
        yield
        o, orel = o_of()
        nb = n // 128
        for b in range(nb):
            mm(o, values[b], ptv[:, b, :], b == 0, b == nb - 1, d, orel, vneed)
        t = pe.tick()
        pT.free(qq, t)
        yield t, free

    def attention(make, bias, finish):
        hold, left, toks = {}, [8] * 4, [[] for _ in range(4)]

        def o_of(hp, off, j):
            if hp not in hold:
                hold[hp] = OY.take()
            kd, bank, rel = hold[hp]
            return bank[off:off + 64, 128 * j:128 * j + 128], rel

        def item(h, j):
            hp = h // 2
            if j == 0:
                bias.need(h)
            k, tile, bt = bias.now[h]
            for x in make(h, j, tile, bt, o_of):
                if x:
                    t, free = x
                    bias.read(h, free)
                    left[hp] -= 1
                    if not left[hp]:
                        kd, bank, rel = hold[hp]
                        at, hi, lo, src = finish(hp, bank)
                        h_ = copy(act, hi, src, t)
                        yield
                        yield
                        U.tok[at] = [h_, tt(dve, lo, src, hi.bitcast(F), ALU.subtract, h_)]
                        OY.free(kd, U.tok[at])
                yield

        yield from pipeline([item(h, j) for h in range(8) for j in range(4)])

    class Biases:

        def __init__(self, ring, sems, src):
            self.ring, self.sems, self.src, self.now, self.reads = ring, sems, src, {}, {}

        def issue(self, h):
            k, tile, last = self.ring.take()
            t = load_on(sp, tile, self.src[h], self.sems[h % 2], h // 2 + 1, last, old)
            self.now[h], self.reads[h] = (k, tile, t), []

        def need(self, h):
            if h not in self.now:
                self.issue(h)

        def read(self, h, tok):
            self.reads[h].append(tok)
            if len(self.reads[h]) == 4:
                self.ring.free(self.now[h][0], self.reads[h])
                if h + 2 < 8:
                    self.issue(h + 2)

    def make_a(h, j, bias, bt, o_of):
        off, kt = 64 * (h % 2), h // 2
        return scores_item(qa[off:off + 64, kt, 128 * j:128 * j + 128],
                           ka[off:off + 64, kt, A_SPAN[j]:A_SPAN[j] + 256], 256,
                           bias[:, A_KIND[j], :], None, [tq[("qa", kt)], tq[("ka", kt)], bt],
                           [z[:, 64 * h:64 * h + 64] for z in A_V[j]], lambda: o_of(kt, off, j), t_va)

    def finish_a(hp, bank):
        return hp, Uhi[:, hp, :], Ulo[:, hp, :], bank[:]

    def make_b(h, n, bias, bt, o_of):
        off, kt, kv = 64 * (h % 2), h // 2, h // 4
        a, b = max(0, n - 1), min(4, n + 2)
        w = 128 * (b - a)
        o = 128 * (a - n + 1)
        return scores_item(qb[off:off + 64, kt, 128 * n:128 * n + 128],
                           kbr[off:off + 64, kv, 128 * a:128 * b], w, bias[:, o:o + w],
                           v("sink", h), [tq[("qb", kt)], tq["kb"], bt],
                           [vb[:, i, 64 * kv:64 * kv + 64] for i in range(a, b)],
                           lambda: o_of(kt, off, n), tq["vb"])

    def finish_b(hp, bank):
        return 4 + hp, columns(Uhi[:, 4 + hp, :]), columns(Ulo[:, 4 + hp, :]), rows(bank[:])

    OY = Ring([O.items[0], Y.items[0]])
    OY.last = [O.last[0], Y.last[0]]

    def some_gates(ids, *need):
        for i in ids:
            yield from tile_t(("wi", 18 + i), H, range(8), gate_epi(i, *need))

    bias_a = Biases(bA, sem_bA, biasA)
    bias_a.issue(0)
    bias_a.issue(1)
    lows[0] = pool
    filler = some_gates(range(4))
    weave(attention(make_a, bias_a, finish_a), filler, FILL_A)
    run(filler)
    a_done = [pe.tick(), U.tok[0:4]]

    def gated_a(i):
        def epi(bank, t):
            d = stt(gates[i], gates[i], 1.0, bank[:], ALU.add, ALU.mult, t, t_g[i])
            t_g[i] = d
            return [d]
        return epi

    def branch_a():
        for m in range(4):
            hold = []
            yield from tile_t(("ba", m), U, range(4), gated_a(2 * m), hold=hold)
            yield from tile_t(("ba", m), U, range(4), gated_a(2 * m + 1), j0=4, keep=hold[0])

    def side_b():
        yield from some_gates(range(4, 8), a_done)
        yield from branch_a()
        yield from some_gates(range(8, 16), a_done)

    bB.last = bA.last
    bias_b = Biases(bB, sem_bB, biasB)
    bias_b.issue(0)
    bias_b.issue(1)
    filler = side_b()
    weave(attention(make_b, bias_b, finish_b), filler, FILL_B)
    run(filler)
    flush()
    flush()


    hfree = pe.tick()

    def both(i):
        def epi(bank, t):
            q, tile, last = tmps.take()
            d = stt(tile[:], gates[8 + i], 1.0, bank[:], ALU.add, ALU.mult, t, last, t_g[8 + i])
            d2 = tt(dve, tile[:], tile[:], gates[i], ALU.add, d, t_g[i])
            h = actf(Hhi[:, i, :], tile[:], ACT.Copy, 0.5, None, d2, hfree)
            H.tok[i] = [h, stt(Hlo[:, i, :], tile[:], 0.5, Hhi[:, i, :].bitcast(F), ALU.mult,
                               ALU.subtract, h)]
            tmps.free(q, H.tok[i])
            return [d]
        return epi

    for m in range(4):
        hold = []
        run(tile_t(("bb", m), U, range(4, 8), both(2 * m), hold=hold))
        run(tile_t(("bb", m), U, range(4, 8), both(2 * m + 1), j0=4, keep=hold[0]))
    lows[0] = dve
    for i in range(8):
        run(tile_t(("wo2", i), H, range(8), residual(i, "gffn2", U, True)))
    t_rs = []
    ahead_of.append(norm_x(t_rs))

    glu = {}

    def gate1(bank, t):
        q, tile, last = tmps.take()
        z, sig, last2 = tmps.take()
        d = tt(dve, tile[:], bank[:], RSb[:], ALU.mult, t, last, t_rs)
        a = actf(sig[:], tile[:], ACT.Sigmoid, 1.0, None, d, last2)
        m = tt(pool, tile[:], tile[:], sig[:], ALU.mult, a)
        glu["x"] = (q, tile, m, z, sig)
        return [d]

    def up1(i):
        def epi(bank, t):
            q, tile, m, z, up = glu["x"]
            d = tt(dve, up[:], bank[:], RSb[:], ALU.mult, m, t)
            m = tt(pool, up[:], up[:], tile[:], ALU.mult, d)
            H.tok[i] = split(Hhi[:, i, :], Hlo[:, i, :], up[:], m)
            tmps.free(q, m)
            tmps.free(z, H.tok[i])
            return [d]
        return epi

    s_out = sem("s_out")

    def final(i):
        r = residual(i)

        def epi(bank, t):
            d = r(bank, t)
            sp_out.append((i, d))
            return d
        return epi

    sp_out = []
    for chn, n in enumerate((8, 8, 6)):
        tiles(tile_t((w, 8 * chn + i), U, range(8), epi(i)) for i in range(n)
              for w, epi in (("fg", lambda i: gate1), ("fu", up1)))
        for i in range(8):
            run(tile_t(("fd", chn, i), H, range(n), final(i) if chn == 2 else residual(i)))
            while sp_out:
                k, d = sp_out.pop(0)
                load_on(sp, out[k], X[:, k, :], s_out, k + 1, d)
    assert W.got == len(units), (W.got, len(units))

    with nc.Block() as block:
        @block.sync
        def _(e):
            sp.emit(e)
            e.wait_ge(s_out, 16 * 8)

        @block.gpsimd
        def _(e):
            pool.emit(e)

        @block.scalar
        def _(e):
            act.emit(e)

        @block.vector
        def _(e):
            dve.emit(e)

        @block.tensor
        def _(e):
            pe.emit(e)


def unit_list():
    u = [(("rw", m), 1024) for m in (18, 19, 0, 6, 12, 20, 21)]
    u += [(("memk", i), 1024) for i in range(2)] + [(("memv", i), 1024) for i in range(2)]
    u += [(("rw", 6 * i + p), 1024) for p in range(1, NP) for i in range(3)]
    u += [(("wo", i), 1024) for i in range(8)]
    for ch in range(4):
        u += [(("f1", 8 * ch + i), 1024) for i in range(8)] + [(("f2", ch, i), 1024) for i in range(8)]
    u += [(("wi", i), 1024) for i in range(8)] + [(("va", i), 1024) for i in range(4)]
    u += [(("wi", i), 1024) for i in range(12, 18)]
    u += [(("wi", i), 1024) for i in range(18, 26)] + [(("ba", m), 1024) for m in range(4)]
    u += [(("wi", i), 1024) for i in range(26, 34)] + [(("bb", m), 1024) for m in range(4)]
    u += [(("wo2", i), 1024) for i in range(8)]
    for ch, n in enumerate((8, 8, 6)):
        for i in range(n):
            u += [(("fg", 8 * ch + i), 1024), (("fu", 8 * ch + i), 1024)]
        u += [(("fd", ch, i), 128 * n) for i in range(8)]
    return u


def constants():
    out = np.zeros((128, NCST), np.float32)

    def put(name, a):
        o, n = C_AT[name]
        out[:, o:o + n] = a

    p = np.arange(128)
    same = (p[:, None] // 64 == p[None, :] // 64).astype(np.float32)
    s, t = p[:, None] % 64, np.arange(64)[None, :]
    both = lambda a: np.concatenate([a, a], 1) * same
    put("bd64", same / 64.0)
    put("mean", np.full((128, 128), 1.0 / 1024))
    put("ident", np.eye(128))
    put("mneg", both(-1.0 * (s < t)))
    put("mpos", both(1.0 * (s < t)))
    put("inclneg", both(-1.0 * (s <= t)))
    put("inclnegs", -1.0 * (s <= t))
    put("inclpos", both(1.0 * (s <= t)))
    level = lambda m, a, b: ((a // m) % 2 == 1) & (b // m == a // m - 1)
    put("level", np.concatenate([both(level(m, s, t)) for m in LEVELS[1:]], 1))
    put("level1t", both(level(1, t, s)))
    put("scan", np.broadcast_to((np.arange(512) % 64 != 0), (128, 512)))
    put("rmseps", RMS_EPS)
    put("gneps", GN_EPS)
    return out


def t5_buckets():
    rel = np.arange(384)[None, :] - 128 - np.arange(128)[:, None]
    half, exact = 16, 8
    n = np.abs(rel)
    large = exact + (np.log(np.maximum(n, 1) / exact) / np.log(128 / exact) * (half - exact)).astype(np.int32)
    return (rel > 0) * half + np.where(n < exact, n, np.minimum(large, half - 1)), n <= 128


def kernel(**inputs):
    import concourse.bacc as _bacc
    from concourse.bass_utils import run_bass_kernel_spmd as _run

    a = {k: np.asarray(x) for k, x in inputs.items()}
    f32 = np.float32

    def tiles(w, m, ks):
        x = w[ks[0] * 128:(ks[-1] + 1) * 128, 128 * m:128 * m + 128]
        return x.reshape(len(ks), 128, 128).transpose(1, 0, 2).reshape(128, -1)

    k8 = range(8)
    wi = a["w_in_2"][0]

    def unit(name):
        kind = name[0]
        if kind == "memk":
            return tiles(a["w_mem_kv"], name[1], k8)
        if kind == "memv":
            x = a["w_mem_kv"][512 * name[1]:512 * name[1] + 512, 256:512]
            return x.reshape(4, 128, 256).transpose(1, 0, 2).reshape(128, 1024)
        if kind == "rw":
            return tiles(a["rw_in"][0], name[1], k8)
        if kind == "wo":
            return tiles(a["w_out"][0], name[1], k8)
        if kind == "f1":
            return tiles(a["w_ff1"][0], name[1], k8)
        if kind == "f2":
            return tiles(a["w_ff2"][0], name[2], range(8 * name[1], 8 * name[1] + 8))
        if kind == "wi":
            return tiles(wi, name[1], k8)
        if kind == "va":
            x = wi[256 * name[1]:256 * name[1] + 256, 1024:1536]
            return x.reshape(2, 128, 512).transpose(1, 0, 2).reshape(128, 1024)
        if kind in ("ba", "bb"):
            w = a["w_branch_a_2" if kind == "ba" else "w_branch_b_2"][0]
            return np.concatenate([tiles(w, 2 * name[1] + i, range(4)) for i in range(2)], 1)
        if kind == "wo2":
            return tiles(a["w_out_2"][0], name[1], k8)
        if kind in ("fg", "fu"):
            return tiles(a["w_gate_2" if kind == "fg" else "w_up_2"][0], name[1], k8)
        return tiles(a["w_down_2"][0], name[2], range(8 * name[1], min(22, 8 * name[1] + 8)))

    units = unit_list()
    wts = np.zeros((len(units), 128, 1024), f32)
    for i, (name, n) in enumerate(units):
        wts[i, :, 0:n] = unit(name)

    def cols(x):
        return np.asarray(x, f32).reshape(-1, 128).T

    def twice(x):
        return np.concatenate([x.reshape(64), x.reshape(64)]).reshape(128, 1)

    vec = {"gmem": cols(a["mem_norm_g"]), "gmix": cols(a["norm_mix_g"]), "gffn": cols(a["norm_ffn_g"]),
           "mu": cols(a["rw_mu"]), "w0": cols(a["rw_w0"]), "a0": cols(a["rw_a0"]), "kk": cols(a["rw_k_k"]),
           "ka": cols(a["rw_k_a"]), "rk": cols(a["rw_r_k"]), "lng": cols(a["rw_lnx_g"]),
           "lnb": cols(a["rw_lnx_b"]), "gmix2": cols(a["norm_mix_2"]), "gffn2": cols(a["norm_ffn_2"]),
           "mq": twice(a["mem_q_norm_g"]), "mk": twice(a["mem_k_norm_g"]), "qa": twice(a["q_norm_a_2"]),
           "ka2": twice(a["k_norm_a_2"]), "qb": twice(a["q_norm_b_2"]), "kb": twice(a["k_norm_b_2"]),
           "sink": np.broadcast_to(a["sink_b_2"].reshape(1, 8), (128, 8))}
    vecs = np.concatenate([vec[n] for n, _ in VECS], 1)

    rpb, t5 = a["rpb_a_2"][0], a["t5_table_2"]
    col, row = np.arange(16), np.arange(8)
    bias_a = np.empty((8, 128, 3, 256), f32)
    for kind, (q0, k0) in enumerate(((0, 0), (16, 8), (48, 32))):
        qc, kc = q0 + col, k0 + np.arange(32)
        win = np.clip(qc - 8, 0, 48)
        ok = (kc[None, :] >= win[:, None]) & (kc[None, :] < win[:, None] + 16)
        dc = np.clip(kc[None, :] - qc[:, None], -15, 15) + 15
        dr = row[None, :] - row[:, None] + 7
        g = rpb[dr[None, :, None, :], dc[:, None, :, None]]
        g = np.where(ok[:, None, :, None, None], g, f32(-1e30))
        bias_a[:, :, kind, :] = g.reshape(128, 256, 8).transpose(2, 0, 1)
    bucket, ok = t5_buckets()
    bias_b = np.where(ok[:, :, None], t5[bucket], f32(-1e30)).transpose(2, 0, 1)

    arrays = {
        "xT": a["x"][0].T.reshape(8, 128, 512), "memT": a["mem"][0].T.reshape(8, 128, 256),
        "wts": wts, "vecs": vecs, "cst": constants(),
        "w2a2": np.concatenate([a["rw_w2"][0], a["rw_a2"][0]], 0), "g2": a["rw_g2"][0],
        "biasA": bias_a, "biasB": bias_b,
    }
    arrays = {f"in_{k}": np.ascontiguousarray(x, dtype=x.dtype) for k, x in arrays.items()}
    nc = _bacc.Bacc("TRN2", target_bir_lowering=False, num_devices=1)
    args = [nc.dram_tensor(k, x.shape, mybir.dt.from_np(x.dtype), kind="ExternalInput").ap()
            for k, x in arrays.items()]
    o = nc.dram_tensor("out", (8, 128, 512), F, kind="ExternalOutput").ap()
    block_program(nc, *args, o, units)
    r = _run(nc, [arrays], core_ids=[0])
    y = np.asarray(r.results[0]["out"])
    return y.reshape(1024, 512).T.reshape(1, 512, 1024).copy()
```
